# Optimizing a Trainium2 kernel written in Bass

```python
import jax
import jax.numpy as jnp
from jax import lax
import numpy as np

D_MODEL = 1024
BATCH = 1
SEQ = 512
DEPTH = 2

GRID_W = 64
CTX_LEN = 256
N_MOD = 6
LN_EPS = 1e-6
DEEPNORM_ALPHA = (2 * DEPTH) ** 0.25
DEEPNORM_BETA = (8 * DEPTH) ** -0.25

MLA_HEADS = 8
MLA_Q_RANK = 384
MLA_KV_RANK = 256
MLA_NOPE = 64
MLA_ROPE = 32
MLA_V = 64
MLA_SCALE = (MLA_NOPE + MLA_ROPE) ** -0.5
ROPE_BASE = 10000.0
ATTN_BLOCK = 128

GLA_HEADS = 4
GLA_DK = 64
GLA_DV = 128
GLA_GATE_RANK = 16
GLA_TAU = 16.0
GLA_CHUNK = 64

EV_WIDTHS = (MLA_Q_RANK, MLA_KV_RANK, MLA_ROPE,
             GLA_HEADS * GLA_DK, GLA_HEADS * GLA_DK, GLA_HEADS * GLA_DV, GLA_HEADS * GLA_DV,
             GLA_GATE_RANK, GLA_GATE_RANK)
EV_SPLITS = tuple(sum(EV_WIDTHS[:i + 1]) for i in range(len(EV_WIDTHS) - 1))
EV_IN = sum(EV_WIDTHS)
MIX_OUT = MLA_HEADS * MLA_V + GLA_HEADS * GLA_DV

RG_WIDTH = 1280
RG_BLOCKS = 10
RG_BW = RG_WIDTH // RG_BLOCKS
RG_CONV = 4
RG_CONV_LEFT = 2
RG_C = 8.0

PEER_HEADS = 8
PEER_NK = 128
PEER_N = PEER_NK * PEER_NK
PEER_TOPK = 16
PEER_QDIM = 256
PEER_HALF = PEER_QDIM // 2
PEER_BLOCK = 128

kernel_name = 'hybrid_mla_gla_rglru_peer_diffusion_block'

def layer_norm(x, g, b):
    xf = x.astype(jnp.float32)
    mu = jnp.mean(xf, axis=-1, keepdims=True)
    var = jnp.mean(jnp.square(xf - mu), axis=-1, keepdims=True)
    return ((xf - mu) * lax.rsqrt(var + LN_EPS) * g + b).astype(x.dtype)

def rms_norm(x, g):
    xf = x.astype(jnp.float32)
    y = xf * lax.rsqrt(jnp.mean(jnp.square(xf), axis=-1, keepdims=True) + LN_EPS)
    return (y * g).astype(x.dtype)

def modulate(h, shift, scale):
    return h * (1.0 + scale) + shift

def tflip(z):
    return jnp.flip(z, axis=1)

def axial_rope(seq_len):
    rows = seq_len // GRID_W
    row = jnp.repeat(jnp.arange(rows, dtype=jnp.float32), GRID_W)
    col = jnp.tile(jnp.arange(GRID_W, dtype=jnp.float32), rows)
    n_freq = MLA_ROPE // 4
    inv = jnp.power(ROPE_BASE, -jnp.arange(n_freq, dtype=jnp.float32) / n_freq)
    ang = jnp.concatenate([row[:, None] * inv, col[:, None] * inv], axis=-1)
    return jnp.cos(ang), jnp.sin(ang)

def apply_rope(x, cos, sin):
    half = x.shape[-1] // 2
    x1, x2 = x[..., :half], x[..., half:]
    return jnp.concatenate([x1 * cos - x2 * sin, x1 * sin + x2 * cos], axis=-1).astype(x.dtype)

def mla_queries(c_q, q_norm, w_uq, cos, sin):
    q = (rms_norm(c_q, q_norm) @ w_uq).reshape(c_q.shape[:-1] + (MLA_HEADS, MLA_NOPE + MLA_ROPE))
    q_nope, q_pe = q[..., :MLA_NOPE], q[..., MLA_NOPE:]
    if cos is not None:
        q_pe = apply_rope(q_pe, cos[:, None, :], sin[:, None, :])
    return jnp.concatenate([q_nope, q_pe], axis=-1)

def mla_keys_values(c_kv, k_pe, kv_norm, w_ukv, cos, sin):
    kv = (rms_norm(c_kv, kv_norm) @ w_ukv).reshape(c_kv.shape[:-1] + (MLA_HEADS, MLA_NOPE + MLA_V))
    k_nope, v = kv[..., :MLA_NOPE], kv[..., MLA_NOPE:]
    if cos is not None:
        k_pe = apply_rope(k_pe, cos, sin)
    k_pe = jnp.broadcast_to(k_pe[..., None, :], k_nope.shape[:-1] + (MLA_ROPE,))
    return jnp.concatenate([k_nope, k_pe], axis=-1), v

def softmax_attend(q, k, v):
    s = jnp.einsum('bqhd,bkhd->bhqk', q, k).astype(jnp.float32) * MLA_SCALE
    p = jax.nn.softmax(s, axis=-1).astype(v.dtype)
    return jnp.einsum('bhqk,bkhd->bqhd', p, v)

def blocked_attend(q, k, v):
    b, s, h, d = q.shape
    nb = s // ATTN_BLOCK
    qb = q.reshape(b, nb, ATTN_BLOCK, h, d).transpose(1, 0, 2, 3, 4)
    ob = lax.map(lambda qi: softmax_attend(qi, k, v), qb)
    return ob.transpose(1, 0, 2, 3, 4).reshape(b, s, h, v.shape[-1])

def gla_project(gq, gk, gv, gaf, gab, wa2, ba):
    lead = gq.shape[:-1]
    q = gq.reshape(lead + (GLA_HEADS, GLA_DK)) * (GLA_DK ** -0.5)
    k = gk.reshape(lead + (GLA_HEADS, GLA_DK))
    v = gv.reshape(lead + (GLA_HEADS, GLA_DV))

    def log_decay(ga, w, bias):
        z = (ga @ w + bias).astype(jnp.float32)
        return (jax.nn.log_sigmoid(z) / GLA_TAU).reshape(lead + (GLA_HEADS, GLA_DK))

    return q, k, v, log_decay(gaf, wa2[0], ba[0]), log_decay(gab, wa2[1], ba[1])

def gla_chunked(q, k, v, log_a, s0):
    b, t, h, dk = q.shape
    dv = v.shape[-1]
    n = t // GLA_CHUNK

    def chunks(z):
        return z.astype(jnp.float32).reshape(b, n, GLA_CHUNK, h, z.shape[-1]).transpose(1, 0, 3, 2, 4)

    lower = jnp.tril(jnp.ones((GLA_CHUNK, GLA_CHUNK), dtype=bool))[:, :, None]

    def step(state, inp):
        qc, kc, vc, ac = inp
        cum = jnp.cumsum(ac, axis=2)
        diff = cum[:, :, :, None, :] - cum[:, :, None, :, :]
        decay = jnp.exp(jnp.where(lower, diff, -jnp.inf))
        scores = jnp.einsum('bhid,bhjd,bhijd->bhij', qc, kc, decay)
        out = scores @ vc + jnp.einsum('bhid,bhde->bhie', qc * jnp.exp(cum), state)
        last = cum[:, :, -1:, :]
        state = (jnp.exp(last[:, :, 0, :])[..., None] * state
                 + jnp.einsum('bhjd,bhje->bhde', kc * jnp.exp(last - cum), vc))
        return state, out

    s_fin, o = lax.scan(step, s0, (chunks(q), chunks(k), chunks(v), chunks(log_a)))
    o = o.transpose(1, 0, 3, 2, 4).reshape(b, t, h, dv).astype(v.dtype)
    return o, s_fin

def gla_final_state(k, v, log_a):
    cum = jnp.cumsum(log_a, axis=1)
    w = jnp.exp(cum[:, -1:] - cum)
    return jnp.einsum('bthd,bthe->bhde', k.astype(jnp.float32) * w, v.astype(jnp.float32))

def gla_output(o, g, norm):
    lead = o.shape[:-2]
    y = rms_norm(o, norm.reshape(GLA_HEADS, GLA_DV)).reshape(lead + (GLA_HEADS * GLA_DV,))
    return y * jax.nn.silu(g)

def mla_gla_mixer(h_ctx, h_lat, cos, sin, w_in, q_norm, kv_norm, w_uq, w_ukv,
                  gla_wa2, gla_ba, gla_norm, w_out, with_ctx_out):
    b = h_lat.shape[0]
    pc = jnp.split(h_ctx @ w_in, EV_SPLITS, axis=-1)
    px = jnp.split(h_lat @ w_in, EV_SPLITS, axis=-1)
    k_c, v_c = mla_keys_values(pc[1], pc[2], kv_norm, w_ukv, None, None)
    k_x, v_x = mla_keys_values(px[1], px[2], kv_norm, w_ukv, cos, sin)
    q_x = mla_queries(px[0], q_norm, w_uq, cos, sin)
    att_x = blocked_attend(q_x, jnp.concatenate([k_c, k_x], axis=1), jnp.concatenate([v_c, v_x], axis=1))
    gq_c, gk_c, gv_c, laf_c, lab_c = gla_project(pc[3], pc[4], pc[5], pc[7], pc[8], gla_wa2, gla_ba)
    gq_x, gk_x, gv_x, laf_x, lab_x = gla_project(px[3], px[4], px[5], px[7], px[8], gla_wa2, gla_ba)
    zero = jnp.zeros((b, GLA_HEADS, GLA_DK, GLA_DV), jnp.float32)
    if with_ctx_out:
        o_cf, s_f = gla_chunked(gq_c, gk_c, gv_c, laf_c, zero)
        o_cb, s_b = gla_chunked(tflip(gq_c), tflip(gk_c), tflip(gv_c), tflip(lab_c), zero)
    else:
        s_f = gla_final_state(gk_c, gv_c, laf_c)
        s_b = gla_final_state(tflip(gk_c), tflip(gv_c), tflip(lab_c))
    o_xf, _ = gla_chunked(gq_x, gk_x, gv_x, laf_x, s_f)
    o_xb, _ = gla_chunked(tflip(gq_x), tflip(gk_x), tflip(gv_x), tflip(lab_x), s_b)
    gla_x = gla_output(o_xf + tflip(o_xb), px[6], gla_norm)
    out_x = jnp.concatenate([att_x.reshape(att_x.shape[:2] + (MLA_HEADS * MLA_V,)), gla_x], axis=-1) @ w_out
    out_c = None
    if with_ctx_out:
        q_c = mla_queries(pc[0], q_norm, w_uq, None, None)
        att_c = softmax_attend(q_c, k_c, v_c)
        gla_c = gla_output(o_cf + tflip(o_cb), pc[6], gla_norm)
        out_c = jnp.concatenate([att_c.reshape(att_c.shape[:2] + (MLA_HEADS * MLA_V,)), gla_c], axis=-1) @ w_out
    return out_c, out_x

def dwconv_centred(z, w, bias):
    t = z.shape[1]
    zp = jnp.pad(z, ((0, 0), (RG_CONV_LEFT, RG_CONV - 1 - RG_CONV_LEFT), (0, 0)))
    y = bias + zp[:, 0:t] * w[0]
    for tap in range(1, RG_CONV):
        y = y + zp[:, tap:tap + t] * w[tap]
    return y

def rg_gates(z, gw, gb, lam):
    zf = z.astype(jnp.float32)
    zb = zf.reshape(z.shape[:-1] + (RG_BLOCKS, RG_BW))

    def gate(w, bias):
        return jax.nn.sigmoid(jnp.einsum('btnc,ncd->btnd', zb, w.astype(jnp.float32)).reshape(zf.shape) + bias)

    r = gate(gw[0], gb[0])
    i = gate(gw[1], gb[1])
    log_a = -RG_C * jax.nn.softplus(-lam.astype(jnp.float32)) * r
    x_in = jnp.sqrt(-jnp.expm1(2.0 * log_a)) * (i * zf)
    return log_a, x_in

def linear_scan(log_a, x_in, h0, reverse):
    a = jnp.exp(log_a)
    if h0 is not None:
        edge = -1 if reverse else 0
        x_in = x_in.at[:, edge].add(a[:, edge] * h0)

    def combine(left, right):
        a_l, b_l = left
        a_r, b_r = right
        return a_l * a_r, a_r * b_l + b_r

    _, h = lax.associative_scan(combine, (a, x_in), reverse=reverse, axis=1)
    return h, (h[:, 0] if reverse else h[:, -1])

def rglru_mixer(h_ctx, h_lat, w_in, conv_w, conv_b, gate_w, gate_b, lam, w_out, with_ctx_out):
    proj_x = h_lat @ w_in
    branch_x, rnn_x = proj_x[..., :RG_WIDTH], proj_x[..., RG_WIDTH:]
    rnn_c = h_ctx @ w_in[:, RG_WIDTH:]
    rnn_x = dwconv_centred(rnn_x, conv_w, conv_b)
    rnn_c = dwconv_centred(rnn_c, conv_w, conv_b)
    ys_x = []
    ys_c = []
    for d, reverse in enumerate((False, True)):
        la_c, in_c = rg_gates(rnn_c, gate_w[d], gate_b[d], lam[d])
        la_x, in_x = rg_gates(rnn_x, gate_w[d], gate_b[d], lam[d])
        y_c, h_ctx_final = linear_scan(la_c, in_c, None, reverse)
        y_x, _ = linear_scan(la_x, in_x, h_ctx_final, reverse)
        ys_c.append(y_c)
        ys_x.append(y_x)
    out_x = (jax.nn.gelu(branch_x, approximate=False) * (ys_x[0] + ys_x[1]).astype(h_lat.dtype)) @ w_out
    out_c = None
    if with_ctx_out:
        branch_c = h_ctx @ w_in[:, :RG_WIDTH]
        out_c = (jax.nn.gelu(branch_c, approximate=False) * (ys_c[0] + ys_c[1]).astype(h_ctx.dtype)) @ w_out
    return out_c, out_x

def peer_ffn(h, wq, k1, k2, u, v):
    b, t, d = h.shape
    n_tok = b * t
    ht = h.reshape(n_tok, d)
    q = (ht @ wq).reshape(n_tok, PEER_HEADS, PEER_QDIM)
    s1 = jnp.einsum('thd,kd->thk', q[..., :PEER_HALF], k1).astype(jnp.float32)
    s2 = jnp.einsum('thd,kd->thk', q[..., PEER_HALF:], k2).astype(jnp.float32)
    t1, i1 = lax.top_k(s1, PEER_TOPK)
    t2, i2 = lax.top_k(s2, PEER_TOPK)
    cand_s = (t1[..., :, None] + t2[..., None, :]).reshape(n_tok, PEER_HEADS, PEER_TOPK * PEER_TOPK)
    cand_i = (i1[..., :, None] * PEER_NK + i2[..., None, :]).reshape(n_tok, PEER_HEADS, PEER_TOPK * PEER_TOPK)
    top_s, pos = lax.top_k(cand_s, PEER_TOPK)
    idx = jnp.take_along_axis(cand_i, pos, axis=-1)
    g = jax.nn.softmax(top_s, axis=-1).astype(h.dtype)
    nb = n_tok // PEER_BLOCK

    def block(args):
        hb, ib, gb = args
        ue = jnp.take(u, ib, axis=0)
        ve = jnp.take(v, ib, axis=0)
        act = jax.nn.gelu(jnp.einsum('td,thkd->thk', hb, ue), approximate=False)
        return jnp.einsum('thk,thkd->td', gb * act, ve)

    out = lax.map(block, (ht.reshape(nb, PEER_BLOCK, d),
                          idx.reshape(nb, PEER_BLOCK, PEER_HEADS, PEER_TOPK),
                          g.reshape(nb, PEER_BLOCK, PEER_HEADS, PEER_TOPK)))
    return out.reshape(b, t, d)

def setup_inputs(seed: int = 0) -> dict:
    key = jax.random.key(seed)
    ks = jax.random.split(key, 32)
    f32 = jnp.float32
    D = D_MODEL
    NE = (DEPTH + 1) // 2
    NO = DEPTH // 2

    def nrm(k, shape, scale):
        return jax.random.normal(k, shape, f32) * scale

    a_c = jax.random.uniform(ks[24], (NO, 2, RG_WIDTH), f32, minval=0.9, maxval=0.999)
    sig = jnp.power(a_c, 1.0 / RG_C)
    od_lambda = jnp.log(sig) - jnp.log1p(-sig)
    return {
        'x': nrm(ks[0], (BATCH, SEQ, D), 1.0),
        'c': nrm(ks[1], (BATCH, D), 1.0),
        'ctx': nrm(ks[2], (BATCH, CTX_LEN, D), 1.0),
        'c_ctx': nrm(ks[3], (D,), 1.0),
        'mod_w': nrm(ks[4], (DEPTH, D, N_MOD * D), D ** -0.5),
        'mod_b': nrm(ks[5], (DEPTH, N_MOD * D), 0.02),
        'ln_g': 1.0 + nrm(ks[6], (DEPTH, 2, D), 0.02),
        'ln_b': nrm(ks[7], (DEPTH, 2, D), 0.02),
        'ev_w_in': nrm(ks[8], (NE, D, EV_IN), D ** -0.5),
        'ev_q_norm': 1.0 + nrm(ks[9], (NE, MLA_Q_RANK), 0.02),
        'ev_kv_norm': 1.0 + nrm(ks[10], (NE, MLA_KV_RANK), 0.02),
        'ev_w_uq': nrm(ks[11], (NE, MLA_Q_RANK, MLA_HEADS * (MLA_NOPE + MLA_ROPE)), MLA_Q_RANK ** -0.5),
        'ev_w_ukv': nrm(ks[12], (NE, MLA_KV_RANK, MLA_HEADS * (MLA_NOPE + MLA_V)), MLA_KV_RANK ** -0.5),
        'ev_gla_wa2': nrm(ks[13], (NE, 2, GLA_GATE_RANK, GLA_HEADS * GLA_DK), GLA_GATE_RANK ** -0.5),
        'ev_gla_ba': nrm(ks[14], (NE, 2, GLA_HEADS * GLA_DK), 0.1),
        'ev_gla_norm': 1.0 + nrm(ks[15], (NE, GLA_HEADS * GLA_DV), 0.02),
        'ev_w_out': nrm(ks[16], (NE, MIX_OUT, D), (MIX_OUT ** -0.5) * DEEPNORM_BETA),
        'od_w_in': nrm(ks[17], (NO, D, 2 * RG_WIDTH), D ** -0.5),
        'od_conv_w': nrm(ks[18], (NO, RG_CONV, RG_WIDTH), RG_CONV ** -0.5),
        'od_conv_b': nrm(ks[19], (NO, RG_WIDTH), 0.02),
        'od_gate_w': nrm(ks[20], (NO, 2, 2, RG_BLOCKS, RG_BW, RG_BW), RG_BW ** -0.5),
        'od_gate_b': nrm(ks[21], (NO, 2, 2, RG_WIDTH), 0.02),
        'od_lambda': od_lambda,
        'od_w_out': nrm(ks[22], (NO, RG_WIDTH, D), (RG_WIDTH ** -0.5) * DEEPNORM_BETA),
        'peer_wq': nrm(ks[23], (DEPTH, D, PEER_HEADS * PEER_QDIM), D ** -0.5),
        'peer_k1': nrm(ks[25], (DEPTH, PEER_NK, PEER_HALF), PEER_HALF ** -0.5),
        'peer_k2': nrm(ks[26], (DEPTH, PEER_NK, PEER_HALF), PEER_HALF ** -0.5),
        'peer_u': nrm(ks[27], (DEPTH, PEER_N, D), D ** -0.5),
        'peer_v': nrm(ks[28], (DEPTH, PEER_N, D), DEEPNORM_BETA),
    }

def reference(x, c, ctx, c_ctx, mod_w, mod_b, ln_g, ln_b,
              ev_w_in, ev_q_norm, ev_kv_norm, ev_w_uq, ev_w_ukv, ev_gla_wa2, ev_gla_ba, ev_gla_norm, ev_w_out,
              od_w_in, od_conv_w, od_conv_b, od_gate_w, od_gate_b, od_lambda, od_w_out,
              peer_wq, peer_k1, peer_k2, peer_u, peer_v):
    seq_len = x.shape[1]
    cos, sin = axial_rope(seq_len)
    silu_c = jax.nn.silu(c)
    silu_cc = jax.nn.silu(c_ctx)
    h_lat, h_ctx = x, ctx
    for layer in range(DEPTH):
        last = layer == DEPTH - 1
        j = layer // 2
        mx = jnp.split((silu_c @ mod_w[layer] + mod_b[layer])[:, None, :], N_MOD, axis=-1)
        mc = jnp.split((silu_cc @ mod_w[layer] + mod_b[layer])[None, None, :], N_MOD, axis=-1)
        in_x = modulate(h_lat, mx[0], mx[1])
        in_c = modulate(h_ctx, mc[0], mc[1])
        if layer % 2 == 0:
            mix_c, mix_x = mla_gla_mixer(in_c, in_x, cos, sin, ev_w_in[j], ev_q_norm[j], ev_kv_norm[j],
                                         ev_w_uq[j], ev_w_ukv[j], ev_gla_wa2[j], ev_gla_ba[j],
                                         ev_gla_norm[j], ev_w_out[j], not last)
        else:
            mix_c, mix_x = rglru_mixer(in_c, in_x, od_w_in[j], od_conv_w[j], od_conv_b[j], od_gate_w[j],
                                       od_gate_b[j], od_lambda[j], od_w_out[j], not last)
        h_lat = layer_norm(DEEPNORM_ALPHA * h_lat + mx[2] * mix_x, ln_g[layer, 0], ln_b[layer, 0])
        f_x = peer_ffn(modulate(h_lat, mx[3], mx[4]), peer_wq[layer], peer_k1[layer], peer_k2[layer],
                       peer_u[layer], peer_v[layer])
        h_lat = layer_norm(DEEPNORM_ALPHA * h_lat + mx[5] * f_x, ln_g[layer, 1], ln_b[layer, 1])
        if not last:
            h_ctx = layer_norm(DEEPNORM_ALPHA * h_ctx + mc[2] * mix_c, ln_g[layer, 0], ln_b[layer, 0])
            f_c = peer_ffn(modulate(h_ctx, mc[3], mc[4]), peer_wq[layer], peer_k1[layer], peer_k2[layer],
                           peer_u[layer], peer_v[layer])
            h_ctx = layer_norm(DEEPNORM_ALPHA * h_ctx + mc[5] * f_c, ln_g[layer, 1], ln_b[layer, 1])
    return h_lat


_drawn_inputs = setup_inputs


def setup_inputs(seed=0):
    import zlib

    import numpy as np

    out = dict(_drawn_inputs(seed))
    spreads = {}
    factors = {'ev_q_norm': 8.0,
     'ev_kv_norm': 5.712,
     'ev_gla_ba': 3.016,
     'ev_gla_norm': 4.548,
     'od_gate_b': 5.589}
    for name, (base, spread) in spreads.items():
        noise = np.random.default_rng([zlib.crc32(name.encode()), seed]).standard_normal(out[name].shape)
        drawn = base * np.exp(spread * noise) if base else spread * noise
        out[name] = jnp.asarray(drawn.astype(out[name].dtype))
    for name, factor in factors.items():
        out[name] = (out[name] * factor).astype(out[name].dtype)
    return out
```

```python
from contextlib import ExitStack, contextmanager
from itertools import count

import numpy as np
import concourse.bass as bass
from concourse import mybir

F32 = mybir.dt.float32
BF16 = mybir.dt.bfloat16
I32 = mybir.dt.int32
U32 = mybir.dt.uint32
ALU = mybir.AluOpType
ACT = mybir.ActivationFunctionType
AX = mybir.AxisListType

P = 128
D = 1024
KD = D // P
SEQ, CTX = 512, 256
TOK = CTX + SEQ
TILES = TOK // P
CTX_TILES = CTX // P
N_MOD = 6
DEPTH = 2
ALPHA = (2 * DEPTH) ** 0.25
EPS = 1e-6
HALVES = ((0, 512), (512, 256))

HEADS, Q_RANK, KV_RANK, NOPE, ROPE, V_DIM = 8, 384, 256, 64, 32, 64
MLA_SCALE = (NOPE + ROPE) ** -0.5
GH, GDK, GDV, GRANK, TAU, CHUNK = 4, 64, 128, 16, 16.0, 64
CHUNKS = TOK // CHUNK
CTX_CHUNKS = CTX // CHUNK
C_Q, C_KV, C_GQ, C_GK, C_GG, C_MISC, N_PROJ = 0, 3, 5, 7, 9, 13, 14
GAF, GAB, KPE, KPE_SWAPPED = 0, 32, 64, 96

RG_W, RG_N, RG_CONV, RG_LEFT, RG_C = 1280, 10, 4, 2, 8.0
PH, PK, PTOP = 8, 128, 16
PCH = 128


STAGE = count()


@contextmanager
def signals(nc, *names):
    stage = next(STAGE)
    sems = [nc.alloc_semaphore(f"{n}_{stage}") for n in names]
    yield sems
    nc.clear_and_free_semaphores(sems)
    nc.all_engine_barrier()


class InOrder:

    def __init__(self, eng, sem):
        self.eng, self.sem, self.n, self.base = eng, sem, 0, 0

    def start(self, i, per):
        self.base, self.n = i * per, 0

    def mark(self, ins):
        self.n += 1
        ins.then_inc(self.sem, 1)

    def wait(self):
        self.eng.wait_ge(self.sem, self.base + self.n)

    def __call__(self, ins):
        self.mark(ins)
        self.wait()


def row_to_all(ap_row, n):
    return ap_row.rearrange("(o n) -> o n", o=1).broadcast_to([P, n])


def modulation_vectors(nc, io, mods, ones):
    LOADS = 2 * N_MOD
    with ExitStack() as c:
        sb = lambda n, s: c.enter_context(nc.sbuf_tensor(n, s, F32))
        cond = sb("cond", [P, KD, 2])
        w = [sb(f"mod_w{j}", [P, KD, 1024]) for j in range(3)]
        rows = sb("mod_rows", [2, LOADS * 1024])
        pm = [c.enter_context(nc.psum_tensor(f"mod_ps{j}", [P, 1024], F32)) for j in range(3)]
        with signals(nc, "cond_in", "bias_in", "silu_done", "rows_done", "stored",
                     *[f"w_in{j}" for j in range(3)], *[f"prod{j}" for j in range(3)],
                     *[f"added{j}" for j in range(3)]) as sems:
            cond_in, bias_in, silu_done, rows_done, stored = sems[:5]
            w_in, prod, added = sems[5:8], sems[8:11], sems[11:14]
            with nc.Block() as block:
                @block.sync
                def _(sp):
                    sp.dma_start(cond[:, :, :], io["cond"]).then_inc(cond_in, 16)
                    for j in range(3):
                        sp.dma_start(w[j][:, :, :], io["mod_w"][j].rearrange("p (k n) -> p k n", k=KD)).then_inc(w_in[j], 16)
                    sp.dma_start(rows[:, :], io["mod_b"].rearrange("(o n) -> o n", o=1).broadcast_to([2, LOADS * 1024])).then_inc(bias_in, 16)
                    with sp.Fori(1, LOADS // 3) as it:
                        for j in range(3):
                            sp.wait_ge(prod[j], it)
                            sp.dma_start(w[j][:, :, :], io["mod_w"][bass.ds(it * 3 + j, 1)].rearrange("o p (k n) -> p (o k) n", k=KD)).then_inc(w_in[j], 16)
                    sp.wait_ge(rows_done, LOADS)
                    sp.dma_start(mods, rows[:, :]).then_inc(stored, 16)
                    sp.wait_ge(stored, 16)

                @block.scalar
                def _(act):
                    act.wait_ge(cond_in, 16)
                    nc.scalar.activation(cond[:, :, :], cond[:, :, :], ACT.Silu).then_inc(silu_done, 1)

                @block.tensor
                def _(pe):
                    pe.wait_ge(silu_done, 1)
                    with pe.Fori(0, LOADS // 3) as it:
                        for j in range(3):
                            pe.wait_ge(w_in[j], it * 16 + 16)
                            pe.wait_ge(added[j], it + 1)
                            for h in range(2):
                                for k in range(KD):
                                    last = nc.tensor.matmul(pm[j][0:2, h * 512:h * 512 + 512], cond[:, k, :],
                                                            w[j][:, k, h * 512:h * 512 + 512],
                                                            start=(k == 0), stop=(k == KD - 1))
                            last.then_inc(prod[j], 1)

                @block.vector
                def _(dve):
                    for j in range(3):
                        nc.vector.memset(ones[0:1, j:j + 1], 1.0).then_inc(added[j], 1)
                    dve.wait_ge(bias_in, 16)
                    with dve.Fori(0, LOADS // 3) as it:
                        for j in range(3):
                            dve.wait_ge(prod[j], it + 1)
                            piece = rows[:, bass.ds(it * 3072 + j * 1024, 1024)]
                            nc.vector.tensor_tensor(piece, piece, pm[j][0:2, :], ALU.add).then_inc(added[j], 1)
                    for j in range(3):
                        dve.wait_ge(added[j], LOADS // 3 + 1)
                    nc.vector.memset(ones[:, :], 1.0).then_inc(rows_done, LOADS)


def modulate_columns(nc, mods, H, XT, ident, layer, shift, first_tile, tag):
    o_sh, o_sc = (layer * N_MOD + shift) * D, (layer * N_MOD + shift + 1) * D
    tiles = list(range(first_tile, TILES))
    with ExitStack() as c:
        vec = c.enter_context(nc.sbuf_tensor(f"{tag}_vec", [P, 4, D], F32))
        tmp = [c.enter_context(nc.sbuf_tensor(f"{tag}_tmp{j}", [P, D], F32)) for j in range(2)]
        pt = [c.enter_context(nc.psum_tensor(f"{tag}_pt{j}", [P, KD, P], F32)) for j in range(2)]
        with signals(nc, f"{tag}_vec_in", f"{tag}_scaled", f"{tag}_mod", f"{tag}_turned", f"{tag}_copied") as (
                vec_in, scaled, modulated, turned, copied):
            with nc.Block() as block:
                @block.sync
                def _(sp):
                    for v in range(2):
                        sp.dma_start(vec[:, 2 * v, :], row_to_all(mods[v, o_sh:o_sh + D], D)).then_inc(vec_in, 16)
                        sp.dma_start(vec[:, 2 * v + 1, :], row_to_all(mods[v, o_sc:o_sc + D], D)).then_inc(vec_in, 16)

                @block.vector
                def _(dve):
                    dve.wait_ge(vec_in, 64)
                    for i, t in enumerate(tiles):
                        v = 1 if t < CTX_TILES else 0
                        if i >= 2:
                            dve.wait_ge(turned, i - 1)
                        nc.vector.scalar_tensor_tensor(tmp[i % 2][:, :], vec[:, 2 * v + 1, :], 1.0, H[:, t, :],
                                                       ALU.add, ALU.mult).then_inc(scaled, 1)
                        dve.wait_ge(scaled, i + 1)
                        nc.vector.tensor_tensor(tmp[i % 2][:, :], tmp[i % 2][:, :], vec[:, 2 * v, :],
                                                ALU.add).then_inc(modulated, 1)

                @block.tensor
                def _(pe):
                    for i, t in enumerate(tiles):
                        pe.wait_ge(modulated, i + 1)
                        if i >= 2:
                            pe.wait_ge(copied, i - 1)
                        for k in range(KD):
                            last = nc.tensor.transpose(pt[i % 2][:, k, :], tmp[i % 2][:, k * P:k * P + P], ident[:, :])
                        last.then_inc(turned, 1)

                @block.scalar
                def _(act):
                    for i, t in enumerate(tiles):
                        act.wait_ge(turned, i + 1)
                        nc.scalar.activation(XT[:, :, t * P:t * P + P], pt[i % 2][:, :, :], ACT.Copy).then_inc(copied, 1)


def project_l0(nc, io, XT, PT, V):
    with ExitStack() as c:
        w = [c.enter_context(nc.sbuf_tensor(f"pw{j}", [P, KD, P], F32)) for j in range(2)]
        wv = c.enter_context(nc.sbuf_tensor("pwv", [P, KD, GH * GDV], F32))
        ps = [c.enter_context(nc.psum_tensor(f"pps{j}", [P, 1024], F32)) for j in range(2)]
        pv = [c.enter_context(nc.psum_tensor(f"ppv{j}", [P, 512], F32)) for j in range(2)]
        with signals(nc, "wv_in", "v_prod", "v_copied", "w_in0", "w_in1", "prod0", "prod1", "copied0", "copied1") as sems:
            wv_in, v_prod, v_copied = sems[:3]
            w_in, prod, copied = sems[3:5], sems[5:7], sems[7:9]
            with nc.Block() as block:
                @block.sync
                def _(sp):
                    for j in range(2):
                        sp.dma_start(w[j][:, :, :], io["ev_w_in"][j].rearrange("p (k m) -> p k m", k=KD)).then_inc(w_in[j], 16)
                    sp.dma_start(wv[:, :, :], io["ev_w_v"]).then_inc(wv_in, 16)
                    with sp.Fori(1, N_PROJ // 2) as it:
                        for j in range(2):
                            sp.wait_ge(prod[j], it)
                            sp.dma_start(w[j][:, :, :], io["ev_w_in"][bass.ds(it * 2 + j, 1)].rearrange("o p (k m) -> p (o k) m", k=KD)).then_inc(w_in[j], 16)

                @block.tensor
                def _(pe):
                    with pe.Fori(0, N_PROJ // 2) as it:
                        for j in range(2):
                            pe.wait_ge(w_in[j], it * 16 + 16)
                            pe.wait_ge(copied[j], it + 1)
                            for a, n in HALVES:
                                for k in range(KD):
                                    last = nc.tensor.matmul(ps[j][:, a:a + n], w[j][:, k, :], XT[:, k, a:a + n],
                                                            start=(k == 0), stop=(k == KD - 1))
                            last.then_inc(prod[j], 1)
                    pe.wait_ge(wv_in, 16)
                    for t in range(TILES):
                        if t >= 2:
                            pe.wait_ge(v_copied, t - 1)
                        for k in range(KD):
                            last = nc.tensor.matmul(pv[t % 2][:, :], XT[:, k, t * P:t * P + P], wv[:, k, :],
                                                    start=(k == 0), stop=(k == KD - 1))
                        last.then_inc(v_prod, 1)

                @block.scalar
                def _(act):
                    for j in range(2):
                        nc.scalar.activation(V[0:1, 0, j:j + 1], XT[0:1, 0, 0:1], ACT.Copy).then_inc(copied[j], 1)
                    with act.Fori(0, N_PROJ // 2) as it:
                        for j in range(2):
                            act.wait_ge(prod[j], it + 1)
                            nc.scalar.activation(PT[:, bass.ds(it * 2 + j, 1), :].rearrange("p o t -> p (o t)"),
                                                 ps[j][:, 0:TOK], ACT.Copy).then_inc(copied[j], 1)

                @block.vector
                def _(dve):
                    for t in range(TILES):
                        dve.wait_ge(v_prod, t + 1)
                        nc.vector.tensor_copy(V[:, t, :], pv[t % 2][:, :]).then_inc(v_copied, 1)


def latent_norms(nc, io, PT, ones):
    with ExitStack() as c:
        sb = lambda n, s: c.enter_context(nc.sbuf_tensor(n, s, F32))
        sq = sb("ln_sq", [P, 5, TOK])
        g = sb("ln_gain", [P, 5])
        eps = sb("ln_eps", [P, 1])
        r = sb("ln_r", [P, 2, TOK])
        cs = sb("ln_cs", [P, TOK])
        tmp = sb("ln_tmp", [P, TOK])
        ss = [c.enter_context(nc.psum_tensor(f"ln_ss{j}", [P, 1024], F32)) for j in range(2)]
        with signals(nc, "ln_in", "squared", "summed", "rooted", "own", "eps_set") as (
                ln_in, squared, summed, rooted, own, eps_set):
            with nc.Block() as block:
                @block.sync
                def _(sp):
                    sp.dma_start(g[:, :], io["latent_gain"]).then_inc(ln_in, 16)
                    sp.dma_start(cs[64:128, :], io["rope"]).then_inc(ln_in, 16)

                @block.tensor
                def _(pe):
                    pe.wait_ge(squared, 1)
                    for j, (k0, k1) in enumerate(((0, 3), (3, 5))):
                        for a, n in HALVES:
                            for k in range(k0, k1):
                                last = nc.tensor.matmul(ss[j][:, a:a + n], ones[:, :], sq[:, k, a:a + n],
                                                        start=(k == k0), stop=(k == k1 - 1))
                        last.then_inc(summed, 1)

                @block.scalar
                def _(act):
                    act.wait_ge(eps_set, 1)
                    for j, rank in enumerate((Q_RANK, KV_RANK)):
                        act.wait_ge(summed, j + 1)
                        nc.scalar.activation(r[:, j, :], ss[j][:, 0:TOK], ACT.Sqrt, scale=1.0 / rank,
                                             bias=eps[:, :]).then_inc(rooted, 1)

                @block.vector
                def _(dve):
                    step = InOrder(dve, own)
                    nc.vector.memset(eps[:, :], EPS).then_inc(eps_set, 1)
                    nc.vector.tensor_tensor(sq[:, :, :], PT[:, 0:5, :], PT[:, 0:5, :], ALU.mult).then_inc(squared, 1)
                    dve.wait_ge(ln_in, 32)
                    pe_rows = PT[KPE:KPE + ROPE, C_MISC, :]
                    step.mark(nc.vector.tensor_tensor(tmp[64:96, :], PT[96:128, C_MISC, :], cs[96:128, :], ALU.mult))
                    step(nc.vector.tensor_tensor(pe_rows, pe_rows, cs[64:96, :], ALU.mult))
                    step(nc.vector.tensor_tensor(pe_rows, pe_rows, tmp[64:96, :], ALU.add))
                    for j, (k0, k1) in enumerate(((0, 3), (3, 5))):
                        dve.wait_ge(rooted, j + 1)
                        step(nc.vector.reciprocal(r[:, j, :], r[:, j, :]))
                        for k in range(k0, k1):
                            nc.vector.scalar_tensor_tensor(PT[:, k, :], PT[:, k, :], g[:, k:k + 1], r[:, j, :],
                                                           ALU.mult, ALU.mult)


def attention(nc, io, PT, MIX, ident):
    PAIRS = HEADS // 2
    with ExitStack() as c:
        sb = lambda n, s: c.enter_context(nc.sbuf_tensor(n, s, F32))
        cs = sb("at_cs", [P, TOK])
        w = [sb(f"at_w{j}", [P, 5, P]) for j in range(2)]
        q = [sb(f"at_q{j}", [96, TOK]) for j in range(2)]
        k = [sb(f"at_k{j}", [96, TOK]) for j in range(2)]
        v = [sb(f"at_v{j}", [P, TILES, V_DIM]) for j in range(2)]
        rot = sb("at_rot", [P, 2, TOK])
        prob = [sb(f"at_p{j}", [P, TOK]) for j in range(2)]
        probT = [sb(f"at_pT{j}", [P, TOK]) for j in range(2)]
        small = sb("at_small", [P, 2, 4])
        ps = lambda n, s: c.enter_context(nc.psum_tensor(n, s, F32))
        A = [ps(f"at_A{j}", [P, 1024]) for j in range(2)]
        T = ps("at_T", [P, 1024])
        C = ps("at_C", [P, TILES, V_DIM])
        O0 = ps("at_O", [P, P])
        O = (O0[0:64, :], C[0:64, 0:2, :].rearrange("p a d -> p (a d)"))
        names = ("cs_in", "w_in0", "w_in1", "proj_done", "qkv_copied", "roped", "score", "maxed", "exped",
                 "normed", "turned", "pt_copied", "av_done", "out_copied", "own")
        with signals(nc, *names) as (cs_in, w_in0, w_in1, proj_done, qkv_copied, roped, score, maxed, exped,
                                     normed, turned, pt_copied, av_done, out_copied, own):
            w_in = (w_in0, w_in1)
            keys = lambda i: CTX if i < CTX_TILES else TOK
            with nc.Block() as block:
                @block.sync
                def _(sp):
                    sp.dma_start(cs[64:128, :], io["rope"]).then_inc(cs_in, 16)
                    for j in range(2):
                        sp.dma_start(w[j][:, :, :], io["ev_w_up"][j].rearrange("p (k m) -> p k m", k=5)).then_inc(w_in[j], 16)
                    with sp.Fori(1, PAIRS) as it:
                        for j in range(2):
                            sp.wait_ge(proj_done, it * 2 + (j - 1))
                            sp.dma_start(w[j][:, :, :], io["ev_w_up"][bass.ds(it * 2 + j, 1)].rearrange("o p (k m) -> p (o k) m", k=5)).then_inc(w_in[j], 16)

                @block.tensor
                def _(pe):
                    def scores(h6, j, i):
                        if i >= 2:
                            pe.wait_ge(exped, h6 + i)
                        n = keys(i)
                        for a in range(0, n, 512):
                            b = min(n, a + 512)
                            last = nc.tensor.matmul(A[i % 2][:, a:b], q[j][:, i * P:i * P + P], k[j][:, a:b],
                                                    start=True, stop=True)
                        last.then_inc(score, 1)

                    with pe.Fori(0, PAIRS) as it:
                        for j in range(2):
                            h6 = it * 12 + 6 * j
                            pe.wait_ge(w_in[j], it * 16 + 16)
                            pe.wait_ge(exped, h6 + 1)
                            pe.wait_ge(qkv_copied, it * 6 + (3 * j + 1))
                            pe.wait_ge(out_copied, h6 + 2)
                            for a, n in HALVES:
                                for kk in range(3):
                                    nc.tensor.matmul(A[0][:, a:a + n], w[j][:, kk, :], PT[:, kk, a:a + n],
                                                     start=(kk == 0), stop=(kk == 2))
                            for a, n in HALVES:
                                for kk in range(2):
                                    nc.tensor.matmul(A[1][0:64, a:a + n], w[j][:, 3 + kk, 0:64], PT[:, C_KV + kk, a:a + n],
                                                     start=(kk == 0), stop=(kk == 1))
                            for t in range(TILES):
                                for kk in range(2):
                                    last = nc.tensor.matmul(C[:, t, :], PT[:, C_KV + kk, t * P:t * P + P],
                                                            w[j][:, 3 + kk, 64:128], start=(kk == 0), stop=(kk == 1))
                            last.then_inc(proj_done, 1)
                            pe.wait_ge(qkv_copied, it * 6 + (3 * j + 4))
                            pe.wait_ge(roped, it * 2 + (j + 1))
                            scores(h6, j, 0)
                            scores(h6, j, 1)
                            for i in range(TILES):
                                n = keys(i)
                                pe.wait_ge(normed, h6 + (i + 1))
                                pe.wait_ge(pt_copied, h6 + (i + 1))
                                for b in range(n // P):
                                    last = nc.tensor.transpose(T[:, b * P:b * P + P], prob[i % 2][:, b * P:b * P + P], ident[:, :])
                                last.then_inc(turned, 1)
                                if i + 2 < TILES:
                                    scores(h6, j, i + 2)
                                pe.wait_ge(pt_copied, h6 + (i + 2))
                                pe.wait_ge(out_copied, h6 + (i + 1))
                                for b in range(n // P):
                                    last = nc.tensor.matmul(O[i % 2], v[j][:, b, :], probT[i % 2][:, b * P:b * P + P],
                                                            start=(b == 0), stop=(b == n // P - 1))
                                last.then_inc(av_done, 1)

                @block.scalar
                def _(act):
                    act.wait_ge(cs_in, 16)
                    act.sem_inc(exped, 1)
                    act.sem_inc(qkv_copied, 1)
                    act.sem_inc(pt_copied, 1)
                    with act.Fori(0, PAIRS) as it:
                        for j in range(2):
                            h6 = it * 12 + 6 * j
                            act.wait_ge(proj_done, it * 2 + (j + 1))
                            nc.scalar.activation(q[j][0:64, :], A[0][0:64, 0:TOK], ACT.Copy).then_inc(qkv_copied, 1)
                            nc.scalar.activation(k[j][0:64, :], A[1][0:64, 0:TOK], ACT.Copy).then_inc(qkv_copied, 1)
                            nc.scalar.activation(v[j][:, :, :], C[:, :, :], ACT.Copy).then_inc(qkv_copied, 1)
                            for i in range(TILES + 1):
                                if i < TILES:
                                    n = keys(i)
                                    act.wait_ge(maxed, h6 + (i + 1))
                                    act.wait_ge(turned, h6 + (i + 1))
                                    nc.scalar.activation(prob[i % 2][:, 0:n], A[i % 2][:, 0:n], ACT.Exp, scale=MLA_SCALE,
                                                         bias=small[:, i % 2, 1:2], accum_out=small[:, i % 2, 2:3]).then_inc(exped, 1)
                                if i >= 1:
                                    n = keys(i - 1)
                                    act.wait_ge(turned, h6 + (i + 2))
                                    act.wait_ge(av_done, h6 + i)
                                    nc.scalar.activation(probT[(i - 1) % 2][:, 0:n], T[:, 0:n], ACT.Copy).then_inc(pt_copied, 1)

                @block.gpsimd
                def _(pool):
                    pool.sem_inc(turned, 2)
                    pool.sem_inc(av_done, 2)
                    pool.sem_inc(out_copied, 2)

                @block.vector
                def _(dve):
                    step = InOrder(dve, own)
                    dve.wait_ge(cs_in, 16)
                    for j in range(2):
                        nc.vector.tensor_copy(k[j][64:96, :], PT[KPE:KPE + ROPE, C_MISC, :])
                    with dve.Fori(0, PAIRS) as it:
                        step.start(it, 28)
                        for j in range(2):
                            h6 = it * 12 + 6 * j
                            dve.wait_ge(proj_done, it * 2 + (j + 1))
                            step.mark(nc.vector.tensor_tensor(rot[64:96, 0, :], A[0][96:128, 0:TOK], cs[96:128, :], ALU.mult))
                            step(nc.vector.tensor_tensor(rot[64:96, 1, :], A[0][64:96, 0:TOK], cs[64:96, :], ALU.mult))
                            nc.vector.tensor_tensor(q[j][64:96, :], rot[64:96, 0, :], rot[64:96, 1, :], ALU.add).then_inc(roped, 1)
                            for i in range(TILES + 2):
                                if i < TILES:
                                    n = keys(i)
                                    dve.wait_ge(score, h6 + (i + 1))
                                    step(nc.vector.tensor_reduce(small[:, i % 2, 0:1], A[i % 2][:, 0:n], AX.X, ALU.max, negate=True))
                                    nc.vector.tensor_scalar(small[:, i % 2, 1:2], small[:, i % 2, 0:1], MLA_SCALE, None,
                                                            ALU.mult).then_inc(maxed, 1)
                                if 1 <= i <= TILES:
                                    e = i - 1
                                    n = keys(e)
                                    dve.wait_ge(exped, h6 + (e + 2))
                                    step(nc.vector.reciprocal(small[:, e % 2, 3:4], small[:, e % 2, 2:3]))
                                    nc.vector.tensor_scalar(prob[e % 2][:, 0:n], prob[e % 2][:, 0:n], small[:, e % 2, 3:4], None,
                                                            ALU.mult).then_inc(normed, 1)
                                if i >= 2:
                                    o = i - 2
                                    dve.wait_ge(av_done, h6 + (o + 3))
                                    nc.vector.tensor_copy(MIX[64 * j:64 * j + 64, bass.ds(it, 1), o * P:o * P + P].rearrange("p o t -> p (o t)"),
                                                          O[o % 2]).then_inc(out_copied, 1)
                        assert step.n == 28, step.n


VISITS = (list(range(CHUNKS)),
          list(range(CTX_CHUNKS - 1, -1, -1)) + list(range(CHUNKS - 1, CTX_CHUNKS - 1, -1)))
MID = (CHUNK // 2 - 1, CHUNK // 2)
LAST = (CHUNK - 1, 0)


def by_chunk(a):
    return a.rearrange("p (c i) -> p c i", i=CHUNK)


def gla_decays(nc, io, PT, p, g):
    LIM = 80.0 * TAU
    with ExitStack() as c:
        sb = lambda n, s: c.enter_context(nc.sbuf_tensor(f"{n}{p}", s, F32))
        wa = sb("g_wa", [64, GH * GDK])
        ba = sb("g_ba", [P, 2, 2])
        reset = sb("g_reset", [P, 2, TOK])
        z = sb("g_z", [P, 2, TOK])
        az = sb("g_az", [P, 2, TOK])
        cum = sb("g_cum", [P, 2, TOK])
        ex = sb("g_ex", [P, 2, TOK])
        Z = [c.enter_context(nc.psum_tensor(f"g_Z{d}{p}", [P, 1024], F32)) for d in range(2)]
        with signals(nc, "loaded", "reset_set", "z_prod", "z_read", "logs", "mid_diff", "cum_done", "total_diff", "exp_done",
                     "ex_used", "own", "aown") as (
                loaded, reset_set, z_prod, z_read, logs, mid_diff, cum_done, total_diff, exp_done, ex_used, own, aown):
            with nc.Block() as block:
                @block.sync
                def _(sp):
                    sp.dma_start(wa[0:GRANK, :], io["gla_wa2"][0]).then_inc(loaded, 16)
                    sp.dma_start(wa[32:32 + GRANK, :], io["gla_wa2"][1]).then_inc(loaded, 16)
                    sp.dma_start(ba[:, :, :], io["gla_ba"]).then_inc(loaded, 16)

                @block.gpsimd
                def _(pool):
                    nc.gpsimd.memset(reset[:, :, :], 1.0).then_inc(reset_set, 1)
                    pool.wait_ge(reset_set, 1)
                    nc.gpsimd.memset(by_chunk(reset[:, 0, :])[:, :, 0:1], 0.0).then_inc(reset_set, 1)
                    nc.gpsimd.memset(by_chunk(reset[:, 1, :])[:, :, CHUNK - 1:CHUNK], 0.0).then_inc(reset_set, 1)

                @block.tensor
                def _(pe):
                    pe.wait_ge(loaded, 48)
                    for d in range(2):
                        for a, m in HALVES:
                            last = nc.tensor.matmul(Z[d][:, a:a + m], wa[32 * d:32 * d + GRANK, p * P:p * P + P],
                                                    PT[32 * d:32 * d + GRANK, C_MISC, a:a + m], start=True, stop=True)
                        last.then_inc(z_prod, 1)

                @block.scalar
                def _(act):
                    step = InOrder(act, aown)
                    for d in range(2):
                        act.wait_ge(z_prod, d + 1)
                        nc.scalar.activation(z[:, d, :], Z[d][:, 0:TOK], ACT.Identity, bias=ba[:, p, d:d + 1]).then_inc(z_read, 1)
                    act.wait_ge(z_read, 2)
                    step(nc.scalar.activation(az[:, :, :], z[:, :, :], ACT.Abs))
                    step(nc.scalar.activation(az[:, :, :], az[:, :, :], ACT.Exp, scale=-1.0))
                    nc.scalar.activation(az[:, :, :], az[:, :, :], ACT.Ln, bias=1.0).then_inc(logs, 1)
                    act.wait_ge(mid_diff, 1)
                    nc.scalar.activation(ex[:, :, :], z[:, :, :], ACT.Exp, scale=1.0 / TAU).then_inc(exp_done, 1)
                    act.wait_ge(ex_used, 2)
                    nc.scalar.activation(ex[:, :, :], z[:, :, :], ACT.Exp, scale=-1.0 / TAU).then_inc(exp_done, 1)
                    act.wait_ge(ex_used, 3)
                    nc.scalar.activation(ex[:, :, :], cum[:, :, :], ACT.Exp, scale=1.0 / TAU).then_inc(exp_done, 1)
                    act.wait_ge(ex_used, 5)
                    act.wait_ge(total_diff, 1)
                    nc.scalar.activation(ex[:, :, :], az[:, :, :], ACT.Exp, scale=1.0 / TAU).then_inc(exp_done, 1)
                    for d in range(2):
                        nc.scalar.activation(g["dec"][:, d, :], by_chunk(cum[:, d, :])[:, :, LAST[d]], ACT.Exp, scale=1.0 / TAU)

                @block.vector
                def _(dve):
                    step = InOrder(dve, own)
                    dve.wait_ge(reset_set, 3)
                    dve.wait_ge(logs, 1)
                    step(nc.vector.scalar_tensor_tensor(z[:, :, :], z[:, :, :], 0.0, az[:, :, :], ALU.min, ALU.subtract))
                    step.mark(nc.vector.tensor_tensor_scan(cum[:, 0, :], reset[:, 0, :], z[:, 0, :], 0.0, ALU.mult, ALU.add))
                    step(nc.vector.tensor_tensor_scan(cum[:, 1, ::-1], reset[:, 1, ::-1], z[:, 1, ::-1], 0.0, ALU.mult, ALU.add))
                    for d in range(2):
                        cc = by_chunk(cum[:, d, :])
                        step.mark(nc.vector.tensor_tensor(by_chunk(z[:, d, :]), cc, cc[:, :, MID[d]:MID[d] + 1].broadcast_to([P, CHUNKS, CHUNK]), ALU.subtract))
                    step.wait()
                    nc.vector.tensor_scalar(z[:, :, :], z[:, :, :], LIM, -LIM, ALU.min, ALU.max).then_inc(mid_diff, 1)
                    for d in range(2):
                        cc = by_chunk(cum[:, d, :])
                        step.mark(nc.vector.tensor_tensor(by_chunk(az[:, d, :]), cc[:, :, LAST[d]:LAST[d] + 1].broadcast_to([P, CHUNKS, CHUNK]), cc, ALU.subtract))
                    step.wait()
                    nc.vector.memset(reset[0:1, 0, 0:1], 0.0).then_inc(total_diff, 1)
                    q, k = PT[:, C_GQ + p, :], PT[:, C_GK + p, :]
                    both = lambda a: a.unsqueeze(1).broadcast_to([a.shape[0], 2, TOK])
                    dve.wait_ge(exp_done, 1)
                    for h in range(2):
                        rows = slice(64 * h, 64 * h + 64)
                        nc.vector.scalar_tensor_tensor(g["qe"][rows, :, h, :], ex[rows, :, :], GDK ** -0.5, both(q[rows, :]),
                                                       ALU.mult, ALU.mult).then_inc(ex_used, 1)
                    dve.wait_ge(exp_done, 2)
                    nc.vector.tensor_tensor(g["ke"][:, :, :], ex[:, :, :], both(k), ALU.mult).then_inc(ex_used, 1)
                    dve.wait_ge(exp_done, 3)
                    for h in range(2):
                        rows = slice(64 * h, 64 * h + 64)
                        nc.vector.scalar_tensor_tensor(g["qs"][rows, :, h, :], ex[rows, :, :], GDK ** -0.5, both(q[rows, :]),
                                                       ALU.mult, ALU.mult).then_inc(ex_used, 1)
                    dve.wait_ge(exp_done, 4)
                    nc.vector.tensor_tensor(g["kw"][:, :, :], ex[:, :, :], both(k), ALU.mult)


def gla_states(nc, V, ident, p, g):
    with ExitStack() as c:
        kwr = c.enter_context(nc.sbuf_tensor(f"g_kwr{p}", [P, 2, TILES, P], F32))
        T = c.enter_context(nc.psum_tensor(f"g_T{p}", [P, 2, 4, P], F32))
        U = [c.enter_context(nc.psum_tensor(f"g_U{j}{p}", [P, 4, GDV], F32)) for j in range(4)]
        slot = lambda ch: U[2 * (ch % 2) + (ch // 2) // 4][:, (ch // 2) % 4, :]
        kw, S, dec = g["kw"], g["S"], g["dec"]
        with signals(nc, "turned", "copied", "update_done", "state_done", "own") as (turned, copied, update_done, state_done, own):
            with nc.Block() as block:
                @block.tensor
                def _(pe):
                    for d in range(2):
                        if d:
                            pe.wait_ge(copied, 2 * d)
                        for t in range(TILES):
                            last = nc.tensor.transpose(T[:, t // 4, t % 4, :], kw[:, d, t * P:t * P + P], ident[:, :])
                        last.then_inc(turned, 1)
                        pe.wait_ge(copied, 2 * d + 2)
                        if d:
                            pe.wait_ge(state_done, d)
                        for ch in range(CHUNKS):
                            j0 = CHUNK * (ch % 2)
                            for h in range(2):
                                last = nc.tensor.matmul(slot(ch)[64 * h:64 * h + 64, :],
                                                        kwr[j0:j0 + CHUNK, d, ch // 2, 64 * h:64 * h + 64],
                                                        V[j0:j0 + CHUNK, ch // 2, (2 * p + h) * GDV:(2 * p + h + 1) * GDV],
                                                        start=True, stop=True)
                        last.then_inc(update_done, 1)

                @block.scalar
                def _(act):
                    for d in range(2):
                        act.wait_ge(turned, d + 1)
                        nc.scalar.activation(kwr[:, d, 0:4, :], T[:, 0, :, :], ACT.Copy).then_inc(copied, 1)
                        nc.scalar.activation(kwr[:, d, 4:6, :], T[:, 1, 0:2, :], ACT.Copy).then_inc(copied, 1)

                @block.vector
                def _(dve):
                    step = InOrder(dve, own)
                    for d in range(2):
                        dve.wait_ge(update_done, d + 1)
                        order = VISITS[d]
                        step(nc.vector.tensor_copy(S[:, d, order[1], :], slot(order[0])))
                        for ch, nxt in zip(order[1:], order[2:]):
                            ins = nc.vector.scalar_tensor_tensor(S[:, d, nxt, :], S[:, d, ch, :], dec[:, d, ch:ch + 1], slot(ch),
                                                                 ALU.mult, ALU.add)
                            step(ins)
                        nc.vector.memset(g["tick"][:, :], 0.0).then_inc(state_done, 1)


def gla_outputs(nc, V, MIX, keep, p, g):
    with ExitStack() as c:
        SC = [[c.enter_context(nc.psum_tensor(f"g_SC{b}{d}{p}", [P, P], F32)) for d in range(2)] for b in range(2)]
        O = [c.enter_context(nc.psum_tensor(f"g_O{b}{p}", [P, P], F32)) for b in range(2)]
        qe, ke, qs, S, sc = g["qe"], g["ke"], g["qs"], g["S"], g["sc"]
        with signals(nc, "score", "kept", "out_done", "out_copied") as (score, kept, out_done, out_copied):
            with nc.Block() as block:
                @block.tensor
                def _(pe):
                    def scores(n):
                        h, t = divmod(n, TILES)
                        if n >= 2:
                            pe.wait_ge(kept, 2 * (n - 1))
                        for d in range(2):
                            last = nc.tensor.matmul(SC[n % 2][d][:, :], ke[:, d, t * P:t * P + P], qe[:, d, h, t * P:t * P + P],
                                                    start=True, stop=True)
                        last.then_inc(score, 1)

                    scores(0)
                    for n in range(2 * TILES):
                        h, t = divmod(n, TILES)
                        v = V[:, t, (2 * p + h) * GDV:(2 * p + h + 1) * GDV]
                        if n + 1 < 2 * TILES:
                            scores(n + 1)
                        if n >= 2:
                            pe.wait_ge(out_copied, n - 1)
                        pe.wait_ge(kept, 2 * n + 2)
                        nc.tensor.matmul(O[n % 2][:, :], v, sc[:, n % 2, 0, :], start=True, stop=False)
                        for d in range(2):
                            for ch in (2 * t, 2 * t + 1):
                                if ch != VISITS[d][0]:
                                    i0 = CHUNK * (ch % 2)
                                    nc.tensor.matmul(O[n % 2][:, i0:i0 + CHUNK], S[:, d, ch, :],
                                                     qs[:, d, h, ch * CHUNK:ch * CHUNK + CHUNK], start=False, stop=False)
                        nc.tensor.matmul(O[n % 2][:, :], v, sc[:, n % 2, 1, :], start=False, stop=True).then_inc(out_done, 1)

                @block.vector
                def _(dve):
                    for n in range(2 * TILES):
                        dve.wait_ge(score, n + 1)
                        if n >= 2:
                            dve.wait_ge(out_done, n - 1)
                        for d in range(2):
                            nc.vector.copy_predicated(sc[:, n % 2, d, :], keep[:, d, :], SC[n % 2][d][:, :]).then_inc(kept, 1)

                @block.scalar
                def _(act):
                    for n in range(2 * TILES):
                        h, t = divmod(n, TILES)
                        act.wait_ge(out_done, n + 1)
                        nc.scalar.activation(MIX[:, 4 + 2 * p + h, t * P:t * P + P], O[n % 2][:, :], ACT.Copy).then_inc(out_copied, 1)


def gla_norm_gate(nc, io, PT, MIX, ones):
    with ExitStack() as c:
        sb = lambda n, s: c.enter_context(nc.sbuf_tensor(n, s, F32))
        sq = sb("gn_sq", [P, GH, TOK])
        gain = sb("gn_gain", [P, GH])
        eps = sb("gn_eps", [P, 1])
        ss = [c.enter_context(nc.psum_tensor(f"gn_ss{h}", [P, 1024], F32)) for h in range(GH)]
        with signals(nc, "loaded", "eps_set", "squared", "summed", "rooted", "gated", "own") as (
                loaded, eps_set, squared, summed, rooted, gated, own):
            with nc.Block() as block:
                @block.sync
                def _(sp):
                    sp.dma_start(gain[:, :], io["gla_gain"]).then_inc(loaded, 16)

                @block.tensor
                def _(pe):
                    for h in range(GH):
                        pe.wait_ge(squared, h + 1)
                        for a, m in HALVES:
                            last = nc.tensor.matmul(ss[h][:, a:a + m], ones[:, :], sq[:, h, a:a + m], start=True, stop=True)
                        last.then_inc(summed, 1)

                @block.scalar
                def _(act):
                    nc.scalar.activation(PT[:, C_GG:C_GG + GH, :], PT[:, C_GG:C_GG + GH, :], ACT.Silu).then_inc(gated, 1)
                    act.wait_ge(eps_set, 1)
                    for h in range(GH):
                        act.wait_ge(summed, h + 1)
                        nc.scalar.activation(sq[:, h, :], ss[h][:, 0:TOK], ACT.Sqrt, scale=1.0 / GDV, bias=eps[:, :]).then_inc(rooted, 1)

                @block.vector
                def _(dve):
                    step = InOrder(dve, own)
                    nc.vector.memset(eps[:, :], EPS).then_inc(eps_set, 1)
                    for h in range(GH):
                        nc.vector.tensor_tensor(sq[:, h, :], MIX[:, 4 + h, :], MIX[:, 4 + h, :], ALU.mult).then_inc(squared, 1)
                    dve.wait_ge(loaded, 16)
                    dve.wait_ge(gated, 1)
                    for h in range(GH):
                        dve.wait_ge(rooted, h + 1)
                        step(nc.vector.reciprocal(sq[:, h, :], sq[:, h, :]))
                        step(nc.vector.scalar_tensor_tensor(MIX[:, 4 + h, :], MIX[:, 4 + h, :], gain[:, h:h + 1], sq[:, h, :],
                                                            ALU.mult, ALU.mult))
                        nc.vector.tensor_tensor(MIX[:, 4 + h, :], MIX[:, 4 + h, :], PT[:, C_GG + h, :], ALU.mult)


def gla(nc, io, PT, V, MIX, ident, ones):
    with ExitStack() as c:
        sb = lambda n, s, d=F32: c.enter_context(nc.sbuf_tensor(n, s, d))
        g = {"qe": sb("g_qe", [P, 2, 2, TOK]),
             "qs": sb("g_qs", [P, 2, 2, TOK]),
             "ke": sb("g_ke", [P, 2, TOK]),
             "kw": sb("g_kw", [P, 2, TOK]),
             "dec": sb("g_dec", [P, 2, CHUNKS]),
             "tick": sb("g_tick", [1, 1]),
             "S": sb("g_S", [P, 2, CHUNKS, GDV]),
             "sc": sb("g_sc", [P, 2, 2, P])}
        keep = sb("g_keep", [P, 2, P], I32)
        with signals(nc, "keep_in") as (keep_in,):
            with nc.Block() as block:
                @block.sync
                def _(sp):
                    sp.dma_start(keep[:, :, :], io["gla_keep"]).then_inc(keep_in, 16)
                    sp.wait_ge(keep_in, 16)

                @block.gpsimd
                def _(pool):
                    nc.gpsimd.memset(g["qe"][:, :, :, :], 0.0)
                    nc.gpsimd.memset(g["sc"][:, :, :, :], 0.0)

                @block.vector
                def _(dve):
                    nc.vector.memset(g["qs"][:, :, :, :], 0.0)
        for p in range(GH // 2):
            gla_decays(nc, io, PT, p, g)
            gla_states(nc, V, ident, p, g)
            gla_outputs(nc, V, MIX, keep, p, g)
    gla_norm_gate(nc, io, PT, MIX, ones)


def project_and_norm(nc, io, mods, H, src, w_name, tiles, layer, which, tag):
    o_gate = (layer * N_MOD + 2 + 3 * which) * D
    row = 2 * layer + which
    nk = src.shape[1] if w_name else 0
    with ExitStack() as c:
        sb = lambda n, s: c.enter_context(nc.sbuf_tensor(f"{tag}_{n}", s, F32))
        vec = sb("vec", [P, 4, D])
        w = sb("w", [P, max(nk, 1), D])
        y = [sb(f"y{j}", [P, D]) for j in range(2)]
        stats = sb("stats", [P, 2, 2, 6])
        mv = sb("mv", [P, 2, 4])
        eps = sb("eps", [P, 1])
        ps = [c.enter_context(nc.psum_tensor(f"{tag}_ps{j}", [P, D], F32)) for j in range(2)]
        with signals(nc, "vec_in", "w_in", "prod", "read", "var_done", "rooted", "eps_set", "scaled", "normed", "own", "pown") as (
                vec_in, w_in, prod, read, var_done, rooted, eps_set, scaled, normed, own, pown):
            with nc.Block() as block:
                @block.sync
                def _(sp):
                    if w_name:
                        for k in range(nk):
                            sp.dma_start(w[:, k, :], io[w_name][:, k, :]).then_inc(w_in, 16)
                    for v in range(2):
                        sp.dma_start(vec[:, v, :], row_to_all(mods[v, o_gate:o_gate + D], D)).then_inc(vec_in, 16)
                    sp.dma_start(vec[:, 2, :], row_to_all(io["ln_g"][row], D)).then_inc(vec_in, 16)
                    sp.dma_start(vec[:, 3, :], row_to_all(io["ln_b"][row], D)).then_inc(vec_in, 16)

                @block.tensor
                def _(pe):
                    if w_name:
                        pe.wait_ge(w_in, 16 * nk)
                        for i, t in enumerate(tiles):
                            if i >= 2:
                                pe.wait_ge(read, i - 1)
                            for h in range(2):
                                for k in range(nk):
                                    last = nc.tensor.matmul(ps[i % 2][:, h * 512:h * 512 + 512], src[:, k, (t - tiles[0]) * P:(t - tiles[0] + 1) * P],
                                                            w[:, k, h * 512:h * 512 + 512], start=(k == 0), stop=(k == nk - 1))
                            last.then_inc(prod, 1)

                @block.scalar
                def _(act):
                    act.wait_ge(eps_set, 1)
                    for i, t in enumerate(tiles):
                        act.wait_ge(var_done, i + 1)
                        nc.scalar.activation(mv[:, i % 2, 2:3], mv[:, i % 2, 1:2], ACT.Sqrt, bias=eps[:, :]).then_inc(rooted, 1)

                @block.vector
                def _(dve):
                    step = InOrder(dve, own)
                    nc.vector.memset(eps[:, :], EPS).then_inc(eps_set, 1)
                    dve.wait_ge(vec_in, 64)

                    def finish(i):
                        dve.wait_ge(rooted, i + 1)
                        yi = y[i % 2]
                        step(nc.vector.reciprocal(mv[:, i % 2, 3:4], mv[:, i % 2, 2:3]))
                        nc.vector.tensor_scalar(yi[:, :], yi[:, :], mv[:, i % 2, 0:1], mv[:, i % 2, 3:4],
                                                ALU.subtract, ALU.mult).then_inc(scaled, 1)

                    for i, t in enumerate(tiles):
                        yi = y[i % 2]
                        if i >= 2:
                            dve.wait_ge(normed, i - 1)
                        if w_name:
                            dve.wait_ge(prod, i + 1)
                            f = ps[i % 2][:, :]
                        else:
                            f = src[:, t, :]
                        ins = nc.vector.tensor_tensor(yi[:, :], f, vec[:, 1 if t < CTX_TILES else 0, :], ALU.mult)
                        ins.then_inc(read, 1)
                        dve.wait_ge(read, i + 1)
                        step(nc.vector.scalar_tensor_tensor(yi[:, :], H[:, t, :], ALPHA, yi[:, :], ALU.mult, ALU.add))
                        for h in range(2):
                            step.mark(nc.vector.bn_stats(stats[:, i % 2, h, :], yi[:, h * 512:h * 512 + 512]))
                        step.wait()
                        nc.vector.bn_aggr(mv[:, i % 2, 0:2], stats[:, i % 2, :, :].rearrange("p h s -> p (h s)")).then_inc(var_done, 1)
                        if i >= 1:
                            finish(i - 1)
                    finish(len(tiles) - 1)

                @block.gpsimd
                def _(pool):
                    step = InOrder(pool, pown)
                    pool.wait_ge(vec_in, 64)
                    for i, t in enumerate(tiles):
                        pool.wait_ge(scaled, i + 1)
                        step(nc.gpsimd.tensor_tensor(y[i % 2][:, :], y[i % 2][:, :], vec[:, 2, :], ALU.mult))
                        nc.gpsimd.tensor_tensor(H[:, t, :], y[i % 2][:, :], vec[:, 3, :], ALU.add).then_inc(normed, 1)


def peer_scores(nc, io, XT, SCO, layer, first_tile):
    N = 2 * PH
    c0 = first_tile * P
    spans = [(a, min(512, TOK - a)) for a in range(c0, TOK, 512)]
    nt = TILES - first_tile
    with ExitStack() as c:
        w = [c.enter_context(nc.sbuf_tensor(f"sc_w{j}{layer}", [P, KD, P], F32)) for j in range(2)]
        keys = c.enter_context(nc.sbuf_tensor(f"sc_keys{layer}", [P, 2, P], F32))
        qT = [c.enter_context(nc.sbuf_tensor(f"sc_qT{j}{layer}", [P, TOK], F32)) for j in range(2)]
        Q = [c.enter_context(nc.psum_tensor(f"sc_Q{j}{layer}", [P, 1024], F32)) for j in range(2)]
        S = [c.enter_context(nc.psum_tensor(f"sc_S{j}{layer}", [P, 8, P], F32)) for j in range(2)]
        with signals(nc, "keys_in", "w_in0", "w_in1", "q_prod", "q_copied", "s_prod", "s_copied") as (
                keys_in, w_in0, w_in1, q_prod, q_copied, s_prod, s_copied):
            w_in = (w_in0, w_in1)
            src = io["peer_wq"][layer]
            with nc.Block() as block:
                @block.sync
                def _(sp):
                    sp.dma_start(keys[:, :, :], io["peer_keys"][layer]).then_inc(keys_in, 16)
                    for j in range(2):
                        sp.dma_start(w[j][:, :, :], src[j].rearrange("p (k m) -> p k m", k=KD)).then_inc(w_in[j], 16)
                    with sp.Fori(1, N // 2) as it:
                        for j in range(2):
                            sp.wait_ge(q_prod, it * 2 + (j - 1))
                            sp.dma_start(w[j][:, :, :], src[bass.ds(it * 2 + j, 1)].rearrange("o p (k m) -> p (o k) m", k=KD)).then_inc(w_in[j], 16)

                @block.tensor
                def _(pe):
                    pe.wait_ge(keys_in, 16)
                    with pe.Fori(0, N // 2) as it:
                        for j in range(2):
                            pe.wait_ge(w_in[j], it * 16 + 16)
                            pe.wait_ge(q_copied, it * 2 + (j + 1))
                            for a, n in spans:
                                for k in range(KD):
                                    last = nc.tensor.matmul(Q[j][:, a - c0:a - c0 + n], w[j][:, k, :], XT[:, k, a:a + n],
                                                            start=(k == 0), stop=(k == KD - 1))
                            last.then_inc(q_prod, 1)
                        for j in range(2):
                            pe.wait_ge(q_copied, it * 2 + (j + 3))
                            pe.wait_ge(s_copied, it * 2 + (j + 1))
                            for t in range(nt):
                                last = nc.tensor.matmul(S[j][:, t, :], qT[j][:, t * P:t * P + P], keys[:, j, :], start=True, stop=True)
                            last.then_inc(s_prod, 1)

                @block.scalar
                def _(act):
                    act.sem_inc(q_copied, 2)
                    act.sem_inc(s_prod, 2)
                    with act.Fori(0, N // 2) as it:
                        for j in range(2):
                            act.wait_ge(q_prod, it * 2 + (j + 1))
                            act.wait_ge(s_prod, it * 2 + (j + 1))
                            nc.scalar.activation(qT[j][:, 0:nt * P], Q[j][:, 0:nt * P], ACT.Copy).then_inc(q_copied, 1)

                @block.vector
                def _(dve):
                    dve.sem_inc(s_copied, 2)
                    with dve.Fori(0, PH) as h:
                        for j in range(2):
                            dve.wait_ge(s_prod, h * 2 + (j + 3))
                            nc.vector.tensor_copy(SCO[:, first_tile:TILES, bass.ds(h * 2 + j, 1), :].rearrange("p t o k -> p t (o k)"),
                                                  S[j][:, 0:nt, :]).then_inc(s_copied, 1)


RECTS = ((0, 1, 16), (1, 4, 8), (4, 8, 4), (8, 16, 1))
CAND = sum((a1 - a0) * nb for a0, a1, nb in RECTS)


def peer_topk(nc, io, SCO, I1, I2, GW, layer, first_tile):
    with ExitStack() as c:
        sb = lambda n, s, d=F32: c.enter_context(nc.sbuf_tensor(f"tk_{n}{layer}", s, d))
        s = sb("s", [P, 2 * PH, P])
        s2 = sb("s2", [P, 2 * PH, P])
        top = sb("top", [P, PH, 2, PTOP])
        ti = sb("ti", [P, PH, 2, PTOP], U32)
        tf = sb("tf", [P, PH, 2, PTOP])
        cand = sb("cand", [P, PH, CAND])
        cand2 = sb("cand2", [P, PH, CAND])
        ci = sb("ci", [P, 2, PH, CAND])
        best = sb("best", [P, PH, PTOP])
        pos = sb("pos", [P, PH, PTOP], U32)
        posf = sb("posf", [P, PH, PTOP])
        iota = sb("iota", [P, CAND])
        eq = sb("eq", [P, PH, PTOP, CAND])
        mul = sb("mul", [P, PH, PTOP, CAND])
        ex = sb("ex", [P, PH, PTOP])
        sm = sb("sm", [P, PH, 2])
        tick = sb("tick", [1, 1])
        with signals(nc, "iota_in", "staged", "read", "shifted", "exped", "own") as (iota_in, staged, read, shifted, exped, own):
            with nc.Block() as block:
                @block.sync
                def _(sp):
                    sp.dma_start(iota[:, :], io["iota"][:, 0:CAND]).then_inc(iota_in, 16)

                @block.scalar
                def _(act):
                    act.sem_inc(exped, 1)
                    with act.Fori(first_tile, TILES) as t:
                        act.wait_ge(read, t + (1 - first_tile))
                        nc.scalar.activation(s[:, :, :], SCO[:, bass.ds(t, 1), :, :].rearrange("p o h k -> p (o h) k"),
                                             ACT.Copy).then_inc(staged, 1)
                        act.wait_ge(shifted, t + (1 - first_tile))
                        nc.scalar.activation(ex[:, :, :], ex[:, :, :], ACT.Exp).then_inc(exped, 1)

                @block.vector
                def _(dve):
                    step = InOrder(dve, own)

                    def settle():
                        step.wait()
                        step.mark(nc.vector.memset(tick[:, :], 0.0))

                    def best16(src, rest, values, places):
                        n = len(src)
                        for x in range(n):
                            step.mark(nc.vector.max(values[x][:, 0:8], src[x]))
                        settle()
                        for x in range(n):
                            step.mark(nc.vector.max_index(places[x][:, 0:8], values[x][:, 0:8], src[x]))
                            step.mark(nc.vector.match_replace(rest[x], values[x][:, 0:8], src[x], -3.0e38))
                        settle()
                        for x in range(n):
                            step.mark(nc.vector.max(values[x][:, 8:16], rest[x]))
                        settle()
                        for x in range(n):
                            step.mark(nc.vector.max_index(places[x][:, 8:16], values[x][:, 8:16], rest[x]))
                        settle()

                    dve.sem_inc(read, 1)
                    dve.wait_ge(iota_in, 16)
                    with dve.Fori(first_tile, TILES) as t:
                        n = t - first_tile if first_tile else t
                        step.start(n, TOPK_STEPS)
                        dve.wait_ge(staged, n + 1)
                        step.mark(nc.vector.memset(tick[:, :], 0.0))
                        best16([s[:, x, :] for x in range(2 * PH)], [s2[:, x, :] for x in range(2 * PH)],
                               [top[:, x // 2, x % 2, :] for x in range(2 * PH)], [ti[:, x // 2, x % 2, :] for x in range(2 * PH)])
                        dve.sem_inc(read, 1)
                        step.mark(nc.vector.tensor_copy(tf[:, :, :, :], ti[:, :, :, :]))
                        at = 0
                        for a0, a1, nb in RECTS:
                            na = a1 - a0
                            grid = lambda x: x.rearrange("p h (a b) -> p h a b", b=nb)
                            first = lambda x: x[:, :, 0, a0:a1].unsqueeze(3).broadcast_to([P, PH, na, nb])
                            second = lambda x: x[:, :, 1, 0:nb].unsqueeze(2).broadcast_to([P, PH, na, nb])
                            step.mark(nc.vector.tensor_tensor(grid(cand[:, :, at:at + na * nb]), first(top), second(top), ALU.add))
                            at += na * nb
                        step.wait()
                        at = 0
                        for a0, a1, nb in RECTS:
                            na = a1 - a0
                            grid = lambda x: x.rearrange("p h (a b) -> p h a b", b=nb)
                            step.mark(nc.vector.tensor_copy(grid(ci[:, 0, :, at:at + na * nb]), tf[:, :, 0, a0:a1].unsqueeze(3).broadcast_to([P, PH, na, nb])))
                            step.mark(nc.vector.tensor_copy(grid(ci[:, 1, :, at:at + na * nb]), tf[:, :, 1, 0:nb].unsqueeze(2).broadcast_to([P, PH, na, nb])))
                            at += na * nb
                        settle()
                        heads = range(PH)
                        best16([cand[:, h, :] for h in heads], [cand2[:, h, :] for h in heads],
                               [best[:, h, :] for h in heads], [pos[:, h, :] for h in heads])
                        dve.wait_ge(exped, n + 1)
                        ins = nc.vector.tensor_tensor(ex[:, :, :], best[:, :, :], best[:, :, 0:1].broadcast_to([P, PH, PTOP]), ALU.subtract)
                        ins.then_inc(shifted, 1)
                        step(nc.vector.tensor_copy(posf[:, :, :], pos[:, :, :]))
                        step(nc.vector.tensor_tensor(eq[:, :, :, :].rearrange("p h k c -> p (h k) c"),
                                                     iota[:, :].unsqueeze(1).broadcast_to([P, PH * PTOP, CAND]),
                                                     posf[:, :, :].rearrange("p h k -> p (h k)").unsqueeze(2).broadcast_to([P, PH * PTOP, CAND]),
                                                     ALU.is_equal))
                        for side, dst in ((0, I1), (1, I2)):
                            step(nc.vector.tensor_tensor(mul[:, :, :, :], eq[:, :, :, :],
                                                         ci[:, side, :, :].unsqueeze(2).broadcast_to([P, PH, PTOP, CAND]), ALU.mult))
                            step(nc.vector.tensor_reduce(dst[:, bass.ds(t, 1), :].rearrange("p o k -> p (o k)"),
                                                         mul[:, :, :, :].rearrange("p h k c -> p (h k) c"), AX.X, ALU.add))
                        dve.wait_ge(exped, n + 2)
                        step(nc.vector.tensor_reduce(sm[:, :, 0], ex[:, :, :], AX.X, ALU.add))
                        step(nc.vector.reciprocal(sm[:, :, 1], sm[:, :, 0]))
                        step(nc.vector.tensor_tensor(GW[:, bass.ds(t, 1), :].rearrange("p o (h k) -> p (o h) k", h=PH), ex[:, :, :],
                                                     sm[:, :, 1:2].broadcast_to([P, PH, PTOP]), ALU.mult))
                    assert step.n == TOPK_STEPS, step.n


TOPK_STEPS = 5 * 2 * PH + 5 * PH + 1 + 4 + 8 + 1 + 1 + 4 + 3 + 10


F16 = mybir.dt.float16


def peer_gates(nc, io, ident, I1, I2, GW, gates, layer, first_tile):
    tiles = list(range(first_tile, TILES))
    B = 8
    with ExitStack() as c:
        sb = lambda n, s, d=F32: c.enter_context(nc.sbuf_tensor(f"gt_{n}{layer}", s, d))
        stage = [sb(f"stage{j}", [P, P, P]) for j in range(2)]
        cols = [sb(f"cols{j}", [P, 4, P]) for j in range(2)]
        cur = [sb(f"cur{j}", [P, 4, B]) for j in range(2)]
        hot = [sb(f"hot{j}", [P, B, 3, P], F16) for j in range(2)]
        high = sb("high", [P, P], F16)
        iota32 = sb("iota32", [P, P])
        iota = sb("iota", [P, P], F16)
        T = c.enter_context(nc.psum_tensor(f"gt_T{layer}", [P, 3, P], F32))
        G = [c.enter_context(nc.psum_tensor(f"gt_G{j}{layer}", [P, B, P], F32)) for j in range(2)]
        GRP = P // B
        with signals(nc, "iota_in", "turned", "cols_done", "hot_done", "prod", "read", "stored0", "stored1", "own") as (
                iota_in, turned, cols_done, hot_done, prod, read, stored0, stored1, own):
            stored = (stored0, stored1)
            with nc.Block() as block:
                @block.sync
                def _(sp):
                    sp.dma_start(iota32[:, :], io["iota"]).then_inc(iota_in, 16)
                    for n, t in enumerate(tiles):
                        sp.wait_ge(read, GRP * (n + 1) + 2)
                        sp.dma_start(gates.rearrange("a b t -> b a t")[:, :, t * P:t * P + P], stage[n % 2][:, :, :]).then_inc(stored[n % 2], 16)
                    for j in range(2):
                        sp.wait_ge(stored[j], 8 * len(tiles))

                @block.tensor
                def _(pe):
                    for n, t in enumerate(tiles):
                        if n:
                            pe.wait_ge(cols_done, 2 * n)
                        for x, src in enumerate((I1, I2, GW)):
                            last = nc.tensor.transpose(T[:, x, :], src[:, t, :], ident[:, :])
                        last.then_inc(turned, 1)
                        with pe.Fori(0, GRP // 2) as it:
                            for j in range(2):
                                pe.wait_ge(hot_done, it * 2 + (GRP * n + j + 3))
                                pe.wait_ge(read, it * 2 + (GRP * n + j + 1))
                                for x in range(B):
                                    for part in (1, 2):
                                        last = nc.tensor.matmul(G[j][:, x, :], hot[j][:, x, part, :], hot[j][:, x, 0, :],
                                                                start=(part == 1), stop=(part == 2))
                                last.then_inc(prod, 1)

                @block.scalar
                def _(act):
                    act.sem_inc(read, 2)
                    for n, t in enumerate(tiles):
                        if n >= 2:
                            act.wait_ge(stored[n % 2], 16 * (n // 2))
                        with act.Fori(0, GRP // 2) as it:
                            for j in range(2):
                                act.wait_ge(prod, it * 2 + (GRP * n + j + 3))
                                nc.scalar.activation(stage[n % 2][:, :, bass.ds(it * 2 * B + j * B, B)],
                                                     G[j][:, :, :].rearrange("p x i -> p i x"), ACT.Copy).then_inc(read, 1)

                @block.gpsimd
                def _(pool):
                    pool.sem_inc(prod, 2)
                    pool.sem_inc(hot_done, 2)

                @block.vector
                def _(dve):
                    step = InOrder(dve, own)
                    dve.wait_ge(iota_in, 16)
                    step(nc.vector.tensor_copy(iota[:, :], iota32[:, :]))
                    chain = 1
                    for n, t in enumerate(tiles):
                        dve.wait_ge(turned, n + 1)
                        col = cols[n % 2]
                        step.base, step.n = chain, 0
                        nc.vector.tensor_copy(col[:, 0:3, :], T[:, :, :]).then_inc(cols_done, 1)
                        dve.wait_ge(cols_done, 2 * n + 1)
                        step(nc.vector.tensor_copy(high[:, :], col[:, 2, :]))
                        nc.vector.tensor_tensor(col[:, 3, :], col[:, 2, :], high[:, :], ALU.subtract).then_inc(cols_done, 1)
                        dve.wait_ge(cols_done, 2 * n + 2)
                        chain += 1
                        with dve.Fori(0, GRP // 2) as it:
                            step.base, step.n = it * 2 + chain, 0
                            for j in range(2):
                                dve.wait_ge(prod, it * 2 + (GRP * n + j + 1))
                                step(nc.vector.tensor_copy(cur[j][:, :, :], col[:, :, bass.ds(it * 2 * B + j * B, B)]))
                                for x in range(B):
                                    nc.vector.tensor_scalar(hot[j][:, x, 0, :], iota[:, :], cur[j][:, 0, x:x + 1], None, ALU.is_equal)
                                    nc.vector.tensor_scalar(hot[j][:, x, 1, :], iota[:, :], cur[j][:, 1, x:x + 1], cur[j][:, 2, x:x + 1],
                                                            ALU.is_equal, ALU.mult)
                                    last = nc.vector.tensor_scalar(hot[j][:, x, 2, :], iota[:, :], cur[j][:, 1, x:x + 1], cur[j][:, 3, x:x + 1],
                                                                   ALU.is_equal, ALU.mult)
                                last.then_inc(hot_done, 1)
                        chain += GRP


def peer_experts(nc, io, XT, gates, ACC, layer, first_tile):
    c0 = first_tile * P
    NT = TOK - c0
    spans = [(a, min(512, NT - a)) for a in range(0, NT, 512)]
    GC = 4
    NG = PCH // GC
    pieces = [(t, h) for t in range(first_tile, TILES) for h in range(2)]
    NP = len(pieces)
    with ExitStack() as c:
        sb = lambda n, s, d=F32: c.enter_context(nc.sbuf_tensor(f"ex_{n}{layer}", s, d))
        hh, hl = (sb(n, [P, KD, NT], F16) for n in ("hh", "hl"))
        ur = [sb(f"ur{b}", [P, KD, P]) for b in range(4)]
        vr = [sb(f"vr{b}", [P, D]) for b in range(4)]
        gr = [sb(f"gr{b}", [P, NT]) for b in range(4)]
        uh = [sb(f"uh{b}", [P, KD, P], F16) for b in range(2)]
        ul = [sb(f"ul{b}", [P, KD, P], F16) for b in range(2)]
        vh = [sb(f"vh{b}", [P, GC, D], F16) for b in range(2)]
        vl = [sb(f"vl{b}", [P, GC, D], F16) for b in range(2)]
        wh = [sb(f"wh{b}", [P, GC, NT], F16) for b in range(2)]
        wl = [sb(f"wl{b}", [P, GC, NT], F16) for b in range(2)]
        ga = [sb(f"ga{b}", [P, NT]) for b in range(2)]
        zero = sb("zero", [P, KD])
        A = [c.enter_context(nc.psum_tensor(f"ex_A{b}{layer}", [P, 1024], F32)) for b in range(2)]
        R = [c.enter_context(nc.psum_tensor(f"ex_R{b}{layer}", [P, 512], F32)) for b in range(4)]
        names = ["h_cut", "first_done", "second_done", "u_cut", "v_cut", "gelu_done", "w_cut", "added", "own", "pown"]
        names += [f"{x}_in{b}" for x in "uvg" for b in range(4)]
        with signals(nc, *names) as sems:
            h_cut, first_done, second_done, u_cut, v_cut, gelu_done, w_cut, added, own, pown = sems[:10]
            u_in, v_in, g_in = sems[10:14], sems[14:18], sems[18:22]
            u_src, v_src = io["peer_u"][layer], io["peer_v"][layer]
            with nc.Block() as block:
                @block.sync
                def _(sp):
                    with sp.Fori(0, NG // 2) as it:
                        for x in range(2 * GC):
                            s, b = it * (2 * GC) + x, x % 4
                            sp.wait_ge(u_cut, s + 1)
                            sp.dma_start(ur[b][:, :, :], u_src[bass.ds(s, 1)].rearrange("o p (k n) -> p (o k) n", k=KD)).then_inc(u_in[b], 16)
                            sp.wait_ge(w_cut, s + 1)
                            sp.dma_start(gr[b][:, :], gates[bass.ds(s, 1), :, c0:TOK].rearrange("o p t -> p (o t)")).then_inc(g_in[b], 16)
                            sp.wait_ge(v_cut, s + 1)
                            sp.dma_start(vr[b][:, :], v_src[bass.ds(s, 1)].rearrange("o p d -> p (o d)")).then_inc(v_in[b], 16)

                @block.gpsimd
                def _(pool):
                    step = InOrder(pool, pown)
                    step(nc.gpsimd.memset(zero[:, :], 0.0))
                    zero_kn = zero[:, :].unsqueeze(2).broadcast_to([P, KD, P])
                    zero_d = zero[:, 0:1].broadcast_to([P, D])
                    pool.sem_inc(u_cut, 4)
                    pool.sem_inc(v_cut, 4)
                    with pool.Fori(0, NG // 2) as it:
                        step.base, step.n = it * (4 * GC) + 1, 0
                        for x in range(2 * GC):
                            s, b, q = it * (2 * GC) + x, x % 4, x // GC
                            pool.wait_ge(u_in[b], it * 32 + (16 * q + 16))
                            pool.wait_ge(first_done, s + 1)
                            step(nc.gpsimd.tensor_tensor(uh[x % 2][:, :, :], ur[b][:, :, :], zero_kn, ALU.add))
                            nc.gpsimd.tensor_tensor(ul[x % 2][:, :, :], ur[b][:, :, :], uh[x % 2][:, :, :], ALU.subtract).then_inc(u_cut, 1)
                            pool.wait_ge(v_in[b], it * 32 + (16 * q + 16))
                            pool.wait_ge(second_done, it * (2 * NP) + NP * (q + 1))
                            step(nc.gpsimd.tensor_tensor(vh[q][:, x % GC, :], vr[b][:, :], zero_d, ALU.add))
                            nc.gpsimd.tensor_tensor(vl[q][:, x % GC, :], vr[b][:, :], vh[q][:, x % GC, :], ALU.subtract).then_inc(v_cut, 1)

                @block.tensor
                def _(pe):
                    def first(g, q):
                        for x in range(GC):
                            s, b = g * GC + x, x % 2
                            pe.wait_ge(u_cut, s + 5)
                            pe.wait_ge(gelu_done, s + 1)
                            for k in range(KD):
                                for n, (lhs, rhs) in enumerate(((uh, hh), (uh, hl), (ul, hh))):
                                    for a, m in spans:
                                        last = nc.tensor.matmul(A[b][:, a:a + m], lhs[b][:, k, :], rhs[:, k, a:a + m],
                                                                start=(k == 0 and n == 0), stop=(k == KD - 1 and n == 2))
                            last.then_inc(first_done, 1)

                    def second(g, q):
                        pe.wait_ge(v_cut, g * GC + (GC + 4))
                        pe.wait_ge(w_cut, g * GC + (GC + 4))
                        for y, (t, h) in enumerate(pieces):
                            pe.wait_ge(added, g * NP + (y + 1))
                            o = (t - first_tile) * P
                            for x in range(GC):
                                for n, (lhs, rhs) in enumerate(((wh, vh), (wh, vl), (wl, vh))):
                                    last = nc.tensor.matmul(R[y % 4][:, :], lhs[q][:, x, o:o + P], rhs[q][:, x, h * 512:h * 512 + 512],
                                                            start=(x == 0 and n == 0), stop=(x == GC - 1 and n == 2))
                            last.then_inc(second_done, 1)

                    pe.sem_inc(first_done, 2)
                    pe.sem_inc(second_done, 2 * NP)
                    pe.wait_ge(h_cut, 1)
                    first(0, 0)
                    with pe.Fori(0, NG // 2 - 1) as it:
                        first(it * 2 + 1, 1)
                        second(it * 2, 0)
                        first(it * 2 + 2, 0)
                        second(it * 2 + 1, 1)
                    first(NG - 1, 1)
                    second(NG - 2, 0)
                    second(NG - 1, 1)

                @block.scalar
                def _(act):
                    act.sem_inc(gelu_done, 2)
                    with act.Fori(0, NG // 2) as it:
                        for x in range(2 * GC):
                            s, b = it * (2 * GC) + x, x % 2
                            act.wait_ge(first_done, s + 3)
                            act.wait_ge(w_cut, s + 3)
                            nc.scalar.activation(ga[b][:, :], A[b][:, 0:NT], ACT.Gelu).then_inc(gelu_done, 1)

                @block.vector
                def _(dve):
                    step = InOrder(dve, own)

                    def weights(g, q):
                        dve.wait_ge(second_done, g * NP + NP)
                        for x in range(GC):
                            s, b = g * GC + x, x % 2
                            dve.wait_ge(gelu_done, s + 3)
                            dve.wait_ge(g_in[x], g * 16 + 16)
                            step.base, step.n = g * (2 * GC) + 2 * x + 1, 0
                            step(nc.vector.tensor_tensor(ga[b][:, :], ga[b][:, :], gr[x][:, :], ALU.mult))
                            step(nc.vector.tensor_copy(wh[q][:, x, :], ga[b][:, :]))
                            nc.vector.tensor_tensor(wl[q][:, x, :], ga[b][:, :], wh[q][:, x, :], ALU.subtract).then_inc(w_cut, 1)

                    def add(g):
                        dve.wait_ge(added, g * NP + 4)
                        for y, (t, h) in enumerate(pieces):
                            dve.wait_ge(second_done, g * NP + (2 * NP + y + 1))
                            part = ACC[:, t, h * 512:h * 512 + 512]
                            nc.vector.tensor_tensor(part, part, R[y % 4][:, :], ALU.add).then_inc(added, 1)

                    dve.sem_inc(w_cut, 4)
                    step(nc.vector.tensor_copy(hh[:, :, :], XT[:, :, c0:TOK]))
                    nc.vector.tensor_tensor(hl[:, :, :], XT[:, :, c0:TOK], hh[:, :, :], ALU.subtract).then_inc(h_cut, 1)
                    dve.wait_ge(h_cut, 1)
                    nc.vector.memset(ACC, 0.0).then_inc(added, 4)
                    weights(0, 0)
                    with dve.Fori(0, NG // 2 - 1) as it:
                        weights(it * 2 + 1, 1)
                        add(it * 2)
                        weights(it * 2 + 2, 0)
                        add(it * 2 + 1)
                    weights(NG - 1, 1)
                    add(NG - 2)
                    add(NG - 1)


def decay_rates(nc, io, rates):
    with ExitStack() as c:
        sb = lambda n: c.enter_context(nc.sbuf_tensor(f"dr_{n}", [P, RG_N, 2], F32))
        lam, x, s, u, p = (sb(n) for n in ("lam", "x", "s", "u", "p"))
        with signals(nc, "lam_in", "exped", "own", "aown") as (lam_in, exped, own, aown):
            with nc.Block() as block:
                @block.sync
                def _(sp):
                    sp.dma_start(lam[:, :, :], io["od_lambda"]).then_inc(lam_in, 16)

                @block.scalar
                def _(act):
                    step = InOrder(act, aown)
                    act.wait_ge(lam_in, 16)
                    step(nc.scalar.activation(x[:, :, :], lam[:, :, :], ACT.Abs))
                    nc.scalar.activation(x[:, :, :], x[:, :, :], ACT.Exp, scale=-1.0).then_inc(exped, 1)

                @block.vector
                def _(dve):
                    step = InOrder(dve, own)
                    v = lambda t: t[:, :, :]
                    dve.wait_ge(exped, 1)
                    step(nc.vector.tensor_scalar(v(s), v(x), 2.0, None, ALU.add))
                    step(nc.vector.reciprocal(v(s), v(s)))
                    step(nc.vector.tensor_tensor(v(s), v(s), v(x), ALU.mult))
                    step(nc.vector.tensor_tensor(v(u), v(s), v(s), ALU.mult))
                    step(nc.vector.tensor_scalar(v(p), v(u), 1.0 / 17, None, ALU.mult))
                    for n in (15, 13, 11, 9, 7, 5, 3):
                        step(nc.vector.scalar_tensor_tensor(v(p), v(p), 1.0 / n, v(u), ALU.add, ALU.mult))
                    step(nc.vector.scalar_tensor_tensor(v(p), v(p), 1.0, v(s), ALU.add, ALU.mult))
                    step(nc.vector.tensor_scalar(v(s), v(lam), -1.0, 0.0, ALU.mult, ALU.max))
                    step(nc.vector.scalar_tensor_tensor(v(p), v(p), 2.0, v(s), ALU.mult, ALU.add))
                    pair = rates[:, :, :].rearrange("p n (d s) -> p n d s", d=2)
                    nc.vector.tensor_scalar(pair[:, :, :, 0], v(p), -RG_C, None, ALU.mult)
                    nc.vector.tensor_scalar(pair[:, :, :, 1], v(p), RG_C, None, ALU.mult)


def rglru(nc, io, XT, MIX, rates):
    ZC, ZX = RG_LEFT, RG_LEFT + CTX + (RG_CONV - 1 - RG_LEFT) + RG_LEFT
    ZN = ZX + SEQ + (RG_CONV - 1 - RG_LEFT)
    with ExitStack() as c:
        sb = lambda n, s: c.enter_context(nc.sbuf_tensor(f"rg_{n}", s, F32))
        wp = [sb(f"wp{j}", [P, 2, KD, P]) for j in range(2)]
        wg = [sb(f"wg{j}", [P, 4, P]) for j in range(2)]
        cn = [sb(f"cn{j}", [P, 9]) for j in range(2)]
        rate = [sb(f"rate{j}", [P, 4]) for j in range(2)]
        gb = [sb(f"gb{j}", [P, SEQ]) for j in range(2)]
        z = [sb(f"z{j}", [P, ZN]) for j in range(2)]
        cv = [sb(f"cv{j}", [P, TOK]) for j in range(2)]
        r, i, a, t, h = ([sb(f"{n}{d}", [P, TOK]) for d in range(2)] for n in "riath")
        a2 = sb("a2", [P, TOK])
        ps = lambda n, s: c.enter_context(nc.psum_tensor(f"rg_{n}", s, F32))
        B = ps("B", [P, 512])
        Z = ps("Z", [P, 1024])
        G = [ps(f"G{g}", [P, 1024]) for g in range(2)]
        with signals(nc, "wp_in0", "wp_in1", "wg_in0", "wg_in1", "proj", "copied", "conv", "gate", "sig", "decayed",
                     "squared", "rooted", "y_done", "own", "aown") as (
                wp_in0, wp_in1, wg_in0, wg_in1, proj, copied, conv, gate, sig, decayed, squared, rooted, y_done, own, aown):
            wp_in, wg_in = (wp_in0, wp_in1), (wg_in0, wg_in1)

            def loop(eng, near, far):
                near(0, 0)
                with eng.Fori(0, RG_N // 2 - 1) as it:
                    near(it, 1)
                    far(it, 0)
                    near(it + 1, 0)
                    far(it, 1)
                near(RG_N // 2 - 1, 1)
                far(RG_N // 2 - 1, 0)
                far(RG_N // 2 - 1, 1)

            with nc.Block() as block:
                @block.sync
                def _(sp):
                    def load(n, j, projections, gates):
                        at = lambda name: io[name][bass.ds(n, 1)]
                        if projections:
                            sp.dma_start(wp[j][:, :, :, :], at("od_w_in").rearrange("o p (b k m) -> p (o b) k m", b=2, k=KD)).then_inc(wp_in[j], 16)
                        if gates:
                            sp.dma_start(wg[j][:, :, :], at("od_gate_w").rearrange("o p (g m) -> p (o g) m", g=4)).then_inc(wg_in[j], 16)
                            sp.dma_start(cn[j][:, :], at("od_consts").rearrange("o p m -> p (o m)")).then_inc(wg_in[j], 16)
                    for j in range(2):
                        load(j, j, True, True)
                    with sp.Fori(1, RG_N // 2) as it:
                        for j in range(2):
                            sp.wait_ge(proj, it * 2 + (j - 1))
                            load(it * 2 + j, j, True, False)
                            sp.wait_ge(y_done, it * 2 + j)
                            load(it * 2 + j, j, False, True)

                @block.tensor
                def _(pe):
                    def near(m, j):
                        pe.wait_ge(wp_in[j], m * 16 + 16)
                        pe.wait_ge(copied, m * 4 + (2 * j + 2))
                        for k in range(KD):
                            nc.tensor.matmul(B[:, :], wp[j][:, 0, k, :], XT[:, k, CTX:TOK], start=(k == 0), stop=(k == KD - 1))
                        for s, n in HALVES:
                            for k in range(KD):
                                last = nc.tensor.matmul(Z[:, s:s + n], wp[j][:, 1, k, :], XT[:, k, s:s + n],
                                                        start=(k == 0), stop=(k == KD - 1))
                        last.then_inc(proj, 1)

                    def far(m, j):
                        pe.wait_ge(wg_in[j], m * 32 + 32)
                        pe.wait_ge(conv, m * 2 + (j + 1))
                        for d in range(2):
                            pe.wait_ge(sig, m * 8 + (4 * j + 2 * d + 1))
                            for g in range(2):
                                for s, n in HALVES:
                                    last = nc.tensor.matmul(G[g][:, s:s + n], wg[j][:, 2 * d + g, :], cv[j][:, s:s + n],
                                                            start=True, stop=True)
                            last.then_inc(gate, 1)

                    loop(pe, near, far)

                @block.scalar
                def _(act):
                    step = InOrder(act, aown)

                    def near(m, j):
                        act.wait_ge(proj, m * 2 + (j + 1))
                        step.mark(nc.scalar.activation(z[j][:, ZC:ZC + CTX], Z[:, 0:CTX], ACT.Copy))
                        nc.scalar.activation(z[j][:, ZX:ZX + SEQ], Z[:, CTX:TOK], ACT.Copy).then_inc(copied, 1)
                        if not (isinstance(m, int) and (m, j) == (0, 0)):
                            act.wait_ge(y_done, m * 2 + j)
                        nc.scalar.activation(gb[j][:, :], B[:, :], ACT.Gelu).then_inc(copied, 1)

                    def far(m, j):
                        act.wait_ge(wg_in[j], m * 32 + 32)
                        act.wait_ge(y_done, m * 2 + (j + 1))
                        for d in range(2):
                            act.wait_ge(gate, m * 4 + (2 * j + d + 1))
                            nc.scalar.activation(r[d][:, :], G[0][:, 0:TOK], ACT.Sigmoid, bias=cn[j][:, 5 + 2 * d:6 + 2 * d]).then_inc(sig, 1)
                            nc.scalar.activation(i[d][:, :], G[1][:, 0:TOK], ACT.Sigmoid, bias=cn[j][:, 6 + 2 * d:7 + 2 * d]).then_inc(sig, 1)
                        act.wait_ge(sig, m * 8 + (4 * j + 5))
                        for d in range(2):
                            nc.scalar.activation(a[d][:, :], r[d][:, :], ACT.Exp, scale=rate[j][:, 2 * d:2 * d + 1]).then_inc(decayed, 1)
                            nc.scalar.activation(t[d][:, :], r[d][:, :], ACT.Tanh, scale=rate[j][:, 2 * d + 1:2 * d + 2]).then_inc(decayed, 1)
                        for d in range(2):
                            act.wait_ge(squared, m * 4 + (2 * j + d + 1))
                            nc.scalar.activation(t[d][:, :], t[d][:, :], ACT.Sqrt).then_inc(rooted, 1)

                    act.sem_inc(copied, 2)
                    act.sem_inc(sig, 1)
                    act.wait_ge(y_done, 1)
                    loop(act, near, far)

                @block.vector
                def _(dve):
                    step = InOrder(dve, own)
                    NEAR, FAR = 8, 11
                    before = 3

                    def near(m, j):
                        step.base, step.n = m * (2 * (NEAR + FAR)) + (before + j * (NEAR + FAR) - FAR), 0
                        if isinstance(m, int) and (m, j) == (0, 0):
                            step.base = before
                        dve.wait_ge(wg_in[j], m * 32 + 32)
                        dve.wait_ge(copied, m * 4 + (2 * j + 4))
                        step.mark(nc.vector.tensor_copy(rate[j][:, :], rates[:, bass.ds(m * 2 + j, 1), :].rearrange("p o s -> p (o s)")))
                        segs = ((0, ZC, CTX), (CTX, ZX, SEQ))
                        for o, s, n in segs:
                            s -= RG_LEFT
                            step.mark(nc.vector.tensor_scalar(cv[j][:, o:o + n], z[j][:, s:s + n], cn[j][:, 0:1], cn[j][:, 4:5],
                                                              ALU.mult, ALU.add))
                        for tap in range(1, RG_CONV):
                            step.wait()
                            for o, s, n in segs:
                                s += tap - RG_LEFT
                                ins = nc.vector.scalar_tensor_tensor(cv[j][:, o:o + n], z[j][:, s:s + n], cn[j][:, tap:tap + 1],
                                                                     cv[j][:, o:o + n], ALU.mult, ALU.add)
                                if tap < RG_CONV - 1 or o == 0:
                                    step.mark(ins)
                        ins.then_inc(conv, 1)
                        assert step.n == NEAR, step.n

                    def far(m, j):
                        step.base, step.n = m * (2 * (NEAR + FAR)) + (before + j * (NEAR + FAR) + 2 * NEAR), 0
                        if isinstance(m, int) and j == 1:
                            step.base -= NEAR
                        dve.wait_ge(conv, m * 2 + (j + 1))
                        for d in range(2):
                            dve.wait_ge(sig, m * 8 + (4 * j + 2 * d + 3))
                            step.mark(nc.vector.tensor_tensor(i[d][:, :], i[d][:, :], cv[j][:, :], ALU.mult))
                        for d in range(2):
                            dve.wait_ge(decayed, m * 8 + (4 * j + 2 * d + 2))
                            step(nc.vector.tensor_tensor(a2[:, :], a[d][:, :], a[d][:, :], ALU.mult))
                            nc.vector.scalar_tensor_tensor(t[d][:, :], a2[:, :], 1.0, t[d][:, :], ALU.add, ALU.mult).then_inc(squared, 1)
                            dve.wait_ge(squared, m * 4 + (2 * j + d + 1))
                        for d in range(2):
                            dve.wait_ge(rooted, m * 4 + (2 * j + d + 1))
                            step(nc.vector.tensor_tensor(i[d][:, :], i[d][:, :], t[d][:, :], ALU.mult))
                            if d == 0:
                                step.mark(nc.vector.tensor_tensor_scan(h[0][:, :], a[0][:, :], i[0][:, :], 0.0, ALU.mult, ALU.add))
                            else:
                                back = lambda x, s, e: x[:, s:e][:, ::-1]
                                step(nc.vector.tensor_tensor_scan(back(h[1], 0, CTX), back(a[1], 0, CTX), back(i[1], 0, CTX), 0.0,
                                                                  ALU.mult, ALU.add))
                                step(nc.vector.tensor_tensor_scan(back(h[1], CTX, TOK), back(a[1], CTX, TOK), back(i[1], CTX, TOK),
                                                                  h[1][:, 0:1], ALU.mult, ALU.add))
                        step(nc.vector.tensor_tensor(h[0][:, CTX:TOK], h[0][:, CTX:TOK], h[1][:, CTX:TOK], ALU.add))
                        step(nc.vector.tensor_tensor(MIX[:, bass.ds(m * 2 + j, 1), :].rearrange("p o t -> p (o t)"), h[0][:, CTX:TOK],
                                                     gb[j][:, :], ALU.mult))
                        assert step.n == FAR, step.n
                        dve.sem_inc(y_done, 1)

                    step.mark(nc.vector.memset(z[0][:, :], 0.0))
                    step.mark(nc.vector.memset(z[1][:, :], 0.0))
                    step(nc.vector.memset(a2[:, :], 0.0))
                    dve.sem_inc(y_done, 1)
                    loop(dve, near, far)


def peer(nc, io, mods, gates, H, ident, layer, first_tile):
    with nc.sbuf_tensor(f"XTp{layer}", [P, KD, TOK], F32) as XT:
        modulate_columns(nc, mods, H, XT, ident, layer, 3, first_tile, f"mp{layer}")
        with ExitStack() as c:
            I1, I2, GW = (c.enter_context(nc.sbuf_tensor(f"pe_{n}{layer}", [P, TILES, PH * PTOP], F32)) for n in ("I1", "I2", "GW"))
            with nc.sbuf_tensor(f"SCO{layer}", [P, TILES, 2 * PH, P], F32) as SCO:
                peer_scores(nc, io, XT, SCO, layer, first_tile)
                peer_topk(nc, io, SCO, I1, I2, GW, layer, first_tile)
            peer_gates(nc, io, ident, I1, I2, GW, gates, layer, first_tile)
        ACC = XT[:, :, :].rearrange("p k t -> p (k t)").rearrange("p (t d) -> p t d", d=D)
        peer_experts(nc, io, XT, gates, ACC, layer, first_tile)
        project_and_norm(nc, io, mods, H, ACC, None, list(range(first_tile, TILES)), layer, 1, f"n{layer}p")


def build(nc, io, out):
    with ExitStack() as c:
        sb = lambda n, s: c.enter_context(nc.sbuf_tensor(n, s, F32))
        H = sb("H", [P, TILES, D])
        ident = sb("ident", [P, P])
        ones = sb("ones", [P, P])
        mods = nc.dram_tensor("mods", [2, 2 * N_MOD * D], F32, kind="Internal").ap()
        gates = nc.dram_tensor("gates", [P, P, TOK], F32, kind="Internal").ap()
        with signals(nc, "first_in") as (first_in,):
            with nc.Block() as block:
                @block.sync
                def _(sp):
                    sp.dma_start(H[:, 0:CTX_TILES, :], io["ctx"].rearrange("(t p) d -> p t d", p=P)).then_inc(first_in, 16)
                    sp.dma_start(H[:, CTX_TILES:TILES, :], io["x"].rearrange("(t p) d -> p t d", p=P)).then_inc(first_in, 16)
                    sp.dma_start(ident[:, :], io["ident"]).then_inc(first_in, 16)
                    sp.wait_ge(first_in, 48)
        modulation_vectors(nc, io, mods, ones)
        with ExitStack() as c1:
            PT = c1.enter_context(nc.sbuf_tensor("PT", [P, N_PROJ, TOK], F32))
            V = c1.enter_context(nc.sbuf_tensor("V", [P, TILES, GH * GDV], F32))
            MIX = c1.enter_context(nc.sbuf_tensor("MIX", [P, KD, TOK], F32))
            with nc.sbuf_tensor("XTm", [P, KD, TOK], F32) as XT:
                modulate_columns(nc, mods, H, XT, ident, 0, 0, 0, "m0")
                project_l0(nc, io, XT, PT, V)
            latent_norms(nc, io, PT, ones)
            attention(nc, io, PT, MIX, ident)
            gla(nc, io, PT, V, MIX, ident, ones)
            project_and_norm(nc, io, mods, H, MIX, "ev_w_out", list(range(TILES)), 0, 0, "n0")
        peer(nc, io, mods, gates, H, ident, 0, 0)
        with nc.sbuf_tensor("MIX1", [P, RG_N, SEQ], F32) as MIX:
            with nc.sbuf_tensor("XTr", [P, KD, TOK], F32) as XT, nc.sbuf_tensor("rates", [P, RG_N, 4], F32) as rates:
                modulate_columns(nc, mods, H, XT, ident, 1, 0, 0, "m1")
                decay_rates(nc, io, rates)
                rglru(nc, io, XT, MIX, rates)
            project_and_norm(nc, io, mods, H, MIX, "od_w_out", list(range(CTX_TILES, TILES)), 1, 0, "n1")
        peer(nc, io, mods, gates, H, ident, 1, CTX_TILES)
        with signals(nc, "stored") as (so,):
            with nc.Block() as block:
                @block.sync
                def _(sp):
                    sp.dma_start(out.rearrange("(t p) d -> p t d", p=P), H[:, CTX_TILES:, :]).then_inc(so, 16)
                    sp.wait_ge(so, 16)


def more_inputs(give, a, k_major, swap):
    n_freq = ROPE // 4
    inv = np.power(np.float32(10000.0), -np.arange(n_freq, dtype=np.float32) / np.float32(n_freq)).astype(np.float32)
    row = np.repeat(np.arange(SEQ // 64, dtype=np.float32), 64)
    col = np.tile(np.arange(64, dtype=np.float32), SEQ // 64)
    ang = np.concatenate([row[:, None] * inv, col[:, None] * inv], axis=-1).astype(np.float32)
    cos, sin = np.cos(ang).T, np.sin(ang).T
    rope = np.zeros((64, TOK), np.float32)
    rope[0:32, :CTX] = 1.0
    rope[0:32, CTX:] = np.concatenate([cos, cos])
    rope[32:64, CTX:] = np.concatenate([-sin, sin])
    give("rope", rope)
    give("latent_gain", np.concatenate([a["ev_q_norm"][0], a["ev_kv_norm"][0]]).reshape(5, P).T)
    uq = a["ev_w_uq"][0].reshape(3, P, HEADS, NOPE + ROPE)
    uq = np.concatenate([uq, swap(uq[..., NOPE:])], axis=-1)
    ukv = a["ev_w_ukv"][0].reshape(2, P, HEADS, NOPE + V_DIM)
    up = np.concatenate([uq, ukv], axis=0).transpose(2, 1, 0, 3)
    give("ev_w_up", up.reshape(HEADS, P, 5 * P))
    give("gla_wa2", a["ev_gla_wa2"][0])
    give("gla_ba", a["ev_gla_ba"][0].reshape(2, 2, P).transpose(2, 1, 0))
    give("gla_gain", a["ev_gla_norm"][0].reshape(GH, GDV).T)
    j, i = np.arange(P)[:, None], np.arange(P)[None, :]
    same = j // CHUNK == i // CHUNK
    give("gla_keep", np.stack([same & (j <= i), same & (j >= i)], axis=1).astype(np.int32))
    give("ev_w_out", k_major(a["ev_w_out"][0]))
    wq = a["peer_wq"].reshape(DEPTH, KD, P, 2 * PH, P)
    give("peer_wq", wq.transpose(0, 3, 2, 1, 4).reshape(DEPTH, 2 * PH, P, KD * P))
    give("peer_keys", np.stack([a["peer_k1"], a["peer_k2"]], axis=1).transpose(0, 3, 1, 2))
    give("iota", np.broadcast_to(np.arange(P, dtype=np.float32), (P, P)))
    u = a["peer_u"].reshape(DEPTH, PCH, P, KD, P)
    give("peer_u", u.transpose(0, 1, 4, 3, 2).reshape(DEPTH, PCH, P, KD * P))
    give("peer_v", a["peer_v"].reshape(DEPTH, PCH, P, D))
    w = a["od_w_in"][0].reshape(KD, P, 2, RG_N, P)
    give("od_w_in", w.transpose(3, 1, 2, 0, 4).reshape(RG_N, P, 2 * KD * P))
    give("od_gate_w", a["od_gate_w"][0].transpose(2, 3, 0, 1, 4).reshape(RG_N, P, 4 * P))
    consts = np.concatenate([a["od_conv_w"][0], a["od_conv_b"], a["od_gate_b"][0].reshape(4, RG_W)])
    give("od_consts", consts.reshape(9, RG_N, P).transpose(1, 2, 0))
    give("od_lambda", a["od_lambda"][0].reshape(2, RG_N, P).transpose(2, 1, 0))
    give("od_w_out", k_major(a["od_w_out"][0]))


def kernel(**inputs):
    import concourse.bacc as bacc
    from concourse.bass_utils import run_bass_kernel_spmd as run

    a = {k: np.asarray(v) for k, v in inputs.items()}
    nc = bacc.Bacc("TRN2", target_bir_lowering=False, num_devices=1)
    arrays, io = {}, {}

    def give(name, x):
        x = np.ascontiguousarray(x)
        arrays["in_" + name] = x
        io[name] = nc.dram_tensor("in_" + name, x.shape, mybir.dt.from_np(x.dtype), kind="ExternalInput").ap()

    def k_major(w):
        return w.reshape(w.shape[0] // P, P, w.shape[1]).transpose(1, 0, 2)

    give("x", a["x"][0])
    give("ctx", a["ctx"][0])
    give("ident", np.eye(P, dtype=np.float32))
    give("cond", np.stack([a["c"][0], a["c_ctx"]], axis=1).reshape(KD, P, 2).transpose(1, 0, 2))
    give("mod_w", a["mod_w"].reshape(2, KD, P, N_MOD, 1024).transpose(0, 3, 2, 1, 4).reshape(2 * N_MOD, P, KD * 1024))
    give("mod_b", a["mod_b"].reshape(-1))
    give("ln_g", a["ln_g"].reshape(4, D))
    give("ln_b", a["ln_b"].reshape(4, D))

    w = a["ev_w_in"][0]
    b = np.cumsum([0, Q_RANK, KV_RANK, ROPE, GH * GDK, GH * GDK, GH * GDV, GH * GDV, GRANK, GRANK])
    cq, ckv, pe, gq, gk, gv, gg, gaf, gab = [w[:, b[i]:b[i + 1]] for i in range(9)]
    pad = np.zeros((D, 16), np.float32)
    swap = lambda m: np.concatenate([m[..., ROPE // 2:], m[..., :ROPE // 2]], axis=-1)
    ext = np.concatenate([cq, ckv, gq, gk, gg, gaf, pad, gab, pad, pe, swap(pe)], axis=1)
    give("ev_w_in", ext.reshape(KD, P, N_PROJ, P).transpose(2, 1, 0, 3).reshape(N_PROJ, P, KD * P))
    give("ev_w_v", k_major(gv))
    more_inputs(give, a, k_major, swap)

    out = nc.dram_tensor("out_0", (SEQ, D), F32, kind="ExternalOutput").ap()
    build(nc, io, out)
    r = run(nc, [arrays], core_ids=[0])
    return r.results[0]["out_0"].reshape(1, SEQ, D)
```

```python
from contextlib import ExitStack, contextmanager
from itertools import count

import numpy as np
import concourse.bass as bass
from concourse import mybir

F32 = mybir.dt.float32
F16 = mybir.dt.float16
I32 = mybir.dt.int32
U32 = mybir.dt.uint32
ALU = mybir.AluOpType
ACT = mybir.ActivationFunctionType
AX = mybir.AxisListType

P = 128
D = 1024
KD = D // P
SEQ, CTX = 512, 256
TOK = CTX + SEQ
TILES = TOK // P
CTX_TILES = CTX // P
N_MOD = 6
DEPTH = 2
ALPHA = (2 * DEPTH) ** 0.25
EPS = 1e-6
HALVES = ((0, 512), (512, 256))

HEADS, Q_RANK, KV_RANK, NOPE, ROPE, V_DIM = 8, 384, 256, 64, 32, 64
MLA_SCALE = (NOPE + ROPE) ** -0.5
GH, GDK, GDV, GRANK, TAU, CHUNK = 4, 64, 128, 16, 16.0, 64
CHUNKS = TOK // CHUNK
CTX_CHUNKS = CTX // CHUNK
C_Q, C_KV, C_GQ, C_GK, C_GG, C_MISC, N_PROJ = 0, 3, 5, 7, 9, 13, 14
GAF, GAB, KPE, KPE_SWAPPED = 0, 32, 64, 96

RG_W, RG_N, RG_CONV, RG_LEFT, RG_C = 1280, 10, 4, 2, 8.0
PH, PK, PTOP = 8, 128, 16
PCH = 128


STAGE = count()


@contextmanager
def signals(nc, *names):
    stage = next(STAGE)
    sems = [nc.alloc_semaphore(f"{n}_{stage}") for n in names]
    yield sems
    nc.clear_and_free_semaphores(sems)
    nc.all_engine_barrier()


class InOrder:

    def __init__(self, eng, sem):
        self.eng, self.sem, self.n, self.base = eng, sem, 0, 0

    def start(self, i, per):
        self.base, self.n = i * per, 0

    def mark(self, ins):
        self.n += 1
        ins.then_inc(self.sem, 1)

    def wait(self):
        self.eng.wait_ge(self.sem, self.base + self.n)

    def __call__(self, ins):
        self.mark(ins)
        self.wait()


def row_to_all(ap_row, n):
    return ap_row.rearrange("(o n) -> o n", o=1).broadcast_to([P, n])


def modulation_vectors(nc, io, mods, ones, H, ident):
    LOADS = 2 * N_MOD
    with ExitStack() as c:
        sb = lambda n, s: c.enter_context(nc.sbuf_tensor(n, s, F32))
        cond = sb("cond", [P, KD, 2])
        w = [sb(f"mod_w{j}", [P, KD, 1024]) for j in range(3)]
        rows = sb("mod_rows", [2, LOADS * 1024])
        pm = [c.enter_context(nc.psum_tensor(f"mod_ps{j}", [P, 1024], F32)) for j in range(3)]
        with signals(nc, "cond_in", "bias_in", "silu_done", "rows_done", "stored", "rows_in",
                     *[f"w_in{j}" for j in range(3)], *[f"prod{j}" for j in range(3)],
                     *[f"added{j}" for j in range(3)]) as sems:
            cond_in, bias_in, silu_done, rows_done, stored, rows_in = sems[:6]
            w_in, prod, added = sems[6:9], sems[9:12], sems[12:15]
            with nc.Block() as block:
                @block.sync
                def _(sp):
                    sp.dma_start(cond[:, :, :], io["cond"]).then_inc(cond_in, 16)
                    for j in range(3):
                        sp.dma_start(w[j][:, :, :], io["mod_w"][j].rearrange("p (k n) -> p k n", k=KD)).then_inc(w_in[j], 16)
                    sp.dma_start(rows[:, :], io["mod_b"].rearrange("(o n) -> o n", o=1).broadcast_to([2, LOADS * 1024])).then_inc(bias_in, 16)
                    with sp.Fori(1, LOADS // 3) as it:
                        for j in range(3):
                            sp.wait_ge(prod[j], it)
                            sp.dma_start(w[j][:, :, :], io["mod_w"][bass.ds(it * 3 + j, 1)].rearrange("o p (k n) -> p (o k) n", k=KD)).then_inc(w_in[j], 16)
                    sp.wait_ge(rows_done, LOADS)
                    sp.dma_start(mods, rows[:, :]).then_inc(stored, 16)
                    sp.wait_ge(stored, 16)

                @block.scalar
                def _(act):
                    act.wait_ge(cond_in, 16)
                    nc.scalar.activation(cond[:, :, :], cond[:, :, :], ACT.Silu).then_inc(silu_done, 1)
                    act.wait_ge(w_in[1], 16)
                    act.dma_start(H[:, 0:CTX_TILES, :], io["ctx"].rearrange("(t p) d -> p t d", p=P)).then_inc(rows_in, 16)
                    act.dma_start(H[:, CTX_TILES:TILES, :], io["x"].rearrange("(t p) d -> p t d", p=P)).then_inc(rows_in, 16)
                    act.dma_start(ident[:, :], io["ident"]).then_inc(rows_in, 16)
                    act.wait_ge(rows_in, 48)

                @block.tensor
                def _(pe):
                    pe.wait_ge(silu_done, 1)
                    with pe.Fori(0, LOADS // 3) as it:
                        for j in range(3):
                            pe.wait_ge(w_in[j], it * 16 + 16)
                            pe.wait_ge(added[j], it + 1)
                            for h in range(2):
                                for k in range(KD):
                                    last = nc.tensor.matmul(pm[j][0:2, h * 512:h * 512 + 512], cond[:, k, :],
                                                            w[j][:, k, h * 512:h * 512 + 512],
                                                            start=(k == 0), stop=(k == KD - 1))
                            last.then_inc(prod[j], 1)

                @block.vector
                def _(dve):
                    for j in range(3):
                        nc.vector.memset(ones[0:1, j:j + 1], 1.0).then_inc(added[j], 1)
                    dve.wait_ge(bias_in, 16)
                    with dve.Fori(0, LOADS // 3) as it:
                        for j in range(3):
                            dve.wait_ge(prod[j], it + 1)
                            piece = rows[:, bass.ds(it * 3072 + j * 1024, 1024)]
                            nc.vector.tensor_tensor(piece, piece, pm[j][0:2, :], ALU.add).then_inc(added[j], 1)
                    for j in range(3):
                        dve.wait_ge(added[j], LOADS // 3 + 1)
                    nc.vector.memset(ones[:, :], 1.0).then_inc(rows_done, LOADS)


def modulate_columns(nc, mods, H, hh, hl, ident, layer, shift, first_tile, tag):
    o_sh, o_sc = (layer * N_MOD + shift) * D, (layer * N_MOD + shift + 1) * D
    tiles = list(range(first_tile, TILES))
    with ExitStack() as c:
        vec = c.enter_context(nc.sbuf_tensor(f"{tag}_vec", [P, 4, D], F32))
        tmp = [c.enter_context(nc.sbuf_tensor(f"{tag}_tmp{j}", [P, D], F32)) for j in range(2)]
        pt = [c.enter_context(nc.psum_tensor(f"{tag}_pt{j}", [P, KD, P], F32)) for j in range(2)]
        with signals(nc, "vec_in", "scaled", "modulated", "turned", "high_done", "low_done") as (
                vec_in, scaled, modulated, turned, high_done, low_done):
            with nc.Block() as block:
                @block.sync
                def _(sp):
                    for v in range(2):
                        sp.dma_start(vec[:, 2 * v, :], row_to_all(mods[v, o_sh:o_sh + D], D)).then_inc(vec_in, 16)
                        sp.dma_start(vec[:, 2 * v + 1, :], row_to_all(mods[v, o_sc:o_sc + D], D)).then_inc(vec_in, 16)

                @block.vector
                def _(dve):
                    def low(i):
                        dve.wait_ge(high_done, i + 1)
                        nc.vector.tensor_tensor(hl[:, :, i * P:i * P + P], pt[i % 2][:, :, :], hh[:, :, i * P:i * P + P],
                                                ALU.subtract).then_inc(low_done, 1)

                    dve.wait_ge(vec_in, 64)
                    for i, t in enumerate(tiles):
                        v = 1 if t < CTX_TILES else 0
                        if i >= 2:
                            dve.wait_ge(turned, i - 1)
                        nc.vector.scalar_tensor_tensor(tmp[i % 2][:, :], vec[:, 2 * v + 1, :], 1.0, H[:, t, :],
                                                       ALU.add, ALU.mult).then_inc(scaled, 1)
                        dve.wait_ge(scaled, i + 1)
                        nc.vector.tensor_tensor(tmp[i % 2][:, :], tmp[i % 2][:, :], vec[:, 2 * v, :],
                                                ALU.add).then_inc(modulated, 1)
                        if i >= 1:
                            low(i - 1)
                    low(len(tiles) - 1)

                @block.tensor
                def _(pe):
                    for i, t in enumerate(tiles):
                        pe.wait_ge(modulated, i + 1)
                        if i >= 2:
                            pe.wait_ge(low_done, i - 1)
                        for k in range(KD):
                            last = nc.tensor.transpose(pt[i % 2][:, k, :], tmp[i % 2][:, k * P:k * P + P], ident[:, :])
                        last.then_inc(turned, 1)

                @block.scalar
                def _(act):
                    for i, t in enumerate(tiles):
                        act.wait_ge(turned, i + 1)
                        nc.scalar.activation(hh[:, :, i * P:i * P + P], pt[i % 2][:, :, :], ACT.Copy).then_inc(high_done, 1)


def three_products(high, low, by_high, by_low):
    return (high, by_high), (high, by_low), (low, by_high)


def project_l0(nc, io, hh, hl, PT, V):
    with ExitStack() as c:
        sb = lambda n, s, d=F32: c.enter_context(nc.sbuf_tensor(n, s, d))
        w = [sb(f"pw{j}", [P, KD, P]) for j in range(2)]
        wh = [sb(f"pwh{j}", [P, KD, P], F16) for j in range(2)]
        wl = [sb(f"pwl{j}", [P, KD, P], F16) for j in range(2)]
        wv = sb("pwv", [P, KD, GH * GDV])
        vh = sb("pvh", [P, KD, GH * GDV], F16)
        vl = sb("pvl", [P, KD, GH * GDV], F16)
        zero = sb("pzero", [P, KD])
        ps = [c.enter_context(nc.psum_tensor(f"pps{j}", [P, 1024], F32)) for j in range(2)]
        pv = [c.enter_context(nc.psum_tensor(f"ppv{j}", [P, 512], F32)) for j in range(2)]
        with signals(nc, "wv_in", "wv_high", "wv_cut", "v_prod", "v_copied", "w_in0", "w_in1", "w_cut", "prod", "copied",
                     "pown") as (wv_in, wv_high, wv_cut, v_prod, v_copied, w_in0, w_in1, w_cut, prod, copied, pown):
            w_in = (w_in0, w_in1)
            with nc.Block() as block:
                @block.sync
                def _(sp):
                    with sp.Fori(0, N_PROJ // 2) as it:
                        for j in range(2):
                            sp.wait_ge(w_cut, it * 2 + (j + 1))
                            sp.dma_start(w[j][:, :, :], io["ev_w_in"][bass.ds(it * 2 + j, 1)].rearrange("o p (k m) -> p (o k) m", k=KD)).then_inc(w_in[j], 16)

                @block.gpsimd
                def _(pool):
                    step = InOrder(pool, pown)
                    step(nc.gpsimd.memset(zero[:, :], 0.0))
                    zeros = zero[:, :].unsqueeze(2).broadcast_to([P, KD, P])
                    pool.sem_inc(w_cut, 2)
                    with pool.Fori(0, N_PROJ // 2) as it:
                        step.base, step.n = it * 2 + 1, 0
                        for j in range(2):
                            pool.wait_ge(w_in[j], it * 16 + 16)
                            pool.wait_ge(prod, it * 2 + (j + 1))
                            step(nc.gpsimd.tensor_tensor(wh[j][:, :, :], w[j][:, :, :], zeros, ALU.add))
                            nc.gpsimd.tensor_tensor(wl[j][:, :, :], w[j][:, :, :], wh[j][:, :, :], ALU.subtract).then_inc(w_cut, 1)

                @block.tensor
                def _(pe):
                    pe.sem_inc(prod, 2)
                    with pe.Fori(0, N_PROJ // 2) as it:
                        for j in range(2):
                            pe.wait_ge(w_cut, it * 2 + (j + 3))
                            pe.wait_ge(copied, it * 2 + (j + 1))
                            for a, n in HALVES:
                                for k in range(KD):
                                    for x, (lhs, rhs) in enumerate(three_products(wh, wl, hh, hl)):
                                        last = nc.tensor.matmul(ps[j][:, a:a + n], lhs[j][:, k, :], rhs[:, k, a:a + n],
                                                                start=(k == 0 and x == 0), stop=(k == KD - 1 and x == 2))
                            last.then_inc(prod, 1)
                    pe.wait_ge(wv_cut, 1)
                    for t in range(TILES):
                        if t >= 2:
                            pe.wait_ge(v_copied, t - 1)
                        for k in range(KD):
                            for x, (lhs, rhs) in enumerate(three_products(hh, hl, vh, vl)):
                                last = nc.tensor.matmul(pv[t % 2][:, :], lhs[:, k, t * P:t * P + P], rhs[:, k, :],
                                                        start=(k == 0 and x == 0), stop=(k == KD - 1 and x == 2))
                        last.then_inc(v_prod, 1)

                @block.scalar
                def _(act):
                    act.sem_inc(copied, 2)
                    act.dma_start(wv[:, :, :], io["ev_w_v"]).then_inc(wv_in, 16)
                    with act.Fori(0, N_PROJ // 2) as it:
                        for j in range(2):
                            act.wait_ge(prod, it * 2 + (j + 3))
                            nc.scalar.activation(PT[:, bass.ds(it * 2 + j, 1), :].rearrange("p o t -> p (o t)"),
                                                 ps[j][:, 0:TOK], ACT.Copy).then_inc(copied, 1)

                @block.vector
                def _(dve):
                    dve.wait_ge(wv_in, 16)
                    nc.vector.tensor_copy(vh[:, :, :], wv[:, :, :]).then_inc(wv_high, 1)
                    dve.wait_ge(wv_high, 1)
                    nc.vector.tensor_tensor(vl[:, :, :], wv[:, :, :], vh[:, :, :], ALU.subtract).then_inc(wv_cut, 1)
                    for t in range(TILES):
                        dve.wait_ge(v_prod, t + 1)
                        nc.vector.tensor_copy(V[:, t, :], pv[t % 2][:, :]).then_inc(v_copied, 1)


def latent_norms(nc, io, PT, ones):
    with ExitStack() as c:
        sb = lambda n, s: c.enter_context(nc.sbuf_tensor(n, s, F32))
        sq = sb("ln_sq", [P, 5, TOK])
        g = sb("ln_gain", [P, 5])
        eps = sb("ln_eps", [P, 1])
        r = sb("ln_r", [P, 2, TOK])
        cs = sb("ln_cs", [P, TOK])
        tmp = sb("ln_tmp", [P, TOK])
        ss = [c.enter_context(nc.psum_tensor(f"ln_ss{j}", [P, 1024], F32)) for j in range(2)]
        with signals(nc, "ln_in", "squared", "summed", "rooted", "own", "eps_set") as (
                ln_in, squared, summed, rooted, own, eps_set):
            with nc.Block() as block:
                @block.sync
                def _(sp):
                    sp.dma_start(g[:, :], io["latent_gain"]).then_inc(ln_in, 16)
                    sp.dma_start(cs[64:128, :], io["rope"]).then_inc(ln_in, 16)

                @block.tensor
                def _(pe):
                    pe.wait_ge(squared, 1)
                    for j, (k0, k1) in enumerate(((0, 3), (3, 5))):
                        for a, n in HALVES:
                            for k in range(k0, k1):
                                last = nc.tensor.matmul(ss[j][:, a:a + n], ones[:, :], sq[:, k, a:a + n],
                                                        start=(k == k0), stop=(k == k1 - 1))
                        last.then_inc(summed, 1)

                @block.scalar
                def _(act):
                    act.wait_ge(eps_set, 1)
                    for j, rank in enumerate((Q_RANK, KV_RANK)):
                        act.wait_ge(summed, j + 1)
                        nc.scalar.activation(r[:, j, :], ss[j][:, 0:TOK], ACT.Sqrt, scale=1.0 / rank,
                                             bias=eps[:, :]).then_inc(rooted, 1)

                @block.vector
                def _(dve):
                    step = InOrder(dve, own)
                    nc.vector.memset(eps[:, :], EPS).then_inc(eps_set, 1)
                    nc.vector.tensor_tensor(sq[:, :, :], PT[:, 0:5, :], PT[:, 0:5, :], ALU.mult).then_inc(squared, 1)
                    dve.wait_ge(ln_in, 32)
                    pe_rows = PT[KPE:KPE + ROPE, C_MISC, :]
                    step.mark(nc.vector.tensor_tensor(tmp[64:96, :], PT[96:128, C_MISC, :], cs[96:128, :], ALU.mult))
                    step(nc.vector.tensor_tensor(pe_rows, pe_rows, cs[64:96, :], ALU.mult))
                    step(nc.vector.tensor_tensor(pe_rows, pe_rows, tmp[64:96, :], ALU.add))
                    for j, (k0, k1) in enumerate(((0, 3), (3, 5))):
                        dve.wait_ge(rooted, j + 1)
                        step(nc.vector.reciprocal(r[:, j, :], r[:, j, :]))
                        for k in range(k0, k1):
                            nc.vector.scalar_tensor_tensor(PT[:, k, :], PT[:, k, :], g[:, k:k + 1], r[:, j, :],
                                                           ALU.mult, ALU.mult)


def attention(nc, io, PT, MIX, ident):
    PAIRS = HEADS // 2
    with ExitStack() as c:
        sb = lambda n, s: c.enter_context(nc.sbuf_tensor(n, s, F32))
        cs = sb("at_cs", [P, TOK])
        w = [sb(f"at_w{j}", [P, 5, P]) for j in range(2)]
        q = [sb(f"at_q{j}", [96, TOK]) for j in range(2)]
        k = [sb(f"at_k{j}", [96, TOK]) for j in range(2)]
        v = [sb(f"at_v{j}", [P, TILES, V_DIM]) for j in range(2)]
        rot = sb("at_rot", [P, 2, TOK])
        prob = [sb(f"at_p{j}", [P, TOK]) for j in range(2)]
        probT = [sb(f"at_pT{j}", [P, TOK]) for j in range(2)]
        small = sb("at_small", [P, 2, 4])
        ps = lambda n, s: c.enter_context(nc.psum_tensor(n, s, F32))
        A = [ps(f"at_A{j}", [P, 1024]) for j in range(2)]
        T = ps("at_T", [P, 1024])
        C = ps("at_C", [P, TILES, V_DIM])
        O0 = ps("at_O", [P, P])
        O = (O0[0:64, :], C[0:64, 0:2, :].rearrange("p a d -> p (a d)"))
        names = ("cs_in", "w_in0", "w_in1", "proj_done", "qkv_copied", "roped", "score", "maxed", "exped",
                 "normed", "turned", "pt_copied", "av_done", "out_copied", "own")
        with signals(nc, *names) as (cs_in, w_in0, w_in1, proj_done, qkv_copied, roped, score, maxed, exped,
                                     normed, turned, pt_copied, av_done, out_copied, own):
            w_in = (w_in0, w_in1)
            keys = lambda i: CTX if i < CTX_TILES else TOK
            with nc.Block() as block:
                @block.sync
                def _(sp):
                    sp.dma_start(cs[64:128, :], io["rope"]).then_inc(cs_in, 16)
                    for j in range(2):
                        sp.dma_start(w[j][:, :, :], io["ev_w_up"][j].rearrange("p (k m) -> p k m", k=5)).then_inc(w_in[j], 16)
                    with sp.Fori(1, PAIRS) as it:
                        for j in range(2):
                            sp.wait_ge(proj_done, it * 2 + (j - 1))
                            sp.dma_start(w[j][:, :, :], io["ev_w_up"][bass.ds(it * 2 + j, 1)].rearrange("o p (k m) -> p (o k) m", k=5)).then_inc(w_in[j], 16)

                @block.tensor
                def _(pe):
                    def scores(h6, j, i):
                        if i >= 2:
                            pe.wait_ge(exped, h6 + i)
                        n = keys(i)
                        for a in range(0, n, 512):
                            b = min(n, a + 512)
                            last = nc.tensor.matmul(A[i % 2][:, a:b], q[j][:, i * P:i * P + P], k[j][:, a:b],
                                                    start=True, stop=True)
                        last.then_inc(score, 1)

                    with pe.Fori(0, PAIRS) as it:
                        for j in range(2):
                            h6 = it * 12 + 6 * j
                            pe.wait_ge(w_in[j], it * 16 + 16)
                            pe.wait_ge(exped, h6 + 1)
                            pe.wait_ge(qkv_copied, it * 6 + (3 * j + 1))
                            pe.wait_ge(out_copied, h6 + 2)
                            for a, n in HALVES:
                                for kk in range(3):
                                    nc.tensor.matmul(A[0][:, a:a + n], w[j][:, kk, :], PT[:, kk, a:a + n],
                                                     start=(kk == 0), stop=(kk == 2))
                            for a, n in HALVES:
                                for kk in range(2):
                                    nc.tensor.matmul(A[1][0:64, a:a + n], w[j][:, 3 + kk, 0:64], PT[:, C_KV + kk, a:a + n],
                                                     start=(kk == 0), stop=(kk == 1))
                            for t in range(TILES):
                                for kk in range(2):
                                    last = nc.tensor.matmul(C[:, t, :], PT[:, C_KV + kk, t * P:t * P + P],
                                                            w[j][:, 3 + kk, 64:128], start=(kk == 0), stop=(kk == 1))
                            last.then_inc(proj_done, 1)
                            pe.wait_ge(qkv_copied, it * 6 + (3 * j + 4))
                            pe.wait_ge(roped, it * 2 + (j + 1))
                            scores(h6, j, 0)
                            scores(h6, j, 1)
                            for i in range(TILES):
                                n = keys(i)
                                pe.wait_ge(normed, h6 + (i + 1))
                                pe.wait_ge(pt_copied, h6 + (i + 1))
                                for b in range(n // P):
                                    last = nc.tensor.transpose(T[:, b * P:b * P + P], prob[i % 2][:, b * P:b * P + P], ident[:, :])
                                last.then_inc(turned, 1)
                                if i + 2 < TILES:
                                    scores(h6, j, i + 2)
                                pe.wait_ge(pt_copied, h6 + (i + 2))
                                pe.wait_ge(out_copied, h6 + (i + 1))
                                for b in range(n // P):
                                    last = nc.tensor.matmul(O[i % 2], v[j][:, b, :], probT[i % 2][:, b * P:b * P + P],
                                                            start=(b == 0), stop=(b == n // P - 1))
                                last.then_inc(av_done, 1)

                @block.scalar
                def _(act):
                    act.wait_ge(cs_in, 16)
                    act.sem_inc(exped, 1)
                    act.sem_inc(qkv_copied, 1)
                    act.sem_inc(pt_copied, 1)
                    with act.Fori(0, PAIRS) as it:
                        for j in range(2):
                            h6 = it * 12 + 6 * j
                            act.wait_ge(proj_done, it * 2 + (j + 1))
                            nc.scalar.activation(q[j][0:64, :], A[0][0:64, 0:TOK], ACT.Copy).then_inc(qkv_copied, 1)
                            nc.scalar.activation(k[j][0:64, :], A[1][0:64, 0:TOK], ACT.Copy).then_inc(qkv_copied, 1)
                            nc.scalar.activation(v[j][:, :, :], C[:, :, :], ACT.Copy).then_inc(qkv_copied, 1)
                            for i in range(TILES + 1):
                                if i < TILES:
                                    n = keys(i)
                                    act.wait_ge(maxed, h6 + (i + 1))
                                    act.wait_ge(turned, h6 + (i + 1))
                                    nc.scalar.activation(prob[i % 2][:, 0:n], A[i % 2][:, 0:n], ACT.Exp, scale=MLA_SCALE,
                                                         bias=small[:, i % 2, 1:2], accum_out=small[:, i % 2, 2:3]).then_inc(exped, 1)
                                if i >= 1:
                                    n = keys(i - 1)
                                    act.wait_ge(turned, h6 + (i + 2))
                                    act.wait_ge(av_done, h6 + i)
                                    nc.scalar.activation(probT[(i - 1) % 2][:, 0:n], T[:, 0:n], ACT.Copy).then_inc(pt_copied, 1)

                @block.gpsimd
                def _(pool):
                    pool.sem_inc(turned, 2)
                    pool.sem_inc(av_done, 2)
                    pool.sem_inc(out_copied, 2)

                @block.vector
                def _(dve):
                    step = InOrder(dve, own)
                    dve.wait_ge(cs_in, 16)
                    for j in range(2):
                        nc.vector.tensor_copy(k[j][64:96, :], PT[KPE:KPE + ROPE, C_MISC, :])
                    with dve.Fori(0, PAIRS) as it:
                        step.start(it, 28)
                        for j in range(2):
                            h6 = it * 12 + 6 * j
                            dve.wait_ge(proj_done, it * 2 + (j + 1))
                            step.mark(nc.vector.tensor_tensor(rot[64:96, 0, :], A[0][96:128, 0:TOK], cs[96:128, :], ALU.mult))
                            step(nc.vector.tensor_tensor(rot[64:96, 1, :], A[0][64:96, 0:TOK], cs[64:96, :], ALU.mult))
                            nc.vector.tensor_tensor(q[j][64:96, :], rot[64:96, 0, :], rot[64:96, 1, :], ALU.add).then_inc(roped, 1)
                            for i in range(TILES + 2):
                                if i < TILES:
                                    n = keys(i)
                                    dve.wait_ge(score, h6 + (i + 1))
                                    step(nc.vector.tensor_reduce(small[:, i % 2, 0:1], A[i % 2][:, 0:n], AX.X, ALU.max, negate=True))
                                    nc.vector.tensor_scalar(small[:, i % 2, 1:2], small[:, i % 2, 0:1], MLA_SCALE, None,
                                                            ALU.mult).then_inc(maxed, 1)
                                if 1 <= i <= TILES:
                                    e = i - 1
                                    n = keys(e)
                                    dve.wait_ge(exped, h6 + (e + 2))
                                    step(nc.vector.reciprocal(small[:, e % 2, 3:4], small[:, e % 2, 2:3]))
                                    nc.vector.tensor_scalar(prob[e % 2][:, 0:n], prob[e % 2][:, 0:n], small[:, e % 2, 3:4], None,
                                                            ALU.mult).then_inc(normed, 1)
                                if i >= 2:
                                    o = i - 2
                                    dve.wait_ge(av_done, h6 + (o + 3))
                                    nc.vector.tensor_copy(MIX[64 * j:64 * j + 64, bass.ds(it, 1), o * P:o * P + P].rearrange("p o t -> p (o t)"),
                                                          O[o % 2]).then_inc(out_copied, 1)
                        assert step.n == 28, step.n


VISITS = (list(range(CHUNKS)),
          list(range(CTX_CHUNKS - 1, -1, -1)) + list(range(CHUNKS - 1, CTX_CHUNKS - 1, -1)))
MID = (CHUNK // 2 - 1, CHUNK // 2)
LAST = (CHUNK - 1, 0)


def by_chunk(a):
    return a.rearrange("p (c i) -> p c i", i=CHUNK)


def gla_decays(nc, io, PT, p, g):
    LIM = 80.0 * TAU
    with ExitStack() as c:
        sb = lambda n, s: c.enter_context(nc.sbuf_tensor(f"{n}{p}", s, F32))
        wa = sb("g_wa", [64, GH * GDK])
        ba = sb("g_ba", [P, 2, 2])
        reset = sb("g_reset", [P, 2, TOK])
        z = sb("g_z", [P, 2, TOK])
        az = g["kw"]
        cum = sb("g_cum", [P, 2, TOK])
        ex = sb("g_ex", [P, 2, TOK])
        Z = [c.enter_context(nc.psum_tensor(f"g_Z{d}{p}", [P, 1024], F32)) for d in range(2)]
        with signals(nc, "loaded", "reset_set", "z_prod", "z_read", "logs", "mid_diff", "cum_done", "total_diff", "exp_done",
                     "ex_used", "own", "aown") as (
                loaded, reset_set, z_prod, z_read, logs, mid_diff, cum_done, total_diff, exp_done, ex_used, own, aown):
            with nc.Block() as block:
                @block.sync
                def _(sp):
                    sp.dma_start(wa[0:GRANK, :], io["gla_wa2"][0]).then_inc(loaded, 16)
                    sp.dma_start(wa[32:32 + GRANK, :], io["gla_wa2"][1]).then_inc(loaded, 16)
                    sp.dma_start(ba[:, :, :], io["gla_ba"]).then_inc(loaded, 16)

                @block.gpsimd
                def _(pool):
                    nc.gpsimd.memset(reset[:, :, :], 1.0).then_inc(reset_set, 1)
                    pool.wait_ge(reset_set, 1)
                    nc.gpsimd.memset(by_chunk(reset[:, 0, :])[:, :, 0:1], 0.0).then_inc(reset_set, 1)
                    nc.gpsimd.memset(by_chunk(reset[:, 1, :])[:, :, CHUNK - 1:CHUNK], 0.0).then_inc(reset_set, 1)

                @block.tensor
                def _(pe):
                    pe.wait_ge(loaded, 48)
                    for d in range(2):
                        for a, m in HALVES:
                            last = nc.tensor.matmul(Z[d][:, a:a + m], wa[32 * d:32 * d + GRANK, p * P:p * P + P],
                                                    PT[32 * d:32 * d + GRANK, C_MISC, a:a + m], start=True, stop=True)
                        last.then_inc(z_prod, 1)

                @block.scalar
                def _(act):
                    step = InOrder(act, aown)
                    for d in range(2):
                        act.wait_ge(z_prod, d + 1)
                        nc.scalar.activation(z[:, d, :], Z[d][:, 0:TOK], ACT.Identity, bias=ba[:, p, d:d + 1]).then_inc(z_read, 1)
                    act.wait_ge(z_read, 2)
                    step(nc.scalar.activation(az[:, :, :], z[:, :, :], ACT.Abs))
                    step(nc.scalar.activation(az[:, :, :], az[:, :, :], ACT.Exp, scale=-1.0))
                    nc.scalar.activation(az[:, :, :], az[:, :, :], ACT.Ln, bias=1.0).then_inc(logs, 1)
                    act.wait_ge(mid_diff, 1)
                    nc.scalar.activation(ex[:, :, :], z[:, :, :], ACT.Exp, scale=1.0 / TAU).then_inc(exp_done, 1)
                    act.wait_ge(ex_used, 2)
                    nc.scalar.activation(ex[:, :, :], z[:, :, :], ACT.Exp, scale=-1.0 / TAU).then_inc(exp_done, 1)
                    act.wait_ge(ex_used, 3)
                    nc.scalar.activation(ex[:, :, :], cum[:, :, :], ACT.Exp, scale=1.0 / TAU).then_inc(exp_done, 1)
                    act.wait_ge(ex_used, 5)
                    act.wait_ge(total_diff, 1)
                    nc.scalar.activation(ex[:, :, :], az[:, :, :], ACT.Exp, scale=1.0 / TAU).then_inc(exp_done, 1)
                    for d in range(2):
                        nc.scalar.activation(g["dec"][:, d, :], by_chunk(cum[:, d, :])[:, :, LAST[d]], ACT.Exp, scale=1.0 / TAU)

                @block.vector
                def _(dve):
                    step = InOrder(dve, own)
                    dve.wait_ge(reset_set, 3)
                    dve.wait_ge(logs, 1)
                    step(nc.vector.scalar_tensor_tensor(z[:, :, :], z[:, :, :], 0.0, az[:, :, :], ALU.min, ALU.subtract))
                    step.mark(nc.vector.tensor_tensor_scan(cum[:, 0, :], reset[:, 0, :], z[:, 0, :], 0.0, ALU.mult, ALU.add))
                    step(nc.vector.tensor_tensor_scan(cum[:, 1, ::-1], reset[:, 1, ::-1], z[:, 1, ::-1], 0.0, ALU.mult, ALU.add))
                    for d in range(2):
                        cc = by_chunk(cum[:, d, :])
                        step.mark(nc.vector.tensor_tensor(by_chunk(z[:, d, :]), cc, cc[:, :, MID[d]:MID[d] + 1].broadcast_to([P, CHUNKS, CHUNK]), ALU.subtract))
                    step.wait()
                    nc.vector.tensor_scalar(z[:, :, :], z[:, :, :], LIM, -LIM, ALU.min, ALU.max).then_inc(mid_diff, 1)
                    for d in range(2):
                        cc = by_chunk(cum[:, d, :])
                        step.mark(nc.vector.tensor_tensor(by_chunk(az[:, d, :]), cc[:, :, LAST[d]:LAST[d] + 1].broadcast_to([P, CHUNKS, CHUNK]), cc, ALU.subtract))
                    step.wait()
                    nc.vector.memset(reset[0:1, 0, 0:1], 0.0).then_inc(total_diff, 1)
                    q, k = PT[:, C_GQ + p, :], PT[:, C_GK + p, :]
                    both = lambda a: a.unsqueeze(1).broadcast_to([a.shape[0], 2, TOK])
                    dve.wait_ge(exp_done, 1)
                    for h in range(2):
                        rows = slice(64 * h, 64 * h + 64)
                        nc.vector.scalar_tensor_tensor(g["qe"][rows, :, h, :], ex[rows, :, :], GDK ** -0.5, both(q[rows, :]),
                                                       ALU.mult, ALU.mult).then_inc(ex_used, 1)
                    dve.wait_ge(exp_done, 2)
                    nc.vector.tensor_tensor(g["ke"][:, :, :], ex[:, :, :], both(k), ALU.mult).then_inc(ex_used, 1)
                    dve.wait_ge(exp_done, 3)
                    for h in range(2):
                        rows = slice(64 * h, 64 * h + 64)
                        nc.vector.scalar_tensor_tensor(g["qs"][rows, :, h, :], ex[rows, :, :], GDK ** -0.5, both(q[rows, :]),
                                                       ALU.mult, ALU.mult).then_inc(ex_used, 1)
                    dve.wait_ge(exp_done, 4)
                    nc.vector.tensor_tensor(g["kw"][:, :, :], ex[:, :, :], both(k), ALU.mult)


def gla_states(nc, V, ident, p, g):
    with ExitStack() as c:
        kwr = c.enter_context(nc.sbuf_tensor(f"g_kwr{p}", [P, 2, TILES, P], F32))
        T = c.enter_context(nc.psum_tensor(f"g_T{p}", [P, 2, 4, P], F32))
        U = [c.enter_context(nc.psum_tensor(f"g_U{j}{p}", [P, 4, GDV], F32)) for j in range(4)]
        slot = lambda ch: U[2 * (ch % 2) + (ch // 2) // 4][:, (ch // 2) % 4, :]
        kw, S, dec = g["kw"], g["S"], g["dec"]
        with signals(nc, "turned", "copied", "update_done", "state_done", "own") as (turned, copied, update_done, state_done, own):
            with nc.Block() as block:
                @block.tensor
                def _(pe):
                    for d in range(2):
                        if d:
                            pe.wait_ge(copied, 2 * d)
                        for t in range(TILES):
                            last = nc.tensor.transpose(T[:, t // 4, t % 4, :], kw[:, d, t * P:t * P + P], ident[:, :])
                        last.then_inc(turned, 1)
                        pe.wait_ge(copied, 2 * d + 2)
                        if d:
                            pe.wait_ge(state_done, d)
                        for ch in range(CHUNKS):
                            j0 = CHUNK * (ch % 2)
                            for h in range(2):
                                last = nc.tensor.matmul(slot(ch)[64 * h:64 * h + 64, :],
                                                        kwr[j0:j0 + CHUNK, d, ch // 2, 64 * h:64 * h + 64],
                                                        V[j0:j0 + CHUNK, ch // 2, (2 * p + h) * GDV:(2 * p + h + 1) * GDV],
                                                        start=True, stop=True)
                        last.then_inc(update_done, 1)

                @block.scalar
                def _(act):
                    for d in range(2):
                        act.wait_ge(turned, d + 1)
                        nc.scalar.activation(kwr[:, d, 0:4, :], T[:, 0, :, :], ACT.Copy).then_inc(copied, 1)
                        nc.scalar.activation(kwr[:, d, 4:6, :], T[:, 1, 0:2, :], ACT.Copy).then_inc(copied, 1)

                @block.vector
                def _(dve):
                    step = InOrder(dve, own)
                    for d in range(2):
                        dve.wait_ge(update_done, d + 1)
                        order = VISITS[d]
                        step(nc.vector.tensor_copy(S[:, d, order[1], :], slot(order[0])))
                        for ch, nxt in zip(order[1:], order[2:]):
                            ins = nc.vector.scalar_tensor_tensor(S[:, d, nxt, :], S[:, d, ch, :], dec[:, d, ch:ch + 1], slot(ch),
                                                                 ALU.mult, ALU.add)
                            step(ins)
                        nc.vector.memset(g["tick"][:, :], 0.0).then_inc(state_done, 1)


def gla_outputs(nc, V, MIX, keep, p, g):
    with ExitStack() as c:
        SC = [[c.enter_context(nc.psum_tensor(f"g_SC{b}{d}{p}", [P, P], F32)) for d in range(2)] for b in range(2)]
        O = [c.enter_context(nc.psum_tensor(f"g_O{b}{p}", [P, P], F32)) for b in range(2)]
        qe, ke, qs, S, sc = g["qe"], g["ke"], g["qs"], g["S"], g["sc"]
        with signals(nc, "score", "kept", "out_done", "out_copied") as (score, kept, out_done, out_copied):
            with nc.Block() as block:
                @block.tensor
                def _(pe):
                    def scores(n):
                        h, t = divmod(n, TILES)
                        if n >= 2:
                            pe.wait_ge(kept, 2 * (n - 1))
                        for d in range(2):
                            last = nc.tensor.matmul(SC[n % 2][d][:, :], ke[:, d, t * P:t * P + P], qe[:, d, h, t * P:t * P + P],
                                                    start=True, stop=True)
                        last.then_inc(score, 1)

                    scores(0)
                    for n in range(2 * TILES):
                        h, t = divmod(n, TILES)
                        v = V[:, t, (2 * p + h) * GDV:(2 * p + h + 1) * GDV]
                        if n + 1 < 2 * TILES:
                            scores(n + 1)
                        if n >= 2:
                            pe.wait_ge(out_copied, n - 1)
                        pe.wait_ge(kept, 2 * n + 2)
                        nc.tensor.matmul(O[n % 2][:, :], v, sc[:, n % 2, 0, :], start=True, stop=False)
                        for d in range(2):
                            for ch in (2 * t, 2 * t + 1):
                                if ch != VISITS[d][0]:
                                    i0 = CHUNK * (ch % 2)
                                    nc.tensor.matmul(O[n % 2][:, i0:i0 + CHUNK], S[:, d, ch, :],
                                                     qs[:, d, h, ch * CHUNK:ch * CHUNK + CHUNK], start=False, stop=False)
                        nc.tensor.matmul(O[n % 2][:, :], v, sc[:, n % 2, 1, :], start=False, stop=True).then_inc(out_done, 1)

                @block.vector
                def _(dve):
                    for n in range(2 * TILES):
                        dve.wait_ge(score, n + 1)
                        if n >= 2:
                            dve.wait_ge(out_done, n - 1)
                        for d in range(2):
                            nc.vector.copy_predicated(sc[:, n % 2, d, :], keep[:, d, :], SC[n % 2][d][:, :]).then_inc(kept, 1)

                @block.scalar
                def _(act):
                    for n in range(2 * TILES):
                        h, t = divmod(n, TILES)
                        act.wait_ge(out_done, n + 1)
                        nc.scalar.activation(MIX[:, 4 + 2 * p + h, t * P:t * P + P], O[n % 2][:, :], ACT.Copy).then_inc(out_copied, 1)


def gla_norm_gate(nc, io, PT, MIX, ones):
    with ExitStack() as c:
        sb = lambda n, s: c.enter_context(nc.sbuf_tensor(n, s, F32))
        sq = sb("gn_sq", [P, GH, TOK])
        gain = sb("gn_gain", [P, GH])
        eps = sb("gn_eps", [P, 1])
        ss = [c.enter_context(nc.psum_tensor(f"gn_ss{h}", [P, 1024], F32)) for h in range(GH)]
        with signals(nc, "loaded", "eps_set", "squared", "summed", "rooted", "gated", "own") as (
                loaded, eps_set, squared, summed, rooted, gated, own):
            with nc.Block() as block:
                @block.sync
                def _(sp):
                    sp.dma_start(gain[:, :], io["gla_gain"]).then_inc(loaded, 16)

                @block.tensor
                def _(pe):
                    for h in range(GH):
                        pe.wait_ge(squared, h + 1)
                        for a, m in HALVES:
                            last = nc.tensor.matmul(ss[h][:, a:a + m], ones[:, :], sq[:, h, a:a + m], start=True, stop=True)
                        last.then_inc(summed, 1)

                @block.scalar
                def _(act):
                    nc.scalar.activation(PT[:, C_GG:C_GG + GH, :], PT[:, C_GG:C_GG + GH, :], ACT.Silu).then_inc(gated, 1)
                    act.wait_ge(eps_set, 1)
                    for h in range(GH):
                        act.wait_ge(summed, h + 1)
                        nc.scalar.activation(sq[:, h, :], ss[h][:, 0:TOK], ACT.Sqrt, scale=1.0 / GDV, bias=eps[:, :]).then_inc(rooted, 1)

                @block.vector
                def _(dve):
                    step = InOrder(dve, own)
                    nc.vector.memset(eps[:, :], EPS).then_inc(eps_set, 1)
                    for h in range(GH):
                        nc.vector.tensor_tensor(sq[:, h, :], MIX[:, 4 + h, :], MIX[:, 4 + h, :], ALU.mult).then_inc(squared, 1)
                    dve.wait_ge(loaded, 16)
                    dve.wait_ge(gated, 1)
                    for h in range(GH):
                        dve.wait_ge(rooted, h + 1)
                        step(nc.vector.reciprocal(sq[:, h, :], sq[:, h, :]))
                        step(nc.vector.scalar_tensor_tensor(MIX[:, 4 + h, :], MIX[:, 4 + h, :], gain[:, h:h + 1], sq[:, h, :],
                                                            ALU.mult, ALU.mult))
                        nc.vector.tensor_tensor(MIX[:, 4 + h, :], MIX[:, 4 + h, :], PT[:, C_GG + h, :], ALU.mult)


def gla(nc, io, PT, V, MIX, ident, ones):
    with ExitStack() as c:
        sb = lambda n, s, d=F32: c.enter_context(nc.sbuf_tensor(n, s, d))
        g = {"qe": sb("g_qe", [P, 2, 2, TOK]),
             "qs": sb("g_qs", [P, 2, 2, TOK]),
             "ke": sb("g_ke", [P, 2, TOK]),
             "kw": sb("g_kw", [P, 2, TOK]),
             "dec": sb("g_dec", [P, 2, CHUNKS]),
             "tick": sb("g_tick", [1, 1]),
             "S": sb("g_S", [P, 2, CHUNKS, GDV]),
             "sc": sb("g_sc", [P, 2, 2, P])}
        keep = sb("g_keep", [P, 2, P], I32)
        with signals(nc, "keep_in") as (keep_in,):
            with nc.Block() as block:
                @block.sync
                def _(sp):
                    sp.dma_start(keep[:, :, :], io["gla_keep"]).then_inc(keep_in, 16)
                    sp.wait_ge(keep_in, 16)

                @block.gpsimd
                def _(pool):
                    nc.gpsimd.memset(g["qe"][:, :, :, :], 0.0)
                    nc.gpsimd.memset(g["sc"][:, :, :, :], 0.0)

                @block.vector
                def _(dve):
                    nc.vector.memset(g["qs"][:, :, :, :], 0.0)
        for p in range(GH // 2):
            gla_decays(nc, io, PT, p, g)
            gla_states(nc, V, ident, p, g)
            gla_outputs(nc, V, MIX, keep, p, g)
    gla_norm_gate(nc, io, PT, MIX, ones)


def project_and_norm(nc, io, mods, H, src, w_name, tiles, layer, which, tag, after=None, out=None):
    n = len(tiles)
    if after:
        hh, hl, ident, next_layer, shift = after
    o_gate = (layer * N_MOD + 2 + 3 * which) * D
    row = 2 * layer + which
    YB = 3
    nk = src.shape[1] if w_name else 0
    with ExitStack() as c:
        sb = lambda n, s: c.enter_context(nc.sbuf_tensor(f"{tag}_{n}", s, F32))
        vec = sb("vec", [P, 4, D])
        w = sb("w", [P, max(nk, 1), D])
        y = [sb(f"y{j}", [P, D]) for j in range(YB)]
        stats = sb("stats", [P, YB, 2, 6])
        mv = sb("mv", [P, YB, 4])
        eps = sb("eps", [P, 1])
        ps = [c.enter_context(nc.psum_tensor(f"{tag}_ps{j}", [P, D], F32)) for j in range(2)]
        if after:
            mvec = sb("mvec", [P, 4, D])
            tmp = [sb(f"tmp{j}", [P, D]) for j in range(2)]
            pt = [c.enter_context(nc.psum_tensor(f"{tag}_pt{j}", [P, KD, P], F32)) for j in range(2)]
        with signals(nc, "mvec_in", "shifting", "modulated", "turned", "high_done", "low_done", "vec_in", "prod", "read", "var_done", "rooted", "eps_set", "scaled", "normed", "own", "pown", "stored",
                     *[f"w_in{k}" for k in range(nk)]) as (
                mvec_in, shifting, modulated, turned, high_done, low_done, vec_in, prod, read, var_done, rooted, eps_set, scaled, normed, own, pown, stored, *w_in):
            with nc.Block() as block:
                @block.sync
                def _(sp):
                    if w_name:
                        for k in range(nk):
                            sp.dma_start(w[:, k, :], io[w_name][:, k, :]).then_inc(w_in[k], 16)
                    for v in range(2):
                        sp.dma_start(vec[:, v, :], row_to_all(mods[v, o_gate:o_gate + D], D)).then_inc(vec_in, 16)
                    sp.dma_start(vec[:, 2, :], row_to_all(io["ln_g"][row], D)).then_inc(vec_in, 16)
                    sp.dma_start(vec[:, 3, :], row_to_all(io["ln_b"][row], D)).then_inc(vec_in, 16)
                    if after:
                        for v in range(2):
                            for x in range(2):
                                o = (next_layer * N_MOD + shift + x) * D
                                sp.dma_start(mvec[:, 2 * v + x, :], row_to_all(mods[v, o:o + D], D)).then_inc(mvec_in, 16)
                    if out is not None:
                        rows = out.rearrange("(t p) d -> p t d", p=P)
                        for i, t in enumerate(tiles):
                            sp.wait_ge(normed, i + 1)
                            sp.dma_start(rows[:, i, :], H[:, t, :]).then_inc(stored, 16)
                        sp.wait_ge(stored, 16 * n)

                @block.tensor
                def _(pe):
                    def product(i):
                        if i >= 2:
                            pe.wait_ge(read, i - 1)
                        for k in range(nk):
                            if i == 0:
                                pe.wait_ge(w_in[k], 16)
                            for h in range(2):
                                last = nc.tensor.matmul(ps[i % 2][:, h * 512:h * 512 + 512], src[:, k, i * P:i * P + P],
                                                        w[:, k, h * 512:h * 512 + 512], start=(k == 0), stop=(k == nk - 1))
                        last.then_inc(prod, 1)

                    def turn(i):
                        pe.wait_ge(modulated, i + 1)
                        if i >= 2:
                            pe.wait_ge(low_done, i - 1)
                        for k in range(KD):
                            last = nc.tensor.transpose(pt[i % 2][:, k, :], tmp[i % 2][:, k * P:k * P + P], ident[:, :])
                        last.then_inc(turned, 1)

                    for i in range(n + 3):
                        if w_name and i < n:
                            product(i)
                        if after and i >= 3:
                            turn(i - 3)

                @block.scalar
                def _(act):
                    def high(i):
                        act.wait_ge(turned, i + 1)
                        nc.scalar.activation(hh[:, :, i * P:i * P + P], pt[i % 2][:, :, :], ACT.Copy).then_inc(high_done, 1)

                    act.wait_ge(eps_set, 1)
                    for i in range(n + 3):
                        if i < n:
                            act.wait_ge(var_done, i + 1)
                            nc.scalar.activation(mv[:, i % YB, 2:3], mv[:, i % YB, 1:2], ACT.Sqrt, bias=eps[:, :]).then_inc(rooted, 1)
                        if after and i >= 3:
                            high(i - 3)

                @block.vector
                def _(dve):
                    step = InOrder(dve, own)
                    nc.vector.memset(eps[:, :], EPS).then_inc(eps_set, 1)
                    dve.wait_ge(vec_in, 64)
                    if after:
                        dve.wait_ge(mvec_in, 64)

                    def gather(i):
                        t, yi = tiles[i], y[i % YB]
                        if i >= YB:
                            dve.wait_ge(normed, i - YB + 1)
                        if w_name:
                            dve.wait_ge(prod, i + 1)
                            f = ps[i % 2][:, :]
                        else:
                            f = src[:, t, :]
                        nc.vector.tensor_tensor(yi[:, :], f, vec[:, 1 if t < CTX_TILES else 0, :], ALU.mult).then_inc(read, 1)
                        dve.wait_ge(read, i + 1)
                        step(nc.vector.scalar_tensor_tensor(yi[:, :], H[:, t, :], ALPHA, yi[:, :], ALU.mult, ALU.add))
                        for h in range(2):
                            step.mark(nc.vector.bn_stats(stats[:, i % YB, h, :], yi[:, h * 512:h * 512 + 512]))
                        step.wait()
                        nc.vector.bn_aggr(mv[:, i % YB, 0:2], stats[:, i % YB, :, :].rearrange("p h s -> p (h s)")).then_inc(var_done, 1)

                    def scale(i):
                        dve.wait_ge(rooted, i + 1)
                        step(nc.vector.reciprocal(mv[:, i % YB, 3:4], mv[:, i % YB, 2:3]))
                        nc.vector.tensor_scalar(y[i % YB][:, :], y[i % YB][:, :], mv[:, i % YB, 0:1], mv[:, i % YB, 3:4],
                                                ALU.subtract, ALU.mult).then_inc(scaled, 1)

                    def modulate(i):
                        t = tiles[i]
                        v = 1 if t < CTX_TILES else 0
                        dve.wait_ge(normed, i + 1)
                        if i >= 2:
                            dve.wait_ge(turned, i - 1)
                        nc.vector.scalar_tensor_tensor(tmp[i % 2][:, :], mvec[:, 2 * v + 1, :], 1.0, H[:, t, :],
                                                       ALU.add, ALU.mult).then_inc(shifting, 1)
                        dve.wait_ge(shifting, i + 1)
                        nc.vector.tensor_tensor(tmp[i % 2][:, :], tmp[i % 2][:, :], mvec[:, 2 * v, :], ALU.add).then_inc(modulated, 1)

                    def low(i):
                        dve.wait_ge(high_done, i + 1)
                        nc.vector.tensor_tensor(hl[:, :, i * P:i * P + P], pt[i % 2][:, :, :], hh[:, :, i * P:i * P + P],
                                                ALU.subtract).then_inc(low_done, 1)

                    for i in range(n + 3):
                        if i < n:
                            gather(i)
                        if 1 <= i <= n:
                            scale(i - 1)
                        if after and 2 <= i <= n + 1:
                            modulate(i - 2)
                        if after and i >= 3:
                            low(i - 3)

                @block.gpsimd
                def _(pool):
                    step = InOrder(pool, pown)
                    pool.wait_ge(vec_in, 64)
                    for i, t in enumerate(tiles):
                        pool.wait_ge(scaled, i + 1)
                        step(nc.gpsimd.tensor_tensor(y[i % YB][:, :], y[i % YB][:, :], vec[:, 2, :], ALU.mult))
                        nc.gpsimd.tensor_tensor(H[:, t, :], y[i % YB][:, :], vec[:, 3, :], ALU.add).then_inc(normed, 1)

def peer_scores(nc, io, hh, hl, scores, layer, first_tile):
    N = 2 * PH
    c0 = first_tile * P
    spans = [(a, min(512, TOK - c0 - a)) for a in range(0, TOK - c0, 512)]
    nt = TILES - first_tile
    with ExitStack() as c:
        w = [c.enter_context(nc.sbuf_tensor(f"sc_w{j}{layer}", [P, KD, P], F32)) for j in range(2)]
        wh = [c.enter_context(nc.sbuf_tensor(f"sc_wh{j}{layer}", [P, KD, P], F16)) for j in range(2)]
        wl = [c.enter_context(nc.sbuf_tensor(f"sc_wl{j}{layer}", [P, KD, P], F16)) for j in range(2)]
        zero = c.enter_context(nc.sbuf_tensor(f"sc_zero{layer}", [P, KD], F32))
        keys = c.enter_context(nc.sbuf_tensor(f"sc_keys{layer}", [P, 2, P], F32))
        qT = [c.enter_context(nc.sbuf_tensor(f"sc_qT{j}{layer}", [P, TOK], F32)) for j in range(2)]
        so = [c.enter_context(nc.sbuf_tensor(f"sc_so{j}{layer}", [P, nt, P], F32)) for j in range(2)]
        Q = [c.enter_context(nc.psum_tensor(f"sc_Q{j}{layer}", [P, 1024], F32)) for j in range(2)]
        S = [c.enter_context(nc.psum_tensor(f"sc_S{j}{layer}", [P, 8, P], F32)) for j in range(2)]
        with signals(nc, "keys_in", "w_in0", "w_in1", "q_prod", "q_copied", "s_prod", "s_copied", "stored0", "stored1",
                     "w_cut", "pown") as (keys_in, w_in0, w_in1, q_prod, q_copied, s_prod, s_copied, stored0, stored1, w_cut, pown):
            w_in, stored = (w_in0, w_in1), (stored0, stored1)
            src = io["peer_wq"][layer]
            with nc.Block() as block:
                @block.sync
                def _(sp):
                    sp.dma_start(keys[:, :, :], io["peer_keys"][layer]).then_inc(keys_in, 16)
                    with sp.Fori(0, N // 2) as it:
                        for j in range(2):
                            sp.wait_ge(w_cut, it * 2 + (j + 1))
                            sp.dma_start(w[j][:, :, :], src[bass.ds(it * 2 + j, 1)].rearrange("o p (k m) -> p (o k) m", k=KD)).then_inc(w_in[j], 16)

                @block.gpsimd
                def _(pool):
                    step = InOrder(pool, pown)
                    step(nc.gpsimd.memset(zero[:, :], 0.0))
                    zeros = zero[:, :].unsqueeze(2).broadcast_to([P, KD, P])
                    pool.sem_inc(w_cut, 2)
                    with pool.Fori(0, N // 2) as it:
                        step.base, step.n = it * 2 + 1, 0
                        for j in range(2):
                            pool.wait_ge(w_in[j], it * 16 + 16)
                            pool.wait_ge(q_prod, it * 2 + (j + 1))
                            step(nc.gpsimd.tensor_tensor(wh[j][:, :, :], w[j][:, :, :], zeros, ALU.add))
                            nc.gpsimd.tensor_tensor(wl[j][:, :, :], w[j][:, :, :], wh[j][:, :, :], ALU.subtract).then_inc(w_cut, 1)

                @block.tensor
                def _(pe):
                    pe.sem_inc(q_prod, 2)
                    pe.wait_ge(keys_in, 16)
                    with pe.Fori(0, N // 2) as it:
                        for j in range(2):
                            pe.wait_ge(w_cut, it * 2 + (j + 3))
                            pe.wait_ge(q_copied, it * 2 + (j + 1))
                            for a, n in spans:
                                for k in range(KD):
                                    for x, (lhs, rhs) in enumerate(three_products(wh, wl, hh, hl)):
                                        last = nc.tensor.matmul(Q[j][:, a:a + n], lhs[j][:, k, :], rhs[:, k, a:a + n],
                                                                start=(k == 0 and x == 0), stop=(k == KD - 1 and x == 2))
                            last.then_inc(q_prod, 1)
                        for j in range(2):
                            pe.wait_ge(q_copied, it * 2 + (j + 3))
                            pe.wait_ge(s_copied, it * 2 + (j + 1))
                            for t in range(nt):
                                last = nc.tensor.matmul(S[j][:, t, :], qT[j][:, t * P:t * P + P], keys[:, j, :], start=True, stop=True)
                            last.then_inc(s_prod, 1)

                @block.scalar
                def _(act):
                    dst = scores.rearrange("t p (h k) -> p t h k", h=N)
                    act.sem_inc(q_copied, 2)
                    act.sem_inc(s_prod, 2)
                    with act.Fori(0, N // 2) as it:
                        for j in range(2):
                            act.wait_ge(q_prod, it * 2 + (j + 3))
                            act.wait_ge(s_prod, it * 2 + (j + 1))
                            nc.scalar.activation(qT[j][:, 0:nt * P], Q[j][:, 0:nt * P], ACT.Copy).then_inc(q_copied, 1)
                        for j in range(2):
                            act.wait_ge(s_copied, it * 2 + (j + 3))
                            act.dma_start(dst[:, first_tile:TILES, bass.ds(it * 2 + j, 1), :].rearrange("p t o k -> p t (o k)"),
                                          so[j][:, :, :]).then_inc(stored[j], 16)
                    for j in range(2):
                        act.wait_ge(stored[j], 16 * PH + 16)

                @block.vector
                def _(dve):
                    dve.sem_inc(s_copied, 2)
                    for j in range(2):
                        dve.sem_inc(stored[j], 16)
                    with dve.Fori(0, PH) as h:
                        for j in range(2):
                            dve.wait_ge(s_prod, h * 2 + (j + 3))
                            dve.wait_ge(stored[j], h * 16 + 16)
                            nc.vector.tensor_copy(so[j][:, :, :], S[j][:, 0:nt, :]).then_inc(s_copied, 1)


RECTS = ((0, 1, 16), (1, 4, 8), (4, 8, 4), (8, 16, 1))
CAND = sum((a1 - a0) * nb for a0, a1, nb in RECTS)


def choose_and_activate(nc, io, ident, hh, hl, scores, gates, acts, layer, first_tile):
    c0 = first_tile * P
    NT = TOK - c0
    nt = NT // P
    spans = [(a, min(512, NT - a)) for a in range(0, NT, 512)]
    B = 8
    STEPS = P // B
    TURNS = 2
    E = STEPS // TURNS
    ahead, beside = (8, 6) if nt == TILES else (12, 8)
    CT = ahead + TURNS * beside
    tail = PCH - CT * nt
    PARTS = 4
    assert tail >= 2 * PARTS and tail % 2 == ahead % 4 == beside % 2 == 0
    with ExitStack() as c:
        sb = lambda n, s, d=F32: c.enter_context(nc.sbuf_tensor(f"ca_{n}{layer}", s, d))
        ur = [sb(f"ur{b}", [P, KD, P]) for b in range(2)]
        uh = [sb(f"uh{b}", [P, KD, P], F16) for b in range(2)]
        ul = [sb(f"ul{b}", [P, KD, P], F16) for b in range(2)]
        ga = [sb(f"ga{b}", [P, NT]) for b in range(2)]
        zero = sb("zero", [P, KD])
        s = sb("s", [P, 2 * PH, P])
        s2 = sb("s2", [P, 2 * PH, P])
        top = sb("top", [P, PH, 2, PTOP])
        ti = sb("ti", [P, PH, 2, PTOP], U32)
        cand = sb("cand", [P, PH, CAND])
        cand2 = sb("cand2", [P, PH, CAND])
        ci = sb("ci", [P, 2, PH, CAND], F16)
        best = sb("best", [P, PH, PTOP])
        pos = sb("pos", [P, PH, PTOP], U32)
        posf = sb("posf", [P, PH, PTOP], F16)
        HB = 4
        eq = sb("eq", [P, HB, PTOP, CAND], F16)
        mul = sb("mul", [P, HB, PTOP, CAND], F16)
        ex = sb("ex", [P, PH, PTOP])
        sm = sb("sm", [P, PH, 2])
        tick = sb("tick", [1, 1])
        sel = sb("sel", [P, 3, PH, PTOP])
        iota32 = sb("iota32", [P, P])
        iota = sb("iota", [P, P], F16)
        cols = sb("cols", [P, 4, P])
        high = sb("high", [P, P], F16)
        cur = [sb(f"cur{j}", [P, 4, B]) for j in range(2)]
        hot = [sb(f"hot{j}", [P, B, 3, P], F16) for j in range(2)]
        stage = sb("stage", [P, P, P])
        A = [c.enter_context(nc.psum_tensor(f"ca_A{b}{layer}", [P, 1024], F32)) for b in range(2)]
        G = [c.enter_context(nc.psum_tensor(f"ca_G{j}{layer}", [P, B, P], F32)) for j in range(2)]
        T = G[0][:, 0:3, :]
        names = ("u_in0", "u_in1", "act_stored0", "act_stored1", "u_cut", "first_done", "gelu_done", "iota_in", "score_in", "s_read",
                 "shifted", "exped", "chosen", "turned", "cols_done", "hot_done", "prod", "read", "gate_stored",
                 "own", "gown", "pown")
        with signals(nc, *names) as (
                u_in0, u_in1, act_stored0, act_stored1, u_cut, first_done, gelu_done, iota_in, score_in, s_read,
                shifted, exped, chosen, turned, cols_done, hot_done, prod, read, gate_stored, own, gown, pown):
            u_in, act_stored = (u_in0, u_in1), (act_stored0, act_stored1)
            u_src = io["peer_u"][layer]

            def schedule(eng, chunk, begin, midway, choose, step_of, store):
                def gates_of(n):
                    with eng.Fori(0, TURNS) as k:
                        done = 0
                        for e in range(E):
                            while done * E < beside * (e + 1):
                                chunk(n * (CT // 2) + k * (beside // 2) + (ahead // 2 + done // 2), done % 2)
                                done += 1
                            step_of(n, k, e)

                def choices_of(n, last):
                    for half in range(2):
                        if last is not None:
                            store(last, 2 * half)
                        with eng.Fori(0, ahead // 4) as k:
                            for j in range(2):
                                chunk(n * (CT // 2) + k + half * (ahead // 4), j)
                        if last is not None:
                            store(last, 2 * half + 1)
                        if half == 0:
                            midway(n)
                    choose(n)

                choices_of(0, None)
                with eng.Fori(0, nt - 1) as n:
                    begin(n)
                    gates_of(n)
                    choices_of(n + 1, n)
                gates_of(nt - 1)
                for x in range(tail):
                    if x % 2 == 0 and x // 2 < PARTS:
                        store(nt - 1, x // 2)
                    chunk((CT * nt + x) // 2, x % 2)

            with nc.Block() as block:
                @block.sync
                def _(sp):
                    sp.dma_start(iota32[:, :], io["iota"]).then_inc(iota_in, 16)
                    with sp.Fori(0, PCH // 2) as k:
                        for j in range(2):
                            sp.wait_ge(u_cut, k * 2 + (j + 1))
                            sp.dma_start(ur[j][:, :, :], u_src[bass.ds(k * 2 + j, 1)].rearrange("o p (k n) -> p (o k) n", k=KD)).then_inc(u_in[j], 16)

                @block.gpsimd
                def _(pool):
                    step = InOrder(pool, pown)
                    step(nc.gpsimd.memset(zero[:, :], 0.0))
                    zeros = zero[:, :].unsqueeze(2).broadcast_to([P, KD, P])
                    pool.sem_inc(u_cut, 2)
                    with pool.Fori(0, PCH // 2) as k:
                        step.base, step.n = k * 2 + 1, 0
                        for j in range(2):
                            pool.wait_ge(u_in[j], k * 16 + 16)
                            pool.wait_ge(first_done, k * 2 + (j + 1))
                            step(nc.gpsimd.tensor_tensor(uh[j][:, :, :], ur[j][:, :, :], zeros, ALU.add))
                            nc.gpsimd.tensor_tensor(ul[j][:, :, :], ur[j][:, :, :], uh[j][:, :, :], ALU.subtract).then_inc(u_cut, 1)

                @block.tensor
                def _(pe):
                    def chunk(m, b):
                        pe.wait_ge(u_cut, m * 2 + (b + 3))
                        pe.wait_ge(gelu_done, m * 2 + (b + 1))
                        for k in range(KD):
                            for x, (lhs, rhs) in enumerate(three_products(uh, ul, hh, hl)):
                                for a, w in spans:
                                    last = nc.tensor.matmul(A[b][:, a:a + w], lhs[b][:, k, :], rhs[:, k, a:a + w],
                                                            start=(k == 0 and x == 0), stop=(k == KD - 1 and x == 2))
                        last.then_inc(first_done, 1)

                    def choose(n):
                        pe.wait_ge(chosen, n + 1)
                        pe.wait_ge(read, n * STEPS + 2)
                        for x in range(3):
                            last = nc.tensor.transpose(T[:, x, :], sel[:, x, :, :].rearrange("p h k -> p (h k)"), ident[:, :])
                        last.then_inc(turned, 1)

                    def gate_step(n, k, e):
                        j = e % 2
                        pe.wait_ge(hot_done, n * STEPS + k * E + (e + 3))
                        pe.wait_ge(read, n * STEPS + k * E + (e + 1))
                        for x in range(B):
                            for part in (1, 2):
                                last = nc.tensor.matmul(G[j][:, x, :], hot[j][:, x, part, :], hot[j][:, x, 0, :],
                                                        start=(part == 1), stop=(part == 2))
                        last.then_inc(prod, 1)

                    pe.sem_inc(first_done, 2)
                    nothing = lambda *_: None
                    schedule(pe, chunk, nothing, nothing, choose, gate_step, nothing)

                @block.scalar
                def _(act):
                    def chunk(m, b):
                        act.wait_ge(first_done, m * 2 + (b + 3))
                        act.wait_ge(act_stored[b], m * 16 + 16)
                        nc.scalar.activation(ga[b][:, :], A[b][:, 0:NT], ACT.Gelu).then_inc(gelu_done, 1)
                        act.wait_ge(gelu_done, m * 2 + (b + 3))
                        act.dma_start(acts[bass.ds(m * 2 + b, 1), :, 0:NT].rearrange("o p t -> p (o t)"), ga[b][:, :]).then_inc(act_stored[b], 16)

                    def load_scores(n):
                        act.wait_ge(s_read, n + 1)
                        act.dma_start(s[:, :, :], scores[bass.ds(n + (first_tile + 1), 1)].rearrange("o p (h k) -> p (o h) k", h=2 * PH)).then_inc(score_in, 16)

                    def exponentials(n):
                        act.wait_ge(shifted, n + 1)
                        nc.scalar.activation(ex[:, :, :], ex[:, :, :], ACT.Exp).then_inc(exped, 1)

                    def gate_step(n, k, e):
                        if e == 0:
                            act.wait_ge(gate_stored, n * (16 * PARTS) + 16)
                        act.wait_ge(prod, n * STEPS + k * E + (e + 3))
                        nc.scalar.activation(stage[:, :, bass.ds(k * (E * B) + e * B, B)], G[e % 2][:, :, :].rearrange("p x i -> p i x"),
                                             ACT.Copy).then_inc(read, 1)

                    def store(n, part):
                        act.wait_ge(read, n * STEPS + (STEPS + 2))
                        rows = slice(part * (P // PARTS), (part + 1) * (P // PARTS))
                        act.dma_start(gates[rows, :, bass.ds(n * P + c0, P)].rearrange("a b t -> b a t"), stage[:, rows, :]).then_inc(gate_stored, 16)

                    act.sem_inc(gelu_done, 2)
                    act.sem_inc(read, 2)
                    for b in range(2):
                        act.sem_inc(act_stored[b], 16)
                    act.sem_inc(gate_stored, 16)
                    act.dma_start(s[:, :, :], scores[first_tile].rearrange("p (h k) -> p h k", h=2 * PH)).then_inc(score_in, 16)
                    schedule(act, chunk, load_scores, exponentials, lambda n: None, gate_step, store)
                    for b in range(2):
                        act.wait_ge(act_stored[b], 8 * PCH + 16)
                    act.wait_ge(gate_stored, 16 * PARTS * nt + 16)

                @block.vector
                def _(dve):
                    step = InOrder(dve, own)
                    gstep = InOrder(dve, gown)

                    def settle():
                        step.wait()
                        step.mark(nc.vector.memset(tick[:, :], 0.0))

                    def best16(src, rest, values, places):
                        n = len(src)
                        for x in range(n):
                            step.mark(nc.vector.max(values[x][:, 0:8], src[x]))
                        settle()
                        for x in range(n):
                            step.mark(nc.vector.max_index(places[x][:, 0:8], values[x][:, 0:8], src[x]))
                            step.mark(nc.vector.match_replace(rest[x], values[x][:, 0:8], src[x], -3.0e38))
                        settle()
                        for x in range(n):
                            step.mark(nc.vector.max(values[x][:, 8:16], rest[x]))
                        settle()
                        for x in range(n):
                            step.mark(nc.vector.max_index(places[x][:, 8:16], values[x][:, 8:16], rest[x]))
                        settle()

                    def choices(n):
                        step.start(n, CHOICE_STEPS)
                        dve.wait_ge(score_in, n * 16 + 16)
                        step.mark(nc.vector.memset(tick[:, :], 0.0))
                        rows = range(2 * PH)
                        best16([s[:, x, :] for x in rows], [s2[:, x, :] for x in rows],
                               [top[:, x // 2, x % 2, :] for x in rows], [ti[:, x // 2, x % 2, :] for x in rows])
                        dve.sem_inc(s_read, 1)
                        at = 0
                        for a0, a1, nb in RECTS:
                            shape = [P, PH, a1 - a0, nb]
                            grid = lambda x: x[:, :, at:at + (a1 - a0) * nb].rearrange("p h (a b) -> p h a b", b=nb)
                            first = lambda x: x[:, :, 0, a0:a1].unsqueeze(3).broadcast_to(shape)
                            second = lambda x: x[:, :, 1, 0:nb].unsqueeze(2).broadcast_to(shape)
                            step.mark(nc.vector.tensor_tensor(grid(cand), first(top), second(top), ALU.add))
                            step.mark(nc.vector.tensor_copy(grid(ci[:, 0]), first(ti)))
                            step.mark(nc.vector.tensor_copy(grid(ci[:, 1]), second(ti)))
                            at += (a1 - a0) * nb
                        settle()
                        heads = range(PH)
                        best16([cand[:, h, :] for h in heads], [cand2[:, h, :] for h in heads],
                               [best[:, h, :] for h in heads], [pos[:, h, :] for h in heads])
                        nc.vector.tensor_tensor(ex[:, :, :], best[:, :, :], best[:, :, 0:1].broadcast_to([P, PH, PTOP]),
                                                ALU.subtract).then_inc(shifted, 1)
                        step(nc.vector.tensor_copy(posf[:, :, :], pos[:, :, :]))
                        for h0 in range(0, PH, HB):
                            n16 = HB * PTOP
                            flat = lambda x: x.rearrange("p h k -> p (h k)")
                            step(nc.vector.tensor_tensor(eq[:, :, :, :].rearrange("p h k c -> p (h k) c"),
                                                         iota[:, 0:CAND].unsqueeze(1).broadcast_to([P, n16, CAND]),
                                                         flat(posf[:, h0:h0 + HB, :]).unsqueeze(2).broadcast_to([P, n16, CAND]), ALU.is_equal))
                            for side in range(2):
                                step(nc.vector.tensor_tensor(mul[:, :, :, :], eq[:, :, :, :],
                                                             ci[:, side, h0:h0 + HB, :].unsqueeze(2).broadcast_to([P, HB, PTOP, CAND]), ALU.mult))
                                step(nc.vector.tensor_reduce(flat(sel[:, side, h0:h0 + HB, :]), mul[:, :, :, :].rearrange("p h k c -> p (h k) c"),
                                                             AX.X, ALU.add))
                        dve.wait_ge(exped, n + 1)
                        step(nc.vector.tensor_reduce(sm[:, :, 0], ex[:, :, :], AX.X, ALU.add))
                        step(nc.vector.reciprocal(sm[:, :, 1], sm[:, :, 0]))
                        step(nc.vector.tensor_tensor(sel[:, 2, :, :], ex[:, :, :], sm[:, :, 1:2].broadcast_to([P, PH, PTOP]), ALU.mult))
                        dve.sem_inc(chosen, 1)
                        assert step.n == CHOICE_STEPS, step.n

                    dve.sem_inc(hot_done, 2)
                    dve.sem_inc(prod, 2)
                    dve.wait_ge(iota_in, 16)
                    gstep(nc.vector.tensor_copy(iota[:, :], iota32[:, :]))

                    def gates_of(n):
                        dve.wait_ge(turned, n + 1)
                        nc.vector.tensor_copy(cols[:, 0:3, :], T).then_inc(cols_done, 1)
                        dve.wait_ge(cols_done, n * 2 + 1)
                        gstep.base, gstep.n = n * (STEPS + 1) + 1, 0
                        gstep(nc.vector.tensor_copy(high[:, :], cols[:, 2, :]))
                        nc.vector.tensor_tensor(cols[:, 3, :], cols[:, 2, :], high[:, :], ALU.subtract).then_inc(cols_done, 1)
                        with dve.Fori(0, TURNS) as k:
                            gstep.base, gstep.n = n * (STEPS + 1) + k * E + 2, 0
                            for e in range(E):
                                j = e % 2
                                dve.wait_ge(prod, n * STEPS + k * E + (e + 1))
                                if e == 0:
                                    dve.wait_ge(cols_done, n * 2 + 2)
                                gstep(nc.vector.tensor_copy(cur[j][:, :, :], cols[:, :, bass.ds(k * (E * B) + e * B, B)]))
                                for x in range(B):
                                    w = lambda row: cur[j][:, row, x:x + 1]
                                    nc.vector.tensor_scalar(hot[j][:, x, 0, :], iota[:, :], w(0), None, ALU.is_equal)
                                    nc.vector.tensor_scalar(hot[j][:, x, 1, :], iota[:, :], w(1), w(2), ALU.is_equal, ALU.mult)
                                    last = nc.vector.tensor_scalar(hot[j][:, x, 2, :], iota[:, :], w(1), w(3), ALU.is_equal, ALU.mult)
                                last.then_inc(hot_done, 1)

                    choices(0)
                    with dve.Fori(0, nt - 1) as n:
                        gates_of(n)
                        choices(n + 1)
                    gates_of(nt - 1)


CHOICE_STEPS = 1 + (5 * 2 * PH + 4) + (3 * 4 + 1) + (5 * PH + 4) + 1 + 2 * 5 + 3


def combine_experts(nc, io, gates, acts, ACC, layer, first_tile):
    c0 = first_tile * P
    NT = TOK - c0
    GC = 4
    NG = PCH // GC
    pieces = [(t, h) for t in range(first_tile, TILES) for h in range(2)]
    NP = len(pieces)
    BANKS = 8
    assert 2 * NP % BANKS == 0
    with ExitStack() as c:
        sb = lambda n, s, d=F32: c.enter_context(nc.sbuf_tensor(f"ex_{n}{layer}", s, d))
        vr = [sb(f"vr{b}", [P, D]) for b in range(GC)]
        gr = [sb(f"gr{b}", [P, NT]) for b in range(GC)]
        ar = [sb(f"ar{b}", [P, NT]) for b in range(GC)]
        vh = [sb(f"vh{b}", [P, GC, D], F16) for b in range(2)]
        vl = [sb(f"vl{b}", [P, GC, D], F16) for b in range(2)]
        wh = [sb(f"wh{b}", [P, GC, NT], F16) for b in range(2)]
        wl = [sb(f"wl{b}", [P, GC, NT], F16) for b in range(2)]
        zero = sb("zero", [P, 1])
        R = [c.enter_context(nc.psum_tensor(f"ex_R{b}{layer}", [P, 512], F32)) for b in range(BANKS)]
        names = ["second_done", "v_cut", "w_cut", "added", "own", "pown", "cleared"] + [f"{x}_in{b}" for x in "vga" for b in range(GC)]
        with signals(nc, *names) as sems:
            second_done, v_cut, w_cut, added, own, pown, cleared = sems[:7]
            v_in, g_in, a_in = sems[7:11], sems[11:15], sems[15:19]
            v_src = io["peer_v"][layer]
            with nc.Block() as block:
                @block.sync
                def _(sp):
                    with sp.Fori(0, NG) as g:
                        for x in range(GC):
                            s = g * GC + x
                            sp.wait_ge(w_cut, s + 1)
                            sp.dma_start(gr[x][:, :], gates[bass.ds(s, 1), :, c0:TOK].rearrange("o p t -> p (o t)")).then_inc(g_in[x], 16)
                            sp.dma_start(ar[x][:, :], acts[bass.ds(s, 1), :, 0:NT].rearrange("o p t -> p (o t)")).then_inc(a_in[x], 16)
                            sp.wait_ge(v_cut, s + 1)
                            sp.dma_start(vr[x][:, :], v_src[bass.ds(s, 1)].rearrange("o p d -> p (o d)")).then_inc(v_in[x], 16)

                @block.gpsimd
                def _(pool):
                    step = InOrder(pool, pown)
                    step(nc.gpsimd.memset(zero[:, :], 0.0))
                    pool.sem_inc(v_cut, 4)
                    with pool.Fori(0, NG // 2) as it:
                        step.base, step.n = it * (2 * GC) + 1, 0
                        for q in range(2):
                            for x in range(GC):
                                pool.wait_ge(v_in[x], it * 32 + (16 * q + 16))
                                pool.wait_ge(second_done, it * (2 * NP) + NP * (q + 1))
                                step(nc.gpsimd.tensor_tensor(vh[q][:, x, :], vr[x][:, :], zero[:, 0:1].broadcast_to([P, D]), ALU.add))
                                nc.gpsimd.tensor_tensor(vl[q][:, x, :], vr[x][:, :], vh[q][:, x, :], ALU.subtract).then_inc(v_cut, 1)

                @block.tensor
                def _(pe):
                    pe.sem_inc(second_done, 2 * NP)
                    with pe.Fori(0, NG // 2) as it:
                        for q in range(2):
                            pe.wait_ge(v_cut, it * (2 * GC) + GC * (q + 1) + 4)
                            pe.wait_ge(w_cut, it * (2 * GC) + GC * (q + 1) + 4)
                            for y, (t, h) in enumerate(pieces):
                                pe.wait_ge(added, it * (2 * NP) + (NP * q + y + 1))
                                o = (t - first_tile) * P
                                for x in range(GC):
                                    for n, (lhs, rhs) in enumerate(three_products(wh, wl, vh, vl)):
                                        last = nc.tensor.matmul(R[(NP * q + y) % BANKS][:, :], lhs[q][:, x, o:o + P], rhs[q][:, x, h * 512:h * 512 + 512],
                                                                start=(x == 0 and n == 0), stop=(x == GC - 1 and n == 2))
                                last.then_inc(second_done, 1)

                @block.vector
                def _(dve):
                    step = InOrder(dve, own)

                    def weights(g, q):
                        dve.wait_ge(second_done, g * NP + NP)
                        for x in range(GC):
                            dve.wait_ge(g_in[x], g * 16 + 16)
                            dve.wait_ge(a_in[x], g * 16 + 16)
                            step.base, step.n = g * (2 * GC) + 2 * x, 0
                            step(nc.vector.tensor_tensor(ar[x][:, :], ar[x][:, :], gr[x][:, :], ALU.mult))
                            step(nc.vector.tensor_copy(wh[q][:, x, :], ar[x][:, :]))
                            nc.vector.tensor_tensor(wl[q][:, x, :], ar[x][:, :], wh[q][:, x, :], ALU.subtract).then_inc(w_cut, 1)

                    def add(g, q):
                        dve.wait_ge(added, g * NP + BANKS)
                        for y, (t, h) in enumerate(pieces):
                            dve.wait_ge(second_done, g * NP + (2 * NP + y + 1))
                            part = ACC[:, t, h * 512:h * 512 + 512]
                            nc.vector.tensor_tensor(part, part, R[(NP * q + y) % BANKS][:, :], ALU.add).then_inc(added, 1)

                    dve.sem_inc(w_cut, 4)
                    dve.sem_inc(added, BANKS)
                    weights(0, 0)
                    nc.vector.memset(ACC[:, :, :], 0.0).then_inc(cleared, 1)
                    dve.wait_ge(cleared, 1)
                    with dve.Fori(0, NG // 2 - 1) as it:
                        weights(it * 2 + 1, 1)
                        add(it * 2, 0)
                        weights(it * 2 + 2, 0)
                        add(it * 2 + 1, 1)
                    weights(NG - 1, 1)
                    add(NG - 2, 0)
                    add(NG - 1, 1)


def decay_rates(nc, io, rates):
    with ExitStack() as c:
        sb = lambda n: c.enter_context(nc.sbuf_tensor(f"dr_{n}", [P, RG_N, 2], F32))
        lam, x, s, u, p = (sb(n) for n in ("lam", "x", "s", "u", "p"))
        with signals(nc, "lam_in", "exped", "own", "aown") as (lam_in, exped, own, aown):
            with nc.Block() as block:
                @block.sync
                def _(sp):
                    sp.dma_start(lam[:, :, :], io["od_lambda"]).then_inc(lam_in, 16)

                @block.scalar
                def _(act):
                    step = InOrder(act, aown)
                    act.wait_ge(lam_in, 16)
                    step(nc.scalar.activation(x[:, :, :], lam[:, :, :], ACT.Abs))
                    nc.scalar.activation(x[:, :, :], x[:, :, :], ACT.Exp, scale=-1.0).then_inc(exped, 1)

                @block.vector
                def _(dve):
                    step = InOrder(dve, own)
                    v = lambda t: t[:, :, :]
                    dve.wait_ge(exped, 1)
                    step(nc.vector.tensor_scalar(v(s), v(x), 2.0, None, ALU.add))
                    step(nc.vector.reciprocal(v(s), v(s)))
                    step(nc.vector.tensor_tensor(v(s), v(s), v(x), ALU.mult))
                    step(nc.vector.tensor_tensor(v(u), v(s), v(s), ALU.mult))
                    step(nc.vector.tensor_scalar(v(p), v(u), 1.0 / 17, None, ALU.mult))
                    for n in (15, 13, 11, 9, 7, 5, 3):
                        step(nc.vector.scalar_tensor_tensor(v(p), v(p), 1.0 / n, v(u), ALU.add, ALU.mult))
                    step(nc.vector.scalar_tensor_tensor(v(p), v(p), 1.0, v(s), ALU.add, ALU.mult))
                    step(nc.vector.tensor_scalar(v(s), v(lam), -1.0, 0.0, ALU.mult, ALU.max))
                    step(nc.vector.scalar_tensor_tensor(v(p), v(p), 2.0, v(s), ALU.mult, ALU.add))
                    pair = rates[:, :, 0:4].rearrange("p n (d s) -> p n d s", d=2)
                    nc.vector.tensor_scalar(pair[:, :, :, 0], v(p), -RG_C, None, ALU.mult)
                    nc.vector.tensor_scalar(pair[:, :, :, 1], v(p), RG_C, None, ALU.mult)


def rglru(nc, io, hh, hl, MIX, rates):
    ZC, ZX = RG_LEFT, RG_LEFT + CTX + (RG_CONV - 1 - RG_LEFT) + RG_LEFT
    ZN = ZX + SEQ + (RG_CONV - 1 - RG_LEFT)
    with ExitStack() as c:
        sb = lambda n, s: c.enter_context(nc.sbuf_tensor(f"rg_{n}", s, F32))
        wp = [sb(f"wp{j}", [P, 2, KD, P]) for j in range(2)]
        ph, pl = ([c.enter_context(nc.sbuf_tensor(f"rg_{n}{j}", [P, 2, KD, P], F16)) for j in range(2)] for n in ("ph", "pl"))
        zero = sb("zero", [P, KD])
        wg = [sb(f"wg{j}", [P, 4, P]) for j in range(2)]
        cn = [sb(f"cn{j}", [P, 13]) for j in range(2)]
        gb = [sb(f"gb{j}", [P, SEQ]) for j in range(2)]
        z = [sb(f"z{j}", [P, ZN]) for j in range(2)]
        cv = [sb(f"cv{j}", [P, TOK]) for j in range(2)]
        r, h = ([sb(f"{n}{d}", [P, TOK]) for d in range(2)] for n in "rh")
        i, a, t = ([[sb(f"{n}{d}{j}", [P, TOK]) for d in range(2)] for j in range(2)] for n in "iat")
        a2 = sb("a2", [P, TOK])
        ps = lambda n, s: c.enter_context(nc.psum_tensor(f"rg_{n}", s, F32))
        B = ps("B", [P, 512])
        Z = ps("Z", [P, 1024])
        G = [ps(f"G{g}", [P, 1024]) for g in range(2)]
        with signals(nc, "wp_in0", "wp_in1", "wg_in0", "wg_in1", "proj", "copied", "conv", "gate", "sig", "decayed",
                     "squared", "rooted", "y_done", "own", "aown", "wp_cut", "pown", "cn_in", "branch_done") as (
                wp_in0, wp_in1, wg_in0, wg_in1, proj, copied, conv, gate, sig, decayed, squared, rooted, y_done, own, aown, wp_cut, pown, cn_in, branch_done):
            wp_in, wg_in = (wp_in0, wp_in1), (wg_in0, wg_in1)

            def loop(eng, near, far, branch):
                near(0, 0)
                branch(0, 0)
                with eng.Fori(0, RG_N // 2 - 1) as it:
                    near(it, 1)
                    far(it, 0, (it, 1))
                    near(it + 1, 0)
                    far(it, 1, (it + 1, 0))
                near(RG_N // 2 - 1, 1)
                far(RG_N // 2 - 1, 0, (RG_N // 2 - 1, 1))
                far(RG_N // 2 - 1, 1, None)

            with nc.Block() as block:
                @block.sync
                def _(sp):
                    def load(n, j, projections, gates):
                        at = lambda name: io[name][bass.ds(n, 1)]
                        if projections:
                            sp.dma_start(wp[j][:, :, :, :], at("od_w_in").rearrange("o p (b k m) -> p (o b) k m", b=2, k=KD)).then_inc(wp_in[j], 16)
                        if gates:
                            sp.dma_start(wg[j][:, :, :], at("od_gate_w").rearrange("o p (g m) -> p (o g) m", g=4)).then_inc(wg_in[j], 16)
                    sp.dma_start(rates[:, :, 4:13], io["od_consts"].rearrange("n p m -> p n m")).then_inc(cn_in, 16)
                    for j in range(2):
                        load(j, j, True, True)
                    with sp.Fori(1, RG_N // 2) as it:
                        for j in range(2):
                            sp.wait_ge(wp_cut, it * 2 + (j + 1))
                            load(it * 2 + j, j, True, False)
                            sp.wait_ge(gate, it * 4 + (2 * j - 2))
                            load(it * 2 + j, j, False, True)

                @block.gpsimd
                def _(pool):
                    step = InOrder(pool, pown)
                    step(nc.gpsimd.memset(zero[:, :], 0.0))
                    zeros = zero[:, :].unsqueeze(2).broadcast_to([P, KD, P])
                    pool.sem_inc(wp_cut, 2)
                    with pool.Fori(0, RG_N // 2) as it:
                        step.base, step.n = it * 4 + 1, 0
                        for j in range(2):
                            pool.wait_ge(wp_in[j], it * 16 + 16)
                            pool.wait_ge(branch_done, it * 2 + (j + 1))
                            for b in range(2):
                                step(nc.gpsimd.tensor_tensor(ph[j][:, b], wp[j][:, b], zeros, ALU.add))
                                ins = nc.gpsimd.tensor_tensor(pl[j][:, b], wp[j][:, b], ph[j][:, b], ALU.subtract)
                            ins.then_inc(wp_cut, 1)

                @block.tensor
                def _(pe):
                    def project(out, b, j, s, n):
                        for k in range(KD):
                            for x, (lhs, rhs) in enumerate(three_products(ph, pl, hh, hl)):
                                last = nc.tensor.matmul(out, lhs[j][:, b, k, :], rhs[:, k, s:s + n],
                                                        start=(k == 0 and x == 0), stop=(k == KD - 1 and x == 2))
                        return last

                    def near(m, j):
                        pe.wait_ge(wp_cut, m * 2 + (j + 3))
                        pe.wait_ge(copied, m * 4 + (2 * j + 1))
                        for s, n in HALVES:
                            project(Z[:, s:s + n], 1, j, s, n).then_inc(proj, 1)

                    def branch(m, j):
                        pe.wait_ge(copied, m * 4 + (2 * j + 2))
                        project(B[:, :], 0, j, CTX, SEQ).then_inc(branch_done, 1)

                    def far(m, j, following):
                        pe.wait_ge(wg_in[j], m * 16 + 16)
                        pe.wait_ge(conv, m * 2 + (j + 1))
                        for d in range(2):
                            pe.wait_ge(sig, m * 8 + (4 * j + 2 * d + 1))
                            for g in range(2):
                                for s, n in HALVES:
                                    last = nc.tensor.matmul(G[g][:, s:s + n], wg[j][:, 2 * d + g, :], cv[j][:, s:s + n],
                                                            start=True, stop=True)
                            last.then_inc(gate, 1)
                            if d == 0 and following:
                                branch(*following)

                    pe.sem_inc(branch_done, 2)
                    loop(pe, near, far, branch)

                @block.scalar
                def _(act):
                    step = InOrder(act, aown)

                    def near(m, j):
                        act.wait_ge(proj, m * 4 + (2 * j + 2))
                        step.mark(nc.scalar.activation(z[j][:, ZC:ZC + CTX], Z[:, 0:CTX], ACT.Copy))
                        nc.scalar.activation(z[j][:, ZX:ZX + SEQ], Z[:, CTX:TOK], ACT.Copy).then_inc(copied, 1)

                    def branch(m, j):
                        act.wait_ge(branch_done, m * 2 + (j + 3))
                        act.wait_ge(y_done, m * 2 + (j + 1))
                        nc.scalar.activation(gb[j][:, :], B[:, :], ACT.Gelu).then_inc(copied, 1)

                    def far(m, j, following):
                        act.wait_ge(y_done, m * 2 + (j + 1))
                        for d in range(2):
                            act.wait_ge(gate, m * 4 + (2 * j + d + 1))
                            nc.scalar.activation(r[d][:, :], G[0][:, 0:TOK], ACT.Sigmoid, bias=cn[j][:, 9 + 2 * d:10 + 2 * d]).then_inc(sig, 1)
                            nc.scalar.activation(i[j][d][:, :], G[1][:, 0:TOK], ACT.Sigmoid, bias=cn[j][:, 10 + 2 * d:11 + 2 * d]).then_inc(sig, 1)
                            if d == 1 and following:
                                branch(*following)
                        act.wait_ge(sig, m * 8 + (4 * j + 5))
                        for d in range(2):
                            nc.scalar.activation(a[j][d][:, :], r[d][:, :], ACT.Exp, scale=cn[j][:, 2 * d:2 * d + 1]).then_inc(decayed, 1)
                            nc.scalar.activation(t[j][d][:, :], r[d][:, :], ACT.Tanh, scale=cn[j][:, 2 * d + 1:2 * d + 2]).then_inc(decayed, 1)
                        for d in range(2):
                            act.wait_ge(squared, m * 4 + (2 * j + d + 1))
                            nc.scalar.activation(t[j][d][:, :], t[j][d][:, :], ACT.Sqrt).then_inc(rooted, 1)

                    act.sem_inc(copied, 2)
                    act.sem_inc(sig, 1)
                    act.wait_ge(y_done, 2)
                    loop(act, near, far, branch)

                @block.vector
                def _(dve):
                    step = InOrder(dve, own)
                    NEAR, FAR = 8, 11
                    before = 3

                    def near(m, j):
                        step.base, step.n = m * (2 * (NEAR + FAR)) + (before + j * (NEAR + FAR) - FAR), 0
                        if isinstance(m, int) and (m, j) == (0, 0):
                            step.base = before
                        dve.wait_ge(copied, m * 4 + (2 * j + 3))
                        step(nc.vector.tensor_copy(cn[j][:, :], rates[:, bass.ds(m * 2 + j, 1), :].rearrange("p o s -> p (o s)")))
                        segs = ((0, ZC, CTX), (CTX, ZX, SEQ))
                        for o, s, n in segs:
                            s -= RG_LEFT
                            step.mark(nc.vector.tensor_scalar(cv[j][:, o:o + n], z[j][:, s:s + n], cn[j][:, 4:5], cn[j][:, 8:9],
                                                              ALU.mult, ALU.add))
                        for tap in range(1, RG_CONV):
                            step.wait()
                            for o, s, n in segs:
                                s += tap - RG_LEFT
                                ins = nc.vector.scalar_tensor_tensor(cv[j][:, o:o + n], z[j][:, s:s + n], cn[j][:, 4 + tap:5 + tap],
                                                                     cv[j][:, o:o + n], ALU.mult, ALU.add)
                                if tap < RG_CONV - 1 or o == 0:
                                    step.mark(ins)
                        ins.then_inc(conv, 1)
                        assert step.n == NEAR, step.n

                    def far(m, j, following):
                        step.base, step.n = m * (2 * (NEAR + FAR)) + (before + j * (NEAR + FAR) + 2 * NEAR), 0
                        if isinstance(m, int) and j == 1:
                            step.base -= NEAR
                        dve.wait_ge(conv, m * 2 + (j + 1))
                        for d in range(2):
                            dve.wait_ge(sig, m * 8 + (4 * j + 2 * d + 3))
                            step.mark(nc.vector.tensor_tensor(i[j][d][:, :], i[j][d][:, :], cv[j][:, :], ALU.mult))
                        for d in range(2):
                            dve.wait_ge(decayed, m * 8 + (4 * j + 2 * d + 2))
                            step(nc.vector.tensor_tensor(a2[:, :], a[j][d][:, :], a[j][d][:, :], ALU.mult))
                            nc.vector.scalar_tensor_tensor(t[j][d][:, :], a2[:, :], 1.0, t[j][d][:, :], ALU.add, ALU.mult).then_inc(squared, 1)
                            dve.wait_ge(squared, m * 4 + (2 * j + d + 1))
                        for d in range(2):
                            dve.wait_ge(rooted, m * 4 + (2 * j + d + 1))
                            step(nc.vector.tensor_tensor(i[j][d][:, :], i[j][d][:, :], t[j][d][:, :], ALU.mult))
                            if d == 0:
                                step.mark(nc.vector.tensor_tensor_scan(h[0][:, :], a[j][0][:, :], i[j][0][:, :], 0.0, ALU.mult, ALU.add))
                            else:
                                back = lambda x, s, e: x[:, s:e][:, ::-1]
                                step(nc.vector.tensor_tensor_scan(back(h[1], 0, CTX), back(a[j][1], 0, CTX), back(i[j][1], 0, CTX), 0.0,
                                                                  ALU.mult, ALU.add))
                                step(nc.vector.tensor_tensor_scan(back(h[1], CTX, TOK), back(a[j][1], CTX, TOK), back(i[j][1], CTX, TOK),
                                                                  h[1][:, 0:1], ALU.mult, ALU.add))
                        step(nc.vector.tensor_tensor(h[0][:, CTX:TOK], h[0][:, CTX:TOK], h[1][:, CTX:TOK], ALU.add))
                        dve.wait_ge(copied, m * 4 + (2 * j + 4))
                        step(nc.vector.tensor_tensor(MIX[:, bass.ds(m * 2 + j, 1), :].rearrange("p o t -> p (o t)"), h[0][:, CTX:TOK],
                                                     gb[j][:, :], ALU.mult))
                        assert step.n == FAR, step.n
                        dve.sem_inc(y_done, 1)

                    step.mark(nc.vector.memset(z[0][:, :], 0.0))
                    step.mark(nc.vector.memset(z[1][:, :], 0.0))
                    step(nc.vector.memset(a2[:, :], 0.0))
                    dve.wait_ge(cn_in, 16)
                    dve.sem_inc(y_done, 2)
                    loop(dve, near, far, lambda m, j: None)


def peer(nc, io, mods, dram, H, hh, hl, ident, layer, first_tile, after=None, out=None):
    scores, gates, acts = dram
    peer_scores(nc, io, hh, hl, scores, layer, first_tile)
    choose_and_activate(nc, io, ident, hh, hl, scores, gates, acts, layer, first_tile)
    with nc.sbuf_tensor(f"ACC{layer}", [P, TILES, D], F32) as ACC:
        combine_experts(nc, io, gates, acts, ACC, layer, first_tile)
        project_and_norm(nc, io, mods, H, ACC, None, list(range(first_tile, TILES)), layer, 1, f"n{layer}p", after, out)


def build(nc, io, out):
    with ExitStack() as c:
        sb = lambda n, s: c.enter_context(nc.sbuf_tensor(n, s, F32))
        H = sb("H", [P, TILES, D])
        ident = sb("ident", [P, P])
        ones = sb("ones", [P, P])
        hh, hl = (c.enter_context(nc.sbuf_tensor(n, [P, KD, TOK], F16)) for n in ("hh", "hl"))
        mods = nc.dram_tensor("mods", [2, 2 * N_MOD * D], F32, kind="Internal").ap()
        scores = nc.dram_tensor("scores", [TILES, P, 2 * PH * P], F32, kind="Internal").ap()
        gates = nc.dram_tensor("gates", [P, P, TOK], F32, kind="Internal").ap()
        acts = nc.dram_tensor("acts", [PCH, P, TOK], F32, kind="Internal").ap()
        dram = (scores, gates, acts)
        modulation_vectors(nc, io, mods, ones, H, ident)
        modulate_columns(nc, mods, H, hh, hl, ident, 0, 0, 0, "m0")
        with nc.sbuf_tensor("MIX", [P, KD, TOK], F32) as MIX:
            with nc.sbuf_tensor("PT", [P, N_PROJ, TOK], F32) as PT, nc.sbuf_tensor("V", [P, TILES, GH * GDV], F32) as V:
                project_l0(nc, io, hh, hl, PT, V)
                latent_norms(nc, io, PT, ones)
                attention(nc, io, PT, MIX, ident)
                gla(nc, io, PT, V, MIX, ident, ones)
            project_and_norm(nc, io, mods, H, MIX, "ev_w_out", list(range(TILES)), 0, 0, "n0", (hh, hl, ident, 0, 3))
        peer(nc, io, mods, dram, H, hh, hl, ident, 0, 0, (hh, hl, ident, 1, 0))
        with nc.sbuf_tensor("MIX1", [P, RG_N, SEQ], F32) as MIX:
            with nc.sbuf_tensor("rates", [P, RG_N, 13], F32) as rates:
                decay_rates(nc, io, rates)
                rglru(nc, io, hh, hl, MIX, rates)
            project_and_norm(nc, io, mods, H, MIX, "od_w_out", list(range(CTX_TILES, TILES)), 1, 0, "n1", (hh, hl, ident, 1, 3))
        peer(nc, io, mods, dram, H, hh, hl, ident, 1, CTX_TILES, out=out)


def more_inputs(give, a, k_major, swap):
    n_freq = ROPE // 4
    inv = np.power(np.float32(10000.0), -np.arange(n_freq, dtype=np.float32) / np.float32(n_freq)).astype(np.float32)
    row = np.repeat(np.arange(SEQ // 64, dtype=np.float32), 64)
    col = np.tile(np.arange(64, dtype=np.float32), SEQ // 64)
    ang = np.concatenate([row[:, None] * inv, col[:, None] * inv], axis=-1).astype(np.float32)
    cos, sin = np.cos(ang).T, np.sin(ang).T
    rope = np.zeros((64, TOK), np.float32)
    rope[0:32, :CTX] = 1.0
    rope[0:32, CTX:] = np.concatenate([cos, cos])
    rope[32:64, CTX:] = np.concatenate([-sin, sin])
    give("rope", rope)
    give("latent_gain", np.concatenate([a["ev_q_norm"][0], a["ev_kv_norm"][0]]).reshape(5, P).T)
    uq = a["ev_w_uq"][0].reshape(3, P, HEADS, NOPE + ROPE)
    uq = np.concatenate([uq, swap(uq[..., NOPE:])], axis=-1)
    ukv = a["ev_w_ukv"][0].reshape(2, P, HEADS, NOPE + V_DIM)
    up = np.concatenate([uq, ukv], axis=0).transpose(2, 1, 0, 3)
    give("ev_w_up", up.reshape(HEADS, P, 5 * P))
    give("gla_wa2", a["ev_gla_wa2"][0])
    give("gla_ba", a["ev_gla_ba"][0].reshape(2, 2, P).transpose(2, 1, 0))
    give("gla_gain", a["ev_gla_norm"][0].reshape(GH, GDV).T)
    j, i = np.arange(P)[:, None], np.arange(P)[None, :]
    same = j // CHUNK == i // CHUNK
    give("gla_keep", np.stack([same & (j <= i), same & (j >= i)], axis=1).astype(np.int32))
    give("ev_w_out", k_major(a["ev_w_out"][0]))
    wq = a["peer_wq"].reshape(DEPTH, KD, P, 2 * PH, P)
    give("peer_wq", wq.transpose(0, 3, 2, 1, 4).reshape(DEPTH, 2 * PH, P, KD * P))
    give("peer_keys", np.stack([a["peer_k1"], a["peer_k2"]], axis=1).transpose(0, 3, 1, 2))
    give("iota", np.broadcast_to(np.arange(P, dtype=np.float32), (P, P)))
    u = a["peer_u"].reshape(DEPTH, PCH, P, KD, P)
    give("peer_u", u.transpose(0, 1, 4, 3, 2).reshape(DEPTH, PCH, P, KD * P))
    give("peer_v", a["peer_v"].reshape(DEPTH, PCH, P, D))
    w = a["od_w_in"][0].reshape(KD, P, 2, RG_N, P)
    give("od_w_in", w.transpose(3, 1, 2, 0, 4).reshape(RG_N, P, 2 * KD * P))
    give("od_gate_w", a["od_gate_w"][0].transpose(2, 3, 0, 1, 4).reshape(RG_N, P, 4 * P))
    consts = np.concatenate([a["od_conv_w"][0], a["od_conv_b"], a["od_gate_b"][0].reshape(4, RG_W)])
    give("od_consts", consts.reshape(9, RG_N, P).transpose(1, 2, 0))
    give("od_lambda", a["od_lambda"][0].reshape(2, RG_N, P).transpose(2, 1, 0))
    give("od_w_out", k_major(a["od_w_out"][0]))


def kernel(**inputs):
    import concourse.bacc as bacc
    from concourse.bass_utils import run_bass_kernel_spmd as run

    a = {k: np.asarray(v) for k, v in inputs.items()}
    nc = bacc.Bacc("TRN2", target_bir_lowering=False, num_devices=1)
    arrays, io = {}, {}

    def give(name, x):
        x = np.ascontiguousarray(x)
        arrays["in_" + name] = x
        io[name] = nc.dram_tensor("in_" + name, x.shape, mybir.dt.from_np(x.dtype), kind="ExternalInput").ap()

    def k_major(w):
        return w.reshape(w.shape[0] // P, P, w.shape[1]).transpose(1, 0, 2)

    give("x", a["x"][0])
    give("ctx", a["ctx"][0])
    give("ident", np.eye(P, dtype=np.float32))
    give("cond", np.stack([a["c"][0], a["c_ctx"]], axis=1).reshape(KD, P, 2).transpose(1, 0, 2))
    give("mod_w", a["mod_w"].reshape(2, KD, P, N_MOD, 1024).transpose(0, 3, 2, 1, 4).reshape(2 * N_MOD, P, KD * 1024))
    give("mod_b", a["mod_b"].reshape(-1))
    give("ln_g", a["ln_g"].reshape(4, D))
    give("ln_b", a["ln_b"].reshape(4, D))

    w = a["ev_w_in"][0]
    b = np.cumsum([0, Q_RANK, KV_RANK, ROPE, GH * GDK, GH * GDK, GH * GDV, GH * GDV, GRANK, GRANK])
    cq, ckv, pe, gq, gk, gv, gg, gaf, gab = [w[:, b[i]:b[i + 1]] for i in range(9)]
    pad = np.zeros((D, 16), np.float32)
    swap = lambda m: np.concatenate([m[..., ROPE // 2:], m[..., :ROPE // 2]], axis=-1)
    ext = np.concatenate([cq, ckv, gq, gk, gg, gaf, pad, gab, pad, pe, swap(pe)], axis=1)
    give("ev_w_in", ext.reshape(KD, P, N_PROJ, P).transpose(2, 1, 0, 3).reshape(N_PROJ, P, KD * P))
    give("ev_w_v", k_major(gv))
    more_inputs(give, a, k_major, swap)

    out = nc.dram_tensor("out_0", (SEQ, D), F32, kind="ExternalOutput").ap()
    build(nc, io, out)
    r = run(nc, [arrays], core_ids=[0])
    return r.results[0]["out_0"].reshape(1, SEQ, D)
```
